# Optimizing a Trainium2 kernel written in Bass

```python
import math, functools
import jax, jax.numpy as jnp
from jax import lax
import numpy as np

D_MODEL = 2048
BATCH = 1
SEQ = 512
DEPTH = 1
DEC_BATCH = 8
DEC_SEQ = 8
PAST_LEN = 256
PAGE_SIZE = 128

MIX_WIDTH = D_MODEL
FOX_WIDTH = MIX_WIDTH // 2
FOX_HEAD_DIM = 128
FOX_HEADS = FOX_WIDTH // FOX_HEAD_DIM
FOX_SCALE = FOX_HEAD_DIM ** -0.5
Q_BLOCK = 128
FORGET_BIAS_INIT = 3.0
SSM_WIDTH = MIX_WIDTH - FOX_WIDTH
SSM_CH_PER_GROUP = 16
SSM_GROUPS = SSM_WIDTH // SSM_CH_PER_GROUP
SSM_STATE = 64
IN_SPLITS = (FOX_WIDTH, 2 * FOX_WIDTH, 3 * FOX_WIDTH, 3 * FOX_WIDTH + FOX_HEADS)
IN_WIDTH = 3 * FOX_WIDTH + FOX_HEADS + SSM_WIDTH
PEER_HEADS = 8
PEER_N_KEYS = 128
PEER_N_EXPERTS = PEER_N_KEYS * PEER_N_KEYS
PEER_TOPK = 16
PEER_KEY_DIM = 256
PEER_HALF = PEER_KEY_DIM // 2
PEER_BLOCK = 128
N_MOD = 6
EPS = 1e-6

kernel_name = "hymba_fox_s5_peer_adaln_step"

def rms_norm(x, g):
    xf = x.astype(jnp.float32)
    y = xf * lax.rsqrt(jnp.mean(xf * xf, axis=-1, keepdims=True) + EPS)
    return (y * g.astype(jnp.float32)).astype(x.dtype)

def ada_modulation(c, w_ada, b_ada):
    return jnp.split(jax.nn.silu(c) @ w_ada + b_ada, N_MOD, axis=-1)

def modulate(h, shift, scale):
    return h * (1 + scale[:, None, :]) + shift[:, None, :]

def mixer_projections(h, w_in, b_forget):
    b, l, _ = h.shape
    q, k, v, fg, u = jnp.split(h @ w_in, list(IN_SPLITS), axis=-1)
    shape = (b, l, FOX_HEADS, FOX_HEAD_DIM)
    logf = jax.nn.log_sigmoid((fg + b_forget).astype(jnp.float32))
    return q.reshape(shape), k.reshape(shape), v.reshape(shape), logf, u

def fox_attend_prompt(q, k, v, logf):
    b, l, h, d = q.shape
    qb = min(Q_BLOCK, l)
    nb = l // qb
    fcum = jnp.cumsum(logf, axis=1)
    fk = fcum.transpose(0, 2, 1)[:, :, None, :]
    q_blocks = q.reshape(b, nb, qb, h, d).transpose(1, 0, 2, 3, 4)
    fq_blocks = fcum.reshape(b, nb, qb, h).transpose(1, 0, 3, 2)
    k_pos = jnp.arange(l)

    def block(args):
        i, q_i, fq_i = args
        s = jnp.einsum('bqhd,bkhd->bhqk', q_i, k).astype(jnp.float32) * FOX_SCALE
        s = s + fq_i[..., None] - fk
        q_pos = i * qb + jnp.arange(qb)
        s = jnp.where(k_pos[None, :] <= q_pos[:, None], s, -jnp.inf)
        p = jax.nn.softmax(s, axis=-1).astype(v.dtype)
        return jnp.einsum('bhqk,bkhd->bqhd', p, v)

    out = lax.map(block, (jnp.arange(nb), q_blocks, fq_blocks))
    return out.transpose(1, 0, 2, 3, 4).reshape(b, l, h, d)

def fox_attend_sample(q, k, v, logf, k_past, v_past, logf_past):
    n_past = k_past.shape[1]
    n_new = q.shape[1]
    fcum = jnp.cumsum(jnp.concatenate([logf_past.astype(jnp.float32), logf], axis=1), axis=1)
    fq = fcum[:, n_past:].transpose(0, 2, 1)[..., None]
    fk = fcum.transpose(0, 2, 1)[:, :, None, :]
    s = jnp.concatenate([jnp.einsum('bqhd,bkhd->bhqk', q, k_past),
                         jnp.einsum('bqhd,bkhd->bhqk', q, k)], axis=-1).astype(jnp.float32)
    s = s * FOX_SCALE + fq - fk
    mask = jnp.arange(n_past + n_new)[None, :] <= n_past + jnp.arange(n_new)[:, None]
    s = jnp.where(mask, s, -jnp.inf)
    p = jax.nn.softmax(s, axis=-1).astype(v.dtype)
    return (jnp.einsum('bhqk,bkhd->bqhd', p[..., :n_past], v_past)
            + jnp.einsum('bhqk,bkhd->bqhd', p[..., n_past:], v))

def s5_discretise(a_re, a_im, log_dt, b_re, b_im):
    a_re = jnp.minimum(a_re.astype(jnp.float32), -1e-4)
    a_im = a_im.astype(jnp.float32)
    dt = jnp.exp(log_dt.astype(jnp.float32))[:, None]
    mag = jnp.exp(a_re * dt)
    abar_re = mag * jnp.cos(a_im * dt)
    abar_im = mag * jnp.sin(a_im * dt)
    den = a_re * a_re + a_im * a_im
    nr, ni = abar_re - 1.0, abar_im
    coef_re = (nr * a_re + ni * a_im) / den
    coef_im = (ni * a_re - nr * a_im) / den
    b_re = b_re.astype(jnp.float32)
    b_im = b_im.astype(jnp.float32)
    bbar_re = coef_re[..., None] * b_re - coef_im[..., None] * b_im
    bbar_im = coef_re[..., None] * b_im + coef_im[..., None] * b_re
    return abar_re, abar_im, bbar_re, bbar_im

def s5_combine(e1, e2):
    a1r, a1i, b1r, b1i = e1
    a2r, a2i, b2r, b2i = e2
    return (a2r * a1r - a2i * a1i, a2r * a1i + a2i * a1r,
            a2r * b1r - a2i * b1i + b2r, a2r * b1i + a2i * b1r + b2i)

def s5_branch(u, h0_re, h0_im, a_re, a_im, log_dt, b_re, b_im, c_re, c_im, d_skip, w_glu, b_glu):
    bsz, l, _ = u.shape
    abr, abi, bbr, bbi = s5_discretise(a_re, a_im, log_dt, b_re, b_im)
    uf = u.astype(jnp.float32).reshape(bsz, l, SSM_GROUPS, SSM_CH_PER_GROUP)
    bu_re = jnp.einsum('blgc,gpc->blgp', uf, bbr)
    bu_im = jnp.einsum('blgc,gpc->blgp', uf, bbi)
    h0_re = h0_re.astype(jnp.float32)
    h0_im = h0_im.astype(jnp.float32)
    bu_re = bu_re.at[:, 0].add(abr * h0_re - abi * h0_im)
    bu_im = bu_im.at[:, 0].add(abr * h0_im + abi * h0_re)
    elems = (jnp.broadcast_to(abr, bu_re.shape), jnp.broadcast_to(abi, bu_re.shape), bu_re, bu_im)
    _, _, h_re, h_im = lax.associative_scan(s5_combine, elems, axis=1)
    y = (jnp.einsum('blgp,gcp->blgc', h_re, c_re.astype(jnp.float32))
         - jnp.einsum('blgp,gcp->blgc', h_im, c_im.astype(jnp.float32))
         + d_skip.astype(jnp.float32).reshape(SSM_GROUPS, SSM_CH_PER_GROUP) * uf)
    z = jax.nn.gelu(y.reshape(bsz, l, SSM_WIDTH))
    out = z * jax.nn.sigmoid(z @ w_glu.astype(jnp.float32) + b_glu.astype(jnp.float32))
    return out.astype(u.dtype), h_re[:, -1], h_im[:, -1]

def peer_ffn(h, w_q, subkeys, exp_u, exp_v):
    bsz, l, d = h.shape
    n_tok = bsz * l
    n_blk = -(-n_tok // PEER_BLOCK)
    t = jnp.pad(h.reshape(n_tok, d), ((0, n_blk * PEER_BLOCK - n_tok), (0, 0)))
    t = t.reshape(n_blk, PEER_BLOCK, d)
    n_cand = PEER_TOPK * PEER_TOPK

    def block(tb):
        q = (tb @ w_q).reshape(PEER_BLOCK, PEER_HEADS, 2, PEER_HALF)
        s = jnp.einsum('thxd,hxnd->thxn', q, subkeys).astype(jnp.float32)
        sv, si = lax.top_k(s, PEER_TOPK)
        cand_s = (sv[:, :, 0, :, None] + sv[:, :, 1, None, :]).reshape(PEER_BLOCK, PEER_HEADS, n_cand)
        cand_i = (si[:, :, 0, :, None] * PEER_N_KEYS + si[:, :, 1, None, :]).reshape(PEER_BLOCK, PEER_HEADS, n_cand)
        top_s, top_j = lax.top_k(cand_s, PEER_TOPK)
        e = jnp.take_along_axis(cand_i, top_j, axis=-1)
        g = jax.nn.softmax(top_s, axis=-1)
        a = jax.nn.gelu(jnp.einsum('thkd,td->thk', exp_u[e], tb).astype(jnp.float32))
        return jnp.einsum('thk,thkd->td', (g * a).astype(tb.dtype), exp_v[e])

    out = lax.map(block, t)
    return out.reshape(n_blk * PEER_BLOCK, d)[:n_tok].reshape(bsz, l, d)

def trunk_layer(x, c, attend, h0_re, h0_im,
                w_ada, b_ada, g_norm1, g_norm2, w_in, b_forget,
                ssm_a_re, ssm_a_im, ssm_log_dt, ssm_b_re, ssm_b_im, ssm_c_re, ssm_c_im, ssm_d,
                w_glu, b_glu, g_attn_out, g_ssm_out, w_out, peer_w_q, peer_subkeys, peer_u, peer_v):
    bsz, l, _ = x.shape
    shift1, scale1, gate1, shift2, scale2, gate2 = ada_modulation(c, w_ada, b_ada)
    h = modulate(rms_norm(x, g_norm1), shift1, scale1)
    q, k, v, logf, u = mixer_projections(h, w_in, b_forget)
    att = attend(q, k, v, logf).reshape(bsz, l, FOX_WIDTH)
    ssm, s_re, s_im = s5_branch(u, h0_re, h0_im, ssm_a_re, ssm_a_im, ssm_log_dt, ssm_b_re, ssm_b_im,
                                ssm_c_re, ssm_c_im, ssm_d, w_glu, b_glu)
    merged = jnp.concatenate([rms_norm(att, g_attn_out), rms_norm(ssm, g_ssm_out)], axis=-1) @ w_out
    x = x + gate1[:, None, :] * merged
    h = modulate(rms_norm(x, g_norm2), shift2, scale2)
    x = x + gate2[:, None, :] * peer_ffn(h, peer_w_q, peer_subkeys, peer_u, peer_v)
    return x, k, v, logf, s_re, s_im

def setup_inputs(seed: int = 0) -> dict:
    key = jax.random.key(seed)
    keys = iter(jax.random.split(key, 40))

    def nrm(shape, scale):
        return jax.random.normal(next(keys), shape, jnp.float32) * scale

    n_pages = PAST_LEN // PAGE_SIZE
    n_used = DEC_BATCH * n_pages
    n_pool = n_used + (n_used + 3) // 4
    page_table = jax.random.permutation(next(keys), n_pool)[:n_used].reshape(DEC_BATCH, n_pages).astype(jnp.int32)
    G, P, CG = SSM_GROUPS, SSM_STATE, SSM_CH_PER_GROUP
    return {
        'x_prompt': nrm((BATCH, SEQ, D_MODEL), 1.0),
        'x_sample': nrm((DEC_BATCH, DEC_SEQ, D_MODEL), 1.0),
        'cache_k': nrm((DEPTH, n_pool, PAGE_SIZE, FOX_HEADS, FOX_HEAD_DIM), 1.0),
        'cache_v': nrm((DEPTH, n_pool, PAGE_SIZE, FOX_HEADS, FOX_HEAD_DIM), 1.0),
        'cache_logf': jax.nn.log_sigmoid(FORGET_BIAS_INIT + nrm((DEPTH, n_pool, PAGE_SIZE, FOX_HEADS), 1.0)),
        'state_ssm_re': nrm((DEPTH, DEC_BATCH, G, P), 0.3),
        'state_ssm_im': nrm((DEPTH, DEC_BATCH, G, P), 0.3),
        'page_table': page_table,
        'c_prompt': nrm((BATCH, D_MODEL), 1.0),
        'c_sample': nrm((DEC_BATCH, D_MODEL), 1.0),
        'w_ada': nrm((DEPTH, D_MODEL, N_MOD * D_MODEL), 0.5 * D_MODEL ** -0.5),
        'b_ada': nrm((DEPTH, N_MOD * D_MODEL), 0.01),
        'g_norm1': 1.0 + nrm((DEPTH, D_MODEL), 0.02),
        'g_norm2': 1.0 + nrm((DEPTH, D_MODEL), 0.02),
        'w_in': nrm((DEPTH, D_MODEL, IN_WIDTH), D_MODEL ** -0.5),
        'b_forget': FORGET_BIAS_INIT + nrm((DEPTH, FOX_HEADS), 0.1),
        'ssm_a_re': -0.5 + nrm((DEPTH, G, P), 0.01),
        'ssm_a_im': jnp.pi * jnp.arange(P, dtype=jnp.float32) + nrm((DEPTH, G, P), 0.01),
        'ssm_log_dt': jax.random.uniform(next(keys), (DEPTH, G), jnp.float32, math.log(1e-3), math.log(1e-1)),
        'ssm_b_re': nrm((DEPTH, G, P, CG), (2 * CG) ** -0.5),
        'ssm_b_im': nrm((DEPTH, G, P, CG), (2 * CG) ** -0.5),
        'ssm_c_re': nrm((DEPTH, G, CG, P), (2 * P) ** -0.5),
        'ssm_c_im': nrm((DEPTH, G, CG, P), (2 * P) ** -0.5),
        'ssm_d': nrm((DEPTH, SSM_WIDTH), 1.0),
        'w_glu': nrm((DEPTH, SSM_WIDTH, SSM_WIDTH), SSM_WIDTH ** -0.5),
        'b_glu': nrm((DEPTH, SSM_WIDTH), 0.01),
        'g_attn_out': 1.0 + nrm((DEPTH, FOX_WIDTH), 0.02),
        'g_ssm_out': 1.0 + nrm((DEPTH, SSM_WIDTH), 0.02),
        'w_out': nrm((DEPTH, MIX_WIDTH, D_MODEL), MIX_WIDTH ** -0.5),
        'peer_w_q': nrm((DEPTH, D_MODEL, PEER_HEADS * PEER_KEY_DIM), D_MODEL ** -0.5),
        'peer_subkeys': nrm((DEPTH, PEER_HEADS, 2, PEER_N_KEYS, PEER_HALF), PEER_HALF ** -0.5),
        'peer_u': nrm((DEPTH, PEER_N_EXPERTS, D_MODEL), D_MODEL ** -0.5),
        'peer_v': nrm((DEPTH, PEER_N_EXPERTS, D_MODEL), 0.5),
        'g_final': 1.0 + nrm((D_MODEL,), 0.02),
    }

def reference(x_prompt, x_sample, cache_k, cache_v, cache_logf, state_ssm_re, state_ssm_im, page_table,
              c_prompt, c_sample, w_ada, b_ada, g_norm1, g_norm2, w_in, b_forget,
              ssm_a_re, ssm_a_im, ssm_log_dt, ssm_b_re, ssm_b_im, ssm_c_re, ssm_c_im, ssm_d,
              w_glu, b_glu, g_attn_out, g_ssm_out, w_out, peer_w_q, peer_subkeys, peer_u, peer_v, g_final):
    n_batch = x_prompt.shape[0]
    n_dec = x_sample.shape[0]
    past_len = page_table.shape[1] * cache_k.shape[2]
    zero_state = jnp.zeros((n_batch, SSM_GROUPS, SSM_STATE), jnp.float32)
    xp, xs = x_prompt, x_sample
    kp_l, vp_l, fp_l, rp_l, ip_l = [], [], [], [], []
    ks_l, vs_l, fs_l, rs_l, is_l = [], [], [], [], []
    for l in range(DEPTH):
        lw = (w_ada[l], b_ada[l], g_norm1[l], g_norm2[l], w_in[l], b_forget[l],
              ssm_a_re[l], ssm_a_im[l], ssm_log_dt[l], ssm_b_re[l], ssm_b_im[l], ssm_c_re[l], ssm_c_im[l], ssm_d[l],
              w_glu[l], b_glu[l], g_attn_out[l], g_ssm_out[l], w_out[l],
              peer_w_q[l], peer_subkeys[l], peer_u[l], peer_v[l])
        xp, kp, vp, fp, rp, ip = trunk_layer(xp, c_prompt, fox_attend_prompt, zero_state, zero_state, *lw)
        k_past = cache_k[l, page_table].reshape(n_dec, past_len, FOX_HEADS, FOX_HEAD_DIM)
        v_past = cache_v[l, page_table].reshape(n_dec, past_len, FOX_HEADS, FOX_HEAD_DIM)
        f_past = cache_logf[l, page_table].reshape(n_dec, past_len, FOX_HEADS)
        attend_s = functools.partial(fox_attend_sample, k_past=k_past, v_past=v_past, logf_past=f_past)
        xs, ks, vs, fs, rs, is_ = trunk_layer(xs, c_sample, attend_s, state_ssm_re[l], state_ssm_im[l], *lw)
        kp_l.append(kp); vp_l.append(vp); fp_l.append(fp.astype(cache_logf.dtype))
        rp_l.append(rp.astype(state_ssm_re.dtype)); ip_l.append(ip.astype(state_ssm_im.dtype))
        ks_l.append(ks); vs_l.append(vs); fs_l.append(fs.astype(cache_logf.dtype))
        rs_l.append(rs.astype(state_ssm_re.dtype)); is_l.append(is_.astype(state_ssm_im.dtype))
    y_prompt = rms_norm(xp, g_final)
    y_sample = rms_norm(xs, g_final)
    return (y_prompt, y_sample,
            jnp.stack(kp_l), jnp.stack(vp_l), jnp.stack(fp_l), jnp.stack(rp_l), jnp.stack(ip_l),
            jnp.stack(ks_l), jnp.stack(vs_l), jnp.stack(fs_l), jnp.stack(rs_l), jnp.stack(is_l))


_drawn_inputs = setup_inputs


def setup_inputs(seed=0):
    import zlib

    import numpy as np

    out = dict(_drawn_inputs(seed))
    spreads = {}
    factors = {'b_ada': 2.812,
     'g_norm1': 3.012,
     'g_norm2': 36.559,
     'ssm_a_re': 61.594,
     'b_glu': 21.427,
     'g_attn_out': 94.91,
     'g_ssm_out': 111.318,
     'g_final': 22.469,
     'b_forget': 3.143}
    for name, (base, spread) in spreads.items():
        noise = np.random.default_rng([zlib.crc32(name.encode()), seed]).standard_normal(out[name].shape)
        drawn = base * np.exp(spread * noise) if base else spread * noise
        out[name] = __import__('jax').numpy.asarray(drawn.astype(out[name].dtype))
    for name, factor in factors.items():
        out[name] = (out[name] * factor).astype(out[name].dtype)
    return out
```

```python
import math
from contextlib import ExitStack

import concourse.bass as bass
import concourse.mybir as mybir
from concourse.alu_op_type import AluOpType as ALU

F32 = mybir.dt.float32
F32R = mybir.dt.float32r
BF16 = mybir.dt.bfloat16
I32 = mybir.dt.int32
U32 = mybir.dt.uint32
ACT = mybir.ActivationFunctionType
AX = mybir.AxisListType.X

P = 128
D = 2048
KC = D // P
NPR = 512
DB, DS = 8, 8
NSM = DB * DS
T = NPR + NSM
HT = T // 2
NC_ = 1 + DB
MODS = 6
NMOD = MODS * KC
H = 8
DH = 128
SCALE = DH ** -0.5
FW = H * DH
PAST, PAGE = 256, 128
NPG = PAST // PAGE
G, NST, CG = 64, 64, 16
SW = G * CG
LC = 8
NCK = NPR // LC
CK = NCK + DB
GB = P // CG
NGB = G // GB
PH, NK, TK = 8, 128, 16
EPS = 1e-6
NEG = -1e30
WB = 512
TB = 64
NTB = T // TB
NTT = -(-T // P)


class Chain:

    def __init__(self, eng, sem):
        self.eng, self.sem, self.n, self.base = eng, sem, 0, 0

    def __call__(self, ins):
        ins.then_inc(self.sem, 1)
        self.n += 1
        self.eng.wait_ge(self.sem, self.base + self.n)

    def mark(self, ins):
        ins.then_inc(self.sem, 1)
        self.n += 1

    def settle(self):
        self.eng.wait_ge(self.sem, self.base + self.n)

    def loop(self, i, per):
        self.start, self.per = self.n, per
        self.base = i * per

    def end_loop(self, count):
        assert self.n - self.start == self.per, (self.n - self.start, self.per)
        self.base = 0
        self.n = self.start + count * self.per


def fold(psum, n=HT):
    return psum[:, :, 0:n]


def halves(ap):
    return ap.rearrange("p (a t) -> p a t", a=2)


def bc(ap, axis, shape):
    return ap.unsqueeze(axis).broadcast_to(shape)


def project_inputs(nc, I, O, S, C, sem):
    ctx = ExitStack()
    sb = lambda n, s, d=F32: ctx.enter_context(nc.sbuf_tensor(n, s, d))
    ps = lambda n, s, d=F32: ctx.enter_context(nc.psum_tensor(n, s, d))
    with ctx:
        x = sb("x", [P, KC, T])
        ring = [sb(f"w_ring{u}", [P, KC, WB]) for u in range(2)]
        sq = [sb(f"sq{u}", [P, T]) for u in range(2)]
        std = sb("std", [P, T])
        rstd = sb("rstd", [P, T])
        c_in = sb("c_in", [P, KC, NC_])
        c_silu = sb("c_silu", [P, KC, NC_])
        b_ada = sb("b_ada", [P, NMOD])
        g1 = sb("g1", [P, KC])
        scale1 = sb("scale1", [P, KC, NC_])
        row = [sb(f"row{u}", [NC_, WB]) for u in range(2)]
        w_fg = sb("w_fg", [P, KC, H])
        b_fg = sb("b_fg", [H, 1])
        fg, fg_abs, fg_e, fg_s, fg_s2, fg_acc = (sb(n, [H, T]) for n in
                                                 ("fg", "fg_abs", "fg_e", "fg_s", "fg_s2", "fg_acc"))
        ps_norm = ps("ps_norm", [P, 2, 512])
        ps_row = [ps(f"ps_row{u}", [P, 512]) for u in range(2)]
        ps_out = [ps(f"ps_proj{q}", [P, 2, 512]) for q in range(2)]
        ps_mod = [ps_out[u][:, 0, :] for u in range(2)]
        mod, qkvu, logf = S["mod"], S["qkvu"], S["logf"]

        x_in, small_in, w_full = sem("x_in"), sem("small_in"), [sem(f"w_full{u}") for u in range(2)]
        fg_in = sem("fg_in")
        silu_done, sq_done, sq_used = sem("silu_done"), sem("sq_done"), sem("sq_used")
        norm_sum, std_done = sem("norm_sum"), sem("std_done")
        row_done = [sem(f"row_done{u}") for u in range(2)]
        row_copied = [sem(f"row_copied{u}") for u in range(2)]
        mod_t = [sem(f"mod_t{u}") for u in range(2)]
        mod_done = [sem(f"mod_done{u}") for u in range(2)]
        scale_done, h_prompt, h_sample = sem("scale_done"), sem("h_prompt"), sem("h_sample")
        xn_done = sem("xn_done")
        proj_done = [sem(f"proj_done{q}") for q in range(2)]
        proj_copied = [sem(f"proj_copied{q}") for q in range(2)]
        fg_done, fg_copied, fg_abs_done, fg_exp_done, logf_done = (sem(n) for n in
                                                                   ("fg_done", "fg_copied", "fg_abs_done", "fg_exp_done", "logf_done"))
        kv_out = sem("kv_out")
        v_step = sem("proj_v_step")
        held = sem("proj_held")
        NA = NMOD * P // WB // 2
        NW = 32 * P // WB // 2

        block = ctx.enter_context(nc.Block())

        @block.sync
        def _(sp):
            w_ada = I["w_ada"].rearrange("(k p) (b c) -> b p k c", p=P, c=WB)
            w_in = I["w_in"].rearrange("(k p) (b c) -> b p k c", p=P, c=WB)
            sp.dma_start(x[:], I["xT"].rearrange("(k p) t -> p k t", p=P)).then_inc(x_in, 16)
            for u in range(2):
                sp.dma_start(ring[u][:], w_ada[u]).then_inc(w_full[u], 16)
            with sp.Fori(1, NA) as i:
                for u in range(2):
                    sp.wait_ge(row_done[u], i)
                    sp.dma_start(ring[u][:], w_ada[bass.ds(2 * i + u, 1)].rearrange("b p k c -> p (b k) c")
                                 ).then_inc(w_full[u], 16)
            for u in range(2):
                sp.wait_ge(row_done[u], NA)
                sp.dma_start(ring[u][:], w_in[u]).then_inc(w_full[u], 16)
            with sp.Fori(1, NW) as i:
                for u in range(2):
                    sp.wait_ge(proj_done[1], 4 * i + 2 * u - 2)
                    sp.dma_start(ring[u][:], w_in[bass.ds(2 * i + u, 1)].rearrange("b p k c -> p (b k) c")
                                 ).then_inc(w_full[u], 16)
            sp.wait_ge(proj_copied[0], 8 * NW // 2)
            sp.wait_ge(proj_copied[1], 8 * NW // 2)
            sp.dma_start(O["kvT"].rearrange("(c p) t -> p c t", p=P), qkvu[:, H:3 * H, :]).then_inc(kv_out, 16)
            sp.wait_ge(logf_done, 1)
            sp.dma_start(O["logfT"], logf[:]).then_inc(kv_out, 16)
            sp.wait_ge(kv_out, 32)

        @block.scalar
        def _(act):
            act.dma_start(c_in[:], I["cT"].rearrange("(k p) r -> p k r", p=P)).then_inc(small_in, 16)
            act.dma_start(b_ada[:], I["b_adaT"]).then_inc(small_in, 16)
            act.dma_start(g1[:], I["g1T"]).then_inc(small_in, 16)
            act.dma_start(w_fg[:], I["w_fg"].rearrange("(k p) h -> p k h", p=P)).then_inc(fg_in, 16)
            act.dma_start(b_fg[:], I["b_fg"]).then_inc(fg_in, 16)
            act.wait_ge(small_in, 48)
            act.activation(c_silu[:], c_in[:], ACT.Silu).then_inc(silu_done, 1)
            act.wait_ge(x_in, 16)
            for c in range(KC):
                if c >= 2:
                    act.wait_ge(sq_used, c - 1)
                act.activation(sq[c % 2][:], x[:, c, :], ACT.Square).then_inc(sq_done, 1)
            act.wait_ge(norm_sum, 1)
            act.activation(halves(std[:]), fold(ps_norm), ACT.Sqrt, scale=1.0 / D, bias=C["eps"][:, 0:1]
                           ).then_inc(std_done, 1)
            with act.Fori(0, NA) as i:
                for u in range(2):
                    act.wait_ge(row_done[u], i + 1)
                    act.wait_ge(mod_t[u], i)
                    act.activation(row[u][:], ps_row[u][0:NC_, :], ACT.Copy).then_inc(row_copied[u], 1)
            act.wait_ge(scale_done, 1)
            act.wait_ge(xn_done, 1)
            for c in range(KC):
                act.activation(x[:, c, 0:NPR], x[:, c, 0:NPR], ACT.Identity, scale=scale1[:, c, 0:1],
                               bias=mod[:, c, 0:1]).then_inc(h_prompt, 1)
            with act.Fori(0, 2 * NW) as i:
                for m in range(2):
                    act.wait_ge(proj_done[1], 2 * i + m + 1)
                    act.activation(qkvu[:, bass.ds(4 * i + 2 * m + 1, 1), :].rearrange("p c (a t) -> p (c a) t", a=2),
                                   fold(ps_out[1]), ACT.Copy).then_inc(proj_copied[1], 1)
            act.wait_ge(fg_copied, 1)
            act.activation(fg_abs[:], fg[:], ACT.Abs).then_inc(fg_abs_done, 1)
            act.wait_ge(fg_abs_done, 1)
            act.activation(fg_e[:], fg_abs[:], ACT.Exp, scale=-1.0).then_inc(fg_exp_done, 1)

        @block.tensor
        def _(pe):
            for c in range(KC):
                pe.wait_ge(sq_done, c + 1)
                for a in range(2):
                    mm = pe.matmul(ps_norm[:, a, 0:HT], C["ones"][:], sq[c % 2][:, a * HT:(a + 1) * HT],
                                   start=(c == 0), stop=(c == KC - 1))
                if c < KC - 1:
                    mm.then_inc(sq_used, 1)
            mm.then_inc(norm_sum, 1)
            pe.wait_ge(silu_done, 1)
            with pe.Fori(0, NA) as i:
                for u in range(2):
                    pe.wait_ge(w_full[u], 16 * i + 16)
                    pe.wait_ge(row_copied[u], i)
                    for k in range(KC):
                        mm = pe.matmul(ps_row[u][0:NC_, :], c_silu[:, k, :], ring[u][:, k, :],
                                       start=(k == 0), stop=(k == KC - 1))
                    mm.then_inc(row_done[u], 1)
                for u in range(2):
                    pe.wait_ge(row_copied[u], i + 1)
                    pe.wait_ge(mod_done[u], i)
                    pe.sem_inc(held, 1)
                    for j in range(WB // P):
                        mm = pe.transpose(ps_mod[u][:, j * NC_:(j + 1) * NC_], row[u][:, j * P:(j + 1) * P],
                                          C["ident"][0:NC_, 0:NC_])
                    mm.then_inc(mod_t[u], 1)
            pe.wait_ge(h_prompt, KC)
            pe.wait_ge(h_sample, 1)
            for u in range(2):
                pe.wait_ge(mod_done[u], NA)
            with pe.Fori(0, NW) as i:
                for u in range(2):
                    pe.wait_ge(w_full[u], 16 * (NA + 1) + 16 * i)
                    for m in range(4):
                        q = m % 2
                        pe.wait_ge(proj_copied[q], 4 * i + 2 * u + m // 2)
                        for k in range(KC):
                            for a in range(2):
                                mm = pe.matmul(ps_out[q][:, a, 0:HT], ring[u][:, k, m * P:(m + 1) * P],
                                               x[:, k, a * HT:(a + 1) * HT], start=(k == 0), stop=(k == KC - 1))
                        mm.then_inc(proj_done[q], 1)
            pe.wait_ge(fg_in, 32)
            pe.wait_ge(std_done, 1)
            for k in range(KC):
                for a in range(2):
                    mm = pe.matmul(ps_norm[0:H, a, 0:HT], w_fg[:, k, :], x[:, k, a * HT:(a + 1) * HT],
                                   start=(k == 0), stop=(k == KC - 1))
            mm.then_inc(fg_done, 1)

        @block.vector
        def _(dve):
            step = Chain(dve, v_step)
            dve.wait_ge(std_done, 1)
            step(dve.reciprocal(rstd[:], std[:]))
            for c in range(KC):
                ins = dve.tensor_tensor(x[:, c, :], x[:, c, :], rstd[:], ALU.mult)
                if c == KC - 1:
                    ins.then_inc(xn_done, 1)
                else:
                    step.mark(ins)
            dve.wait_ge(small_in, 48)
            with dve.Fori(0, NA) as i:
                for u in range(2):
                    dve.wait_ge(mod_t[u], i + 1)
                    dve.tensor_tensor(mod[:, bass.ds((2 * i + u) * 4, 4), :],
                                      ps_mod[u][:, 0:4 * NC_].rearrange("p (j r) -> p j r", j=4),
                                      bc(b_ada[:, bass.ds((2 * i + u) * 4, 4)], 2, [P, 4, NC_]), ALU.add
                                      ).then_inc(mod_done[u], 1)
            for u in range(2):
                dve.wait_ge(mod_done[u], NA)
            dve.wait_ge(xn_done, 1)
            step.settle()
            step(dve.tensor_scalar(scale1[:], mod[:, KC:2 * KC, :], 1.0, None, ALU.add))
            dve.tensor_tensor(scale1[:], scale1[:], bc(g1[:], 2, [P, KC, NC_]), ALU.mult).then_inc(scale_done, 1)
            dve.wait_ge(scale_done, 1)
            xs = x[:, :, NPR:T].rearrange("p c (b t) -> p c b t", b=DB)
            step(dve.tensor_tensor(xs, xs, bc(scale1[:, :, 1:NC_], 3, [P, KC, DB, DS]), ALU.mult))
            dve.tensor_tensor(xs, xs, bc(mod[:, 0:KC, 1:NC_], 3, [P, KC, DB, DS]), ALU.add).then_inc(h_sample, 1)
            with dve.Fori(0, 2 * NW) as i:
                for m in range(2):
                    dve.wait_ge(proj_done[0], 2 * i + m + 1)
                    dve.tensor_copy(qkvu[:, bass.ds(4 * i + 2 * m, 1), :].rearrange("p c (a t) -> p (c a) t", a=2),
                                    fold(ps_out[0])).then_inc(proj_copied[0], 1)
            dve.wait_ge(fg_done, 1)
            dve.wait_ge(fg_in, 32)
            dve.tensor_scalar(halves(fg[:]), ps_norm[0:H, :, 0:HT], b_fg[:, 0:1], None, ALU.add
                              ).then_inc(fg_copied, 1)
            dve.wait_ge(fg_exp_done, 1)
            step(dve.tensor_scalar(fg[:], fg[:], 0.0, None, ALU.min))
            step(dve.tensor_scalar(fg_s[:], fg_e[:], 2.0, None, ALU.add))
            step(dve.reciprocal(fg_s[:], fg_s[:]))
            step(dve.tensor_tensor(fg_s[:], fg_s[:], fg_e[:], ALU.mult))
            step(dve.tensor_tensor(fg_s2[:], fg_s[:], fg_s[:], ALU.mult))
            step(dve.tensor_scalar(fg_acc[:], fg_s2[:], 1.0 / 17, None, ALU.mult))
            for n in (15, 13, 11, 9, 7, 5, 3):
                step(dve.scalar_tensor_tensor(fg_acc[:], fg_acc[:], 1.0 / n, fg_s2[:], ALU.add, ALU.mult))
            step(dve.scalar_tensor_tensor(fg_acc[:], fg_acc[:], 1.0, fg_s[:], ALU.add, ALU.mult))
            dve.scalar_tensor_tensor(logf[:], fg_acc[:], -2.0, fg[:], ALU.mult, ALU.add).then_inc(logf_done, 1)


def attend_prompt(nc, I, O, S, C, sem):
    ctx = ExitStack()
    sb = lambda n, s, d=F32: ctx.enter_context(nc.sbuf_tensor(n, s, d))
    ps = lambda n, s, d=F32: ctx.enter_context(nc.psum_tensor(n, s, d))
    NQ = NPR // P
    with ctx:
        qkvu, logf, att = S["qkvu"], S["logf"], S["att"]
        fcum = sb("fcum_p", [H, NPR])
        ones_row = sb("ones_row_p", [H, NPR])
        sel = sb("sel_neg_p", [H, H, P])
        tri = sb("tri", [P, P])
        fk = sb("fk", [P, H, NPR])
        fk_diag = sb("fk_diag", [P, H, NQ, P])
        fq = sb("fq", [P, H, NQ])
        q_st = [sb(f"q_st{u}", [P, NPR]) for u in range(2)]
        v_st = [sb(f"v_st{u}", [P, NPR]) for u in range(2)]
        v_tok = [sb(f"v_tok{u}", [P, NQ, DH]) for u in range(2)]
        s_sb = sb("s_sb", [P, NQ, NPR])
        prob = sb("prob", [P, NQ, NPR])
        p_t = [sb(f"p_t{j}", [P, NPR]) for j in range(2)]
        mx, top, bias, rsum, rinv = (sb(n, [P, NQ]) for n in ("mx", "top", "bias", "rsum", "rinv"))
        ps_s = [ps(f"ps_s{j}", [P, 512]) for j in range(NQ)]
        ps_pt = [ps(f"ps_pt{j}", [P, 512]) for j in range(2)]
        ps_o = ps("ps_o", [P, 512])
        ps_v = ps("ps_v", [P, 512])

        masks, masks_in = sem("ones_row_p_ready"), sem("masks_p_in")
        fcum_done, fk_sum, fk_copied = sem("fcum_p_done"), sem("fk_sum"), sem("fk_copied")
        fq_t, fq_done, fkd_done = sem("fq_t"), sem("fq_done"), sem("fkd_done")
        q_staged, v_staged = sem("q_staged"), sem("v_staged")
        v_turned, v_copied = sem("v_turned"), sem("v_copied")
        s_done, s_read = sem("s_done"), sem("s_read")
        bias_done, p_exp, p_norm = sem("bias_done"), sem("p_exp"), sem("p_norm")
        pt_turned, pt_copied = sem("pt_turned"), sem("pt_copied")
        o_done, o_copied = sem("o_done"), sem("o_copied")
        v_step = sem("attp_v_step")

        block = ctx.enter_context(nc.Block())

        @block.gpsimd
        def _(pool):
            pool.memset(ones_row[:], 1.0).then_inc(masks, 1)

        @block.sync
        def _(sp):
            sp.dma_start(sel[:], I["sel_neg"]).then_inc(masks_in, 16)
            sp.dma_start(tri[:], I["tri"]).then_inc(masks_in, 16)

        @block.scalar
        def _(act):
            for h in range(H):
                act.wait_ge(fk_sum, h + 1)
                act.activation(fk[:, h, :], ps_s[h % NQ][:], ACT.Copy).then_inc(fk_copied, 1)

            def stage_q(h, u):
                act.activation(q_st[u][:], qkvu[:, bass.ds(h, 1), 0:NPR].rearrange("p c t -> p (c t)"), ACT.Copy
                               ).then_inc(q_staged, 1)

            def softmax(h):
                act.wait_ge(bias_done, h + 1)
                act.wait_ge(pt_turned, NQ * h)
                for j in range(NQ):
                    n = (j + 1) * P
                    act.activation(prob[:, j, 0:n], s_sb[:, j, 0:n], ACT.Exp, scale=SCALE, bias=bias[:, j:j + 1],
                                   accum_out=rsum[:, j:j + 1]).then_inc(p_exp, 1)

            def copy_turned(h):
                for j in range(NQ):
                    n = (j + 1) * P
                    act.wait_ge(pt_turned, NQ * h + j + 1)
                    if j >= 1:
                        act.wait_ge(o_done, NQ * h + j - 1)
                    act.activation(p_t[j % 2][:, 0:n], ps_pt[j % 2][:, 0:n], ACT.Copy).then_inc(pt_copied, 1)

            stage_q(0, 0)
            stage_q(1, 1)
            with act.Fori(0, H // 2 - 1) as i:
                for u in range(2):
                    softmax(2 * i + u)
                    stage_q(2 * i + u + 2, u)
                    copy_turned(2 * i + u)
            for h in range(H - 2, H):
                softmax(h)
                copy_turned(h)

        @block.tensor
        def _(pe):
            pe.wait_ge(masks_in, 32)
            pe.wait_ge(fcum_done, 1)
            for h in range(H):
                if h >= NQ:
                    pe.wait_ge(fk_copied, h - NQ + 1)
                pe.matmul(ps_s[h % NQ][:], sel[:, h, :], fcum[:], start=True, stop=True).then_inc(fk_sum, 1)
            for j in range(NQ):
                mm = pe.transpose(ps_o[:, j * H:(j + 1) * H], fcum[:, j * P:(j + 1) * P], C["ident"][0:H, 0:H])
            mm.then_inc(fq_t, 1)
            pe.wait_ge(fk_copied, H)
            pe.wait_ge(fq_done, 1)

            def scores(h, u):
                pe.wait_ge(q_staged, h + 1)
                pe.wait_ge(s_read, NQ * h)
                for j in range(NQ):
                    pe.matmul(ps_s[j][:, 0:(j + 1) * P], q_st[u][:, j * P:(j + 1) * P],
                              qkvu[:, bass.ds(H + h, 1), 0:(j + 1) * P].rearrange("p c t -> p (c t)"),
                              start=True, stop=True).then_inc(s_done, 1)
                pe.wait_ge(v_staged, h + 1)
                pe.wait_ge(v_copied, h)
                for j in range(NQ):
                    mm = pe.transpose(ps_v[:, j * P:(j + 1) * P], v_st[u][:, j * P:(j + 1) * P], C["ident"][:])
                mm.then_inc(v_turned, 1)

            def values(h, u):
                pe.wait_ge(v_copied, h + 1)
                pe.wait_ge(p_norm, h + 1)
                pe.wait_ge(o_copied, h)

                def turn(j):
                    if j >= 2:
                        pe.wait_ge(pt_copied, NQ * h + j - 1)
                    else:
                        pe.wait_ge(pt_copied, NQ * h)
                    for b in range(j + 1):
                        mm = pe.transpose(ps_pt[j % 2][:, b * P:(b + 1) * P], prob[:, j, b * P:(b + 1) * P],
                                          C["ident"][:])
                    mm.then_inc(pt_turned, 1)

                turn(0)
                for j in range(NQ):
                    if j + 1 < NQ:
                        turn(j + 1)
                    pe.wait_ge(pt_copied, NQ * h + j + 1)
                    for b in range(j + 1):
                        mm = pe.matmul(ps_o[:, j * P:(j + 1) * P], v_tok[u][:, b, :],
                                       p_t[j % 2][:, b * P:(b + 1) * P], start=(b == 0), stop=(b == j))
                    mm.then_inc(o_done, 1)

            scores(0, 0)
            with pe.Fori(0, H // 2 - 1) as i:
                for u in range(2):
                    scores(2 * i + u + 1, 1 - u)
                    values(2 * i + u, u)
            scores(H - 1, 1)
            values(H - 2, 0)
            values(H - 1, 1)

        @block.vector
        def _(dve):
            step = Chain(dve, v_step)
            dve.wait_ge(masks, 1)
            dve.wait_ge(masks_in, 32)
            dve.tensor_tensor_scan(fcum[:], ones_row[:], logf[:, 0:NPR], 0.0, ALU.mult, ALU.add
                                   ).then_inc(fcum_done, 1)
            dve.wait_ge(fq_t, 1)
            dve.tensor_copy(fq[:].rearrange("p h j -> p j h"), ps_o[:, 0:NQ * H].rearrange("p (j h) -> p j h", j=NQ)
                            ).then_inc(fq_done, 1)
            dve.wait_ge(fk_copied, H)
            for h in range(H):
                dve.tensor_tensor(fk_diag[:, h], fk[:, h, :].rearrange("p (j k) -> p j k", j=NQ),
                                  bc(tri[:], 1, [P, NQ, P]), ALU.add).then_inc(fkd_done, 1)
            dve.wait_ge(fkd_done, H)
            dve.wait_ge(fq_done, 1)

            def stage_v(h, u):
                dve.tensor_copy(v_st[u][:], qkvu[:, bass.ds(2 * H + h, 1), 0:NPR].rearrange("p c t -> p (c t)")
                                ).then_inc(v_staged, 1)

            def maxima(h):
                dve.wait_ge(p_exp, NQ * h)
                for j in range(NQ):
                    dve.wait_ge(s_done, NQ * h + j + 1)
                    n = j * P
                    if j:
                        step.mark(dve.tensor_tensor(s_sb[:, j, 0:n], ps_s[j][:, 0:n],
                                                    fk[:, bass.ds(h, 1), 0:n].rearrange("p c t -> p (c t)"), ALU.add))
                    dve.tensor_tensor(s_sb[:, j, n:n + P], ps_s[j][:, n:n + P],
                                      fk_diag[:, bass.ds(h, 1), j, :].rearrange("p c t -> p (c t)"), ALU.add
                                      ).then_inc(s_read, 1)
                step.settle()
                dve.wait_ge(s_read, NQ * h + NQ)
                for j in range(NQ):
                    step.mark(dve.tensor_reduce(mx[:, j:j + 1], s_sb[:, j, 0:(j + 1) * P], AX, ALU.max))
                step.settle()
                fq_h = fq[:, bass.ds(h, 1), :].rearrange("p c j -> p (c j)")
                step(dve.scalar_tensor_tensor(top[:], mx[:], SCALE, fq_h, ALU.mult, ALU.add))
                dve.scalar_tensor_tensor(bias[:], top[:], -1.0, fq_h, ALU.mult, ALU.add).then_inc(bias_done, 1)

            def copy_v(h, u):
                dve.wait_ge(v_turned, h + 1)
                dve.tensor_copy(v_tok[u][:].rearrange("p j d -> p (j d)"), ps_v[:]).then_inc(v_copied, 1)

            def normalise(h):
                dve.wait_ge(p_exp, NQ * h + NQ)
                step(dve.reciprocal(rinv[:], rsum[:]))
                for j in range(NQ):
                    n = (j + 1) * P
                    ins = dve.tensor_scalar(prob[:, j, 0:n], prob[:, j, 0:n], rinv[:, j:j + 1], None, ALU.mult)
                    step.mark(ins) if j < NQ - 1 else ins.then_inc(p_norm, 1)

            def copy_out(h):
                dve.wait_ge(o_done, NQ * h + NQ)
                dve.tensor_copy(att[:, bass.ds(h, 1), 0:NPR].rearrange("p c t -> p (c t)"), ps_o[:]
                                ).then_inc(o_copied, 1)

            stage_v(0, 0)
            stage_v(1, 1)
            maxima(0)
            copy_v(0, 0)
            with dve.Fori(0, H // 2 - 1) as i:
                step.loop(i, 2 * (NQ + NQ + NQ))
                for u in range(2):
                    normalise(2 * i + u)
                    stage_v(2 * i + u + 2, u)
                    maxima(2 * i + u + 1)
                    copy_out(2 * i + u)
                    copy_v(2 * i + u + 1, 1 - u)
                step.end_loop(H // 2 - 1)
            normalise(H - 2)
            maxima(H - 1)
            copy_out(H - 2)
            copy_v(H - 1, 1)
            normalise(H - 1)
            copy_out(H - 1)


def attend_sample(nc, I, O, S, C, sem):
    ctx = ExitStack()
    sb = lambda n, s, d=F32: ctx.enter_context(nc.sbuf_tensor(n, s, d))
    ps = lambda n, s, d=F32: ctx.enter_context(nc.psum_tensor(n, s, d))
    R = H * DS
    KW = PAST + NSM
    with ctx:
        qkvu, logf, att = S["qkvu"], S["logf"], S["att"]
        pages = sb("pages", [1, DB * NPG], I32)
        lf_past = sb("lf_past", [H, DB, PAST])
        fc_past = sb("fc_past", [H, DB, PAST])
        fc_new = sb("fc_new", [H, NSM])
        ones_row = sb("ones_row_s", [H, PAST])
        sel_neg = sb("sel_neg_s", [H, R])
        sel_pos = sb("sel_pos_s", [H, R])
        mask = sb("mask_s", [R, DB, NSM])
        own_q = sb("own_q", [R, DS])
        fk = sb("fk_s", [R, DB, KW])
        fq_all = sb("fq_all", [R, DB, DS])
        fq = sb("fq_s", [R, DB])
        k_pg = [sb(f"k_pg{u}", [P, NPG, FW]) for u in range(2)]
        v_pg = [sb(f"v_pg{u}", [P, NPG, FW]) for u in range(2)]
        k_t = sb("k_t", [P, H, PAST])
        q_blk = [sb(f"q_blk{u}", [P, H * (R + DS)]) for u in range(2)]
        v_new = sb("v_new", [NSM, FW])
        s_sb = sb("s_sb_s", [R, KW])
        prob = sb("prob_s", [R, KW])
        p_t = sb("p_t_s", [P, 3 * R])
        mx, top, bias, rsum, rinv = (sb(n, [R, 1]) for n in ("mx_s", "top_s", "bias_s", "rsum_s", "rinv_s"))
        ps_k = ps("ps_k", [P, 4, 512])
        ps_s = ps("ps_s_s", [P, 512])
        ps_t = ps("ps_t_s", [P, 512])
        ps_o = ps("ps_o_s", [P, 512])
        ps_x = ps("ps_x_s", [P, 512])

        pages_in, consts_in, lf_in = sem("pages_in"), sem("consts_s_in"), sem("lf_in")
        k_in = [sem(f"k_in{u}") for u in range(2)]
        v_in = [sem(f"v_in{u}") for u in range(2)]
        cleared, fc_done = sem("cleared"), sem("fc_s_done")
        fk_sum, fk_done, fq_sum, fq_done = sem("fk_s_sum"), sem("fk_s_done"), sem("fq_s_sum"), sem("fq_s_done")
        vn_turned, vn_copied = sem("vn_turned"), sem("vn_copied")
        kt_turned, kt_copied_a, kt_copied_v = sem("kt_turned"), sem("kt_copied_a"), sem("kt_copied_v")
        q_done, s_done, bias_done, p_exp, p_norm = (sem(n) for n in ("q_blk_done", "s_s_done", "bias_s_done",
                                                                   "p_s_exp", "p_s_norm"))
        pt_turned, pt_copied, o_done, o_copied = (sem(n) for n in ("pt_s_turned", "pt_s_copied", "o_s_done",
                                                                 "o_s_copied"))
        v_step = sem("atts_v_step")
        held = sem("atts_held")

        block = ctx.enter_context(nc.Block())

        @block.sync
        def _(sp):
            sp.dma_start(pages[:], I["pages"]).then_inc(pages_in, 16)
            sp.dma_start(sel_neg[:], I["sel_neg_s"]).then_inc(consts_in, 16)
            sp.dma_start(sel_pos[:], I["sel_pos_s"]).then_inc(consts_in, 16)
            sp.dma_start(mask[:], I["mask_s"]).then_inc(consts_in, 16)
            sp.dma_start(own_q[:], I["own_q"]).then_inc(consts_in, 16)
            sp.wait_ge(pages_in, 16)

            def load(b, u):
                for g in range(NPG):
                    page = sp.value_load(pages[0:1, bass.ds(b * NPG + g, 1)], min_val=0, max_val=I["cache_k"].shape[0] - 1)
                    sp.dma_start(k_pg[u][:, g, :], I["cache_k"][bass.ds(page, 1)].rearrange("a t n -> t (a n)")
                                 ).then_inc(k_in[u], 16)
                    sp.dma_start(v_pg[u][:, g, :], I["cache_v"][bass.ds(page, 1)].rearrange("a t n -> t (a n)")
                                 ).then_inc(v_in[u], 16)

            load(0, 0)
            load(1, 1)
            with sp.Fori(1, DB // 2) as i:
                for u in range(2):
                    sp.wait_ge(o_done, 2 * i + u - 1)
                    load(2 * i + u, u)

        @block.gpsimd
        def _(pool):
            pool.memset(ones_row[:], 1.0).then_inc(cleared, 1)
            for u in range(2):
                pool.memset(q_blk[u][:], 0.0).then_inc(cleared, 1)
            pool.wait_ge(pages_in, 16)
            for b in range(DB):
                for g in range(NPG):
                    page = pool.value_load(pages[0:1, b * NPG + g:b * NPG + g + 1], min_val=0,
                                           max_val=I["cache_k"].shape[0] - 1)
                    pool.dma_start(lf_past[:, b, g * PAGE:(g + 1) * PAGE],
                                   I["cache_lfT"][bass.ds(page, 1)].rearrange("a h t -> (a h) t")).then_inc(lf_in, 16)

        @block.scalar
        def _(act):
            act.wait_ge(vn_turned, 1)
            act.activation(v_new[:].rearrange("p (a n) -> p a n", a=2), ps_k[0:NSM, 0:2, :], ACT.Copy
                           ).then_inc(vn_copied, 1)

            def copy_keys(b):
                act.wait_ge(kt_turned, b + 1)
                act.wait_ge(s_done, b)
                act.activation(k_t[:, 0:4, :], ps_k[:, 0:2, :], ACT.Copy).then_inc(kt_copied_a, 1)

            def softmax(b):
                act.wait_ge(bias_done, b + 1)
                act.wait_ge(pt_turned, b)
                act.activation(prob[:], s_sb[:], ACT.Exp, scale=SCALE, bias=bias[:], accum_out=rsum[:]
                               ).then_inc(p_exp, 1)

            def copy_turned(b):
                act.wait_ge(pt_turned, b + 1)
                act.wait_ge(o_done, b)
                act.activation(p_t[:, 0:2 * R], ps_t[:, 0:2 * R], ACT.Copy).then_inc(pt_copied, 1)
                act.activation(p_t[0:NSM, 2 * R:3 * R], ps_t[0:NSM, 2 * R:3 * R], ACT.Copy).then_inc(pt_copied, 1)

            copy_keys(0)
            with act.Fori(0, DB - 1) as b:
                softmax(b)
                copy_keys(b + 1)
                copy_turned(b)
            softmax(DB - 1)
            copy_turned(DB - 1)

        @block.tensor
        def _(pe):
            for h in range(H):
                mm = pe.transpose(ps_k[0:NSM, h // 4, (h % 4) * P:(h % 4 + 1) * P], qkvu[:, 2 * H + h, NPR:T],
                                  C["ident"][:])
            mm.then_inc(vn_turned, 1)
            pe.wait_ge(consts_in, 64)
            pe.wait_ge(fc_done, 2 * DB)
            pe.matmul(ps_o[0:R, 0:NSM], sel_pos[:], fc_new[:], start=True, stop=True).then_inc(fq_sum, 1)
            for b in range(DB):
                if b:
                    pe.wait_ge(fk_done, 2 * b)
                pe.matmul(ps_s[0:R, 0:PAST], sel_neg[:], fc_past[:, b, :], start=True, stop=True)
                pe.matmul(ps_s[0:R, PAST:KW], sel_neg[:], fc_new[:], start=True, stop=True).then_inc(fk_sum, 1)
            pe.wait_ge(vn_copied, 1)
            pe.wait_ge(fk_done, 2 * DB)
            pe.wait_ge(fq_done, 2)

            def turn_keys(b, u, turn):
                pe.wait_ge(k_in[u], 32 * turn)
                pe.wait_ge(kt_copied_a, b)
                pe.wait_ge(kt_copied_v, b)
                for h in range(H):
                    for g in range(NPG):
                        mm = pe.transpose(ps_k[:, h // 2, (h % 2) * PAST + g * P:(h % 2) * PAST + (g + 1) * P],
                                          k_pg[u][:, g, h * DH:(h + 1) * DH], C["ident"][:])
                mm.then_inc(kt_turned, 1)

            def scores(b, u):
                pe.wait_ge(kt_copied_a, b + 1)
                pe.wait_ge(kt_copied_v, b + 1)
                pe.wait_ge(q_done, b + 1)
                for h in range(H):
                    pe.matmul(ps_s[0:R, 0:PAST], q_blk[u][:, h * R:(h + 1) * R], k_t[:, h, :],
                              start=(h == 0), stop=(h == H - 1))
                for h in range(H):
                    mm = pe.matmul(ps_s[0:R, PAST:KW], q_blk[u][:, h * R:(h + 1) * R], qkvu[:, H + h, NPR:T],
                                   start=(h == 0), stop=(h == H - 1))
                mm.then_inc(s_done, 1)

            def values(b, u, turn):
                pe.wait_ge(p_norm, b + 1)
                pe.wait_ge(pt_copied, 2 * b)
                pe.sem_inc(held, 1)
                pe.transpose(ps_t[:, 0:R], prob[:, 0:P], C["ident"][0:R, 0:R])
                pe.transpose(ps_t[:, R:2 * R], prob[:, P:2 * P], C["ident"][0:R, 0:R])
                pe.transpose(ps_t[0:NSM, 2 * R:3 * R], prob[:, PAST:KW], C["ident"][0:R, 0:R]).then_inc(pt_turned, 1)
                pe.wait_ge(pt_copied, 2 * b + 2)
                pe.wait_ge(v_in[u], 32 * turn)
                pe.wait_ge(o_copied, b)
                for h in range(H):
                    q = slice(h * DS, (h + 1) * DS)
                    for g in range(NPG):
                        pe.matmul(ps_o[:, q], v_pg[u][:, g, h * DH:(h + 1) * DH],
                                  p_t[:, g * R + h * DS:g * R + (h + 1) * DS], start=(g == 0), stop=False)
                    mm = pe.matmul(ps_o[:, q], v_new[:, h * DH:(h + 1) * DH],
                                   p_t[0:NSM, 2 * R + h * DS:2 * R + (h + 1) * DS], start=False, stop=True)
                mm.then_inc(o_done, 1)

            turn_keys(0, 0, 1)
            with pe.Fori(0, DB // 2 - 1) as i:
                for u in range(2):
                    b = 2 * i + u
                    scores(b, u)
                    turn_keys(b + 1, 1 - u, i + 1 + u)
                    values(b, u, i + 1)
            scores(DB - 2, 0)
            turn_keys(DB - 1, 1, DB // 2)
            values(DB - 2, 0, DB // 2)
            scores(DB - 1, 1)
            values(DB - 1, 1, DB // 2)

        @block.vector
        def _(dve):
            step = Chain(dve, v_step)
            dve.wait_ge(cleared, 3)
            dve.wait_ge(lf_in, 16 * DB * NPG)
            for b in range(DB):
                dve.tensor_tensor_scan(fc_past[:, b, :], ones_row[:], lf_past[:, b, :], 0.0, ALU.mult, ALU.add
                                       ).then_inc(fc_done, 1)
            dve.wait_ge(fc_done, DB)
            for b in range(DB):
                dve.tensor_tensor_scan(fc_new[:, b * DS:(b + 1) * DS], ones_row[:, 0:DS],
                                       logf[:, NPR + b * DS:NPR + (b + 1) * DS], fc_past[:, b, PAST - 1:PAST],
                                       ALU.mult, ALU.add).then_inc(fc_done, 1)
            dve.wait_ge(consts_in, 64)
            dve.wait_ge(fq_sum, 1)
            dve.tensor_tensor(fq_all[:], ps_o[0:R, 0:NSM].rearrange("p (b t) -> p b t", b=DB),
                              bc(own_q[:], 1, [R, DB, DS]), ALU.mult).then_inc(fq_done, 1)
            dve.wait_ge(fq_done, 1)
            dve.tensor_reduce(fq[:], fq_all[:], AX, ALU.add).then_inc(fq_done, 1)
            for b in range(DB):
                dve.wait_ge(fk_sum, b + 1)
                dve.tensor_copy(fk[:, b, 0:PAST], ps_s[0:R, 0:PAST]).then_inc(fk_done, 1)
                dve.tensor_tensor(fk[:, b, PAST:KW], ps_s[0:R, PAST:KW], mask[:, b, :], ALU.add).then_inc(fk_done, 1)
            dve.wait_ge(fk_done, 2 * DB)
            dve.wait_ge(fq_done, 2)

            def spread_queries(b, u):
                dve.tensor_copy(q_blk[u][:].rearrange("p (h x) -> p h x", h=H)[:, :, 0:DS],
                                qkvu[:, 0:H, bass.ds(NPR + b * DS, DS)]).then_inc(q_done, 1)

            def copy_keys(b):
                dve.wait_ge(kt_turned, b + 1)
                dve.wait_ge(s_done, b)
                dve.tensor_copy(k_t[:, 4:8, :].rearrange("p (a h) k -> p a (h k)", a=2), ps_k[:, 2:4, :]
                                ).then_inc(kt_copied_v, 1)

            def maxima(b):
                dve.wait_ge(s_done, b + 1)
                dve.wait_ge(p_exp, b)
                step(dve.tensor_tensor(s_sb[:], ps_s[0:R, 0:KW],
                                       fk[:, bass.ds(b, 1), :].rearrange("p c t -> p (c t)"), ALU.add))
                step(dve.tensor_reduce(mx[:], s_sb[:], AX, ALU.max))
                step(dve.scalar_tensor_tensor(top[:], mx[:], SCALE, fq[:, bass.ds(b, 1)], ALU.mult, ALU.add))
                dve.scalar_tensor_tensor(bias[:], top[:], -1.0, fq[:, bass.ds(b, 1)], ALU.mult, ALU.add
                                         ).then_inc(bias_done, 1)

            def normalise(b):
                dve.wait_ge(p_exp, b + 1)
                step(dve.reciprocal(rinv[:], rsum[:]))
                dve.tensor_scalar(prob[:], prob[:], rinv[:, 0:1], None, ALU.mult).then_inc(p_norm, 1)

            def copy_out(b):
                dve.wait_ge(o_done, b + 1)
                dve.tensor_copy(att[:, :, bass.ds(NPR + b * DS, DS)],
                                ps_o[:, 0:R].rearrange("p (h q) -> p h q", h=H)).then_inc(o_copied, 1)

            spread_queries(0, 0)
            spread_queries(1, 1)
            copy_keys(0)
            with dve.Fori(0, DB // 2 - 1) as i:
                step.loop(i, 8)
                for u in range(2):
                    b = 2 * i + u
                    maxima(b)
                    spread_queries(b + 2, u)
                    copy_keys(b + 1)
                    normalise(b)
                    copy_out(b)
                step.end_loop(DB // 2 - 1)
            maxima(DB - 2)
            copy_keys(DB - 1)
            normalise(DB - 2)
            copy_out(DB - 2)
            maxima(DB - 1)
            normalise(DB - 1)
            copy_out(DB - 1)


def s5_layer(nc, I, O, S, C, sem):
    qkvu = S["qkvu"]
    free = qkvu[:, 0:3 * H, :].rearrange("p c t -> p (c t)")
    u_all = qkvu[:, 3 * H:4 * H, :]
    at = [0]

    def carve(n):
        at[0] += n
        assert at[0] <= 3 * H * T
        return free[:, at[0] - n:at[0]]

    local = carve(CK * 2 * G).rearrange("p (k x g) -> p k x g", x=2, g=G)
    bb = carve(G * CG).rearrange("p (g c) -> p g c", g=G)
    bb_i = carve(G * CG).rearrange("p (g c) -> p g c", g=G)
    c_x = carve(G * CG).rearrange("p (g c) -> p g c", g=G)
    c_y = carve(G * CG).rearrange("p (g c) -> p g c", g=G)
    o_dram = nc.dram_tensor("o_scratch", [NGB, P, GB * P], F32).ap()
    outer = ExitStack()
    with outer:
        osb = lambda n, s, d=F32: outer.enter_context(nc.sbuf_tensor(n, s, d))
        prev = osb("prev", [P, CK, G])
        y_loc = osb("y_loc", [CK, G, P])
        pw_r = osb("pw_r", [P, G, LC + 1])
        pw_i = osb("pw_i", [P, G, LC + 1])

        ctx = ExitStack()
        sb = lambda n, s, d=F32: ctx.enter_context(nc.sbuf_tensor(n, s, d))
        ps = lambda n, s, d=F32: ctx.enter_context(nc.psum_tensor(n, s, d))
        with ctx:
            rev_r, rev_i = sb("rev_r", [P, G, LC]), sb("rev_i", [P, G, LC])
            a_re, a_im, log_dt = (sb(n, [P, G]) for n in ("a_re", "a_im", "log_dt"))
            dt, mag, ang, turns, sin, cos, c_re, c_im, t1, t2, den = (
                sb(n, [P, G]) for n in ("dt", "mag", "ang", "turns", "sin", "cos", "c_re", "c_im", "t1", "t2", "den"))
            sgn = sb("sgn", [P, 2])
            half_pi = sb("half_pi", [P, 1])
            d_col = sb("d_col", [P, G])
            tmp_p, tmp_q = sb("tmp_p", [P, G, 4]), sb("tmp_q", [P, G, 4])
            u_st = sb("u_st", [P, LC, CK])
            u_tok = sb("u_tok", [CK, GB, LC, CG])
            u_lhs = sb("u_lhs", [P, GB, CK])
            o_pad = sb("o_pad", [P, GB, 2 * LC, CG])
            b_pad = sb("b_pad", [P, GB, 2 * LC - 1, CG])
            o_tmp = sb("o_tmp", [P, GB, LC + 1, CG])
            e_s, e_t = (sb(n, [P, GB, LC, CG]) for n in ("e_s", "e_t"))
            e_tmp = sb("e_tmp", [P, GB, LC, CG])
            e_rows = sb("e_rows", [P, GB, 2, P])
            m_rows = sb("m_rows", [P, GB, P])
            ps_a, ps_b, ps_m, ps_e = (ps(n, [P, 2, 512]) for n in ("ps_a", "ps_b", "ps_m", "ps_e"))

            par_in, b_in, h0_in = sem("par_in"), sem("b_in"), sem("h0_in")
            cleared = sem("s5_cleared")
            dt_done, arg_done, trig_done, coef_done = (sem(n) for n in ("dt_done", "arg_done", "trig_done",
                                                                        "coef_done"))
            u_staged, a_turned, u_tok_done, b_turned, u_lhs_done = (
                sem(n) for n in ("u_staged", "a_turned", "u_tok_done", "b_turned", "u_lhs_done"))
            pads_done, m_done, m_copied, e_done, e_turned, e_copied = (
                sem(n) for n in ("pads_done", "m_done", "m_copied", "e_done", "e_turned", "e_copied"))
            yl_done, yl_copied, hs_done, ht_done, h_copied, o_out = (
                sem(n) for n in ("yl_done", "yl_copied", "hs_done", "ht_done", "h_copied", "o_out"))
            v_step, g_step, held = sem("s5_v_step"), sem("s5_g_step"), sem("s5_held")

            block = ctx.enter_context(nc.Block())

            @block.sync
            def _(sp):
                for dst, n in ((a_re, "a_re"), (a_im, "a_im"), (log_dt, "log_dt"), (sgn, "sgn"), (d_col, "d_col")):
                    sp.dma_start(dst[:], I[n]).then_inc(par_in, 16)
                for dst, n in ((bb, "b_ri"), (bb_i, "b_ir"), (c_x, "c_ri"), (c_y, "c_ir")):
                    sp.dma_start(dst, I[n].rearrange("p (g c) -> p g c", g=G)).then_inc(b_in, 16)
                sp.dma_start(prev[:, NCK:CK, :], I["h0_ri"].rearrange("p (b g) -> p b g", b=DB)).then_inc(h0_in, 16)
                with sp.Fori(0, NGB) as cb:
                    sp.wait_ge(pads_done, 2 * cb + 2)
                    sp.dma_start(o_dram[bass.ds(cb, 1)].rearrange("a p (g x) -> (a p) g x", g=GB),
                                 o_pad[:, :, LC:2 * LC, :].rearrange("p g b c -> p g (b c)")).then_inc(o_out, 16)
                sp.wait_ge(o_out, 16 * NGB)
                sp.wait_ge(h0_in, 16)

            @block.scalar
            def _(act):
                act.wait_ge(par_in, 80)
                act.activation(dt[:], log_dt[:], ACT.Exp).then_inc(dt_done, 1)
                act.wait_ge(arg_done, 1)
                act.activation(mag[:], t1[:], ACT.Exp).then_inc(trig_done, 1)
                act.activation(sin[:], ang[:], ACT.Sin).then_inc(trig_done, 1)
                act.wait_ge(cleared, 4)
                act.activation(cos[:], t2[:], ACT.Sin, scale=-1.0, bias=half_pi[:, 0:1]).then_inc(trig_done, 1)
                with act.Fori(0, NGB) as cb:
                    act.wait_ge(a_turned, cb)
                    act.activation(u_st[:], u_all[:, bass.ds(cb, 1), :].rearrange("p c (k s) -> p s (c k)", s=LC),
                                   ACT.Copy).then_inc(u_staged, 1)
                    act.wait_ge(a_turned, cb + 1)
                    act.wait_ge(b_turned, cb)
                    for r in range(2):
                        act.activation(u_tok[:, :, 4 * r:4 * r + 4, :].rearrange("k g s c -> k s g c"),
                                       ps_a[0:CK, r, :].rearrange("k (s g c) -> k s g c", s=4, g=GB), ACT.Copy
                                       ).then_inc(u_tok_done, 1)
                    act.wait_ge(b_turned, cb + 1)
                    act.wait_ge(ht_done, cb)
                    act.activation(u_lhs[:].rearrange("p (r g) k -> p r (g k)", r=2), ps_b[:, :, 0:4 * CK], ACT.Copy
                                   ).then_inc(u_lhs_done, 1)
                    for r in range(2):
                        act.wait_ge(e_turned, 2 * cb + r + 1)
                        act.activation(e_rows[:, 4 * r:4 * r + 4].rearrange("p g x q -> p x g q"),
                                       ps_e[:].rearrange("p x (g q) -> p x g q", g=4), ACT.Copy).then_inc(e_copied, 1)
                    act.wait_ge(yl_done, cb + 1)
                    act.activation(y_loc[:, bass.ds(GB * cb, GB), :].rearrange("k (r g) q -> k r (g q)", r=2),
                                   ps_a[0:CK, :, :], ACT.Copy).then_inc(yl_copied, 1)

            @block.tensor
            def _(pe):
                ident = C["ident"]
                with pe.Fori(0, NGB) as cb:
                    pe.wait_ge(u_staged, cb + 1)
                    pe.wait_ge(yl_copied, cb)
                    for s in range(LC):
                        mm = pe.transpose(ps_a[0:CK, s // 4, (s % 4) * P:(s % 4 + 1) * P], u_st[:, s, :], ident[:])
                    mm.then_inc(a_turned, 1)
                    pe.wait_ge(u_tok_done, 2 * cb + 2)
                    pe.wait_ge(h_copied, 2 * cb)
                    for g in range(GB):
                        mm = pe.transpose(ps_b[:, g // 4, (g % 4) * CK:(g % 4 + 1) * CK],
                                          u_tok[:, g].rearrange("k s c -> k (s c)"), ident[0:CK, 0:CK])
                    mm.then_inc(b_turned, 1)
                    pe.wait_ge(pads_done, 2 * cb + 2)
                    pe.wait_ge(m_copied, GB * cb)
                    for g in range(GB):
                        for s in range(LC):
                            mm = pe.matmul(ps_m[:, g // 4, (g % 4) * P:(g % 4 + 1) * P],
                                           b_pad[:, g, LC - 1 - s:2 * LC - 1 - s, :].rearrange("p b c -> p (b c)"),
                                           o_pad[:, g, LC - 1 - s:2 * LC - 1 - s, :].rearrange("p b c -> p (b c)"),
                                           start=(s == 0), stop=(s == LC - 1))
                    mm.then_inc(m_done, 1)
                    pe.wait_ge(e_done, cb + 1)
                    for r in range(2):
                        pe.wait_ge(e_copied, 2 * cb + r)
                        for g in range(4):
                            for x, e in enumerate((e_s, e_t)):
                                mm = pe.transpose(ps_e[:, x, g * P:(g + 1) * P],
                                                  e[:, 4 * r + g].rearrange("p s c -> p (s c)"), ident[:])
                        mm.then_inc(e_turned, 1)
                    pe.wait_ge(u_lhs_done, cb + 1)
                    pe.wait_ge(m_copied, GB * cb + GB)
                    for g in range(GB):
                        mm = pe.matmul(ps_a[0:CK, g // 4, (g % 4) * P:(g % 4 + 1) * P], u_lhs[:, g, :],
                                       m_rows[:, g, :], start=True, stop=True)
                    mm.then_inc(yl_done, 1)
                    pe.wait_ge(e_copied, 2 * cb + 2)
                    for x, (bank, done) in enumerate(((ps_b, hs_done), (ps_e, ht_done))):
                        for g in range(GB):
                            mm = pe.matmul(bank[:, g // 4, (g % 4) * CK:(g % 4 + 1) * CK], e_rows[:, g, x, :],
                                           u_lhs[:, g, :], start=True, stop=True)
                        mm.then_inc(done, 1)

            @block.gpsimd
            def _(pool):
                pool.memset(o_pad[:], 0.0).then_inc(cleared, 1)
                pool.memset(b_pad[:], 0.0).then_inc(cleared, 1)
                pool.memset(prev[:, 0, :], 0.0).then_inc(cleared, 1)
                pool.memset(half_pi[:], math.pi / 2).then_inc(cleared, 1)
                chain = Chain(pool, g_step)
                pool.wait_ge(coef_done, 1)

                def step(ins):
                    chain(ins)
                    pool.sem_inc(held, 1)

                with pool.Fori(0, NGB) as cb:
                    chain.loop(cb, 5)
                    g8 = bass.ds(GB * cb, GB)
                    full = [P, GB, LC, CG]
                    br, bi = bc(bb[:, g8, :], 2, full), bc(bb_i[:, g8, :], 2, full)
                    pr, pi = bc(rev_r[:, g8, :], 3, full), bc(rev_i[:, g8, :], 3, full)
                    pool.wait_ge(e_turned, 2 * cb)
                    pool.sem_inc(held, 1)
                    step(pool.tensor_tensor(e_tmp[:], pi, bi, ALU.mult))
                    step(pool.tensor_tensor(e_s[:], pr, br, ALU.mult))
                    step(pool.tensor_tensor(e_s[:], e_s[:], e_tmp[:], ALU.add))
                    step(pool.tensor_tensor(e_tmp[:], pi, br, ALU.mult))
                    step(pool.tensor_tensor(e_t[:], pr, bi, ALU.mult))
                    pool.tensor_tensor(e_t[:], e_t[:], e_tmp[:], ALU.subtract).then_inc(e_done, 1)
                    chain.end_loop(NGB)

            @block.vector
            def _(dve):
                step = Chain(dve, v_step)
                tt = lambda o, a, b, op: step(dve.tensor_tensor(o, a, b, op))
                ts = lambda o, a, s1, s2, op0, op1=None: step(dve.tensor_scalar(o, a, s1, s2, op0, op1) if op1
                                                              else dve.tensor_scalar(o, a, s1, s2, op0))
                dve.wait_ge(par_in, 80)
                ts(a_re[:], a_re[:], -1e-4, None, ALU.min)
                dve.wait_ge(dt_done, 1)
                tt(t1[:], a_re[:], dt[:], ALU.mult)
                tt(ang[:], a_im[:], dt[:], ALU.mult)
                ts(turns[:], ang[:], 1 / (2 * math.pi), None, ALU.mult)
                ts(turns[:], turns[:], 12582912.0, None, ALU.add)
                ts(turns[:], turns[:], 12582912.0, None, ALU.subtract)
                for part in (6.28125, 0.0019350051879882812, 3.0199159819e-07):
                    step(dve.scalar_tensor_tensor(ang[:], turns[:], -part, ang[:], ALU.mult, ALU.add))
                ts(ang[:], ang[:], 3.1415925, -3.1415925, ALU.min, ALU.max)
                dve.scalar_tensor_tensor(t2[:], ang[:], -1.0, ang[:], ALU.mult, ALU.max).then_inc(arg_done, 1)
                dve.wait_ge(trig_done, 3)
                dve.wait_ge(arg_done, 1)
                dve.wait_ge(cleared, 4)
                ts(pw_r[:, :, 0], a_re[:], 0.0, 1.0, ALU.mult, ALU.add)
                ts(pw_i[:, :, 0], a_re[:], 0.0, None, ALU.mult)
                tt(pw_r[:, :, 1], mag[:], cos[:], ALU.mult)
                tt(pw_i[:, :, 1], mag[:], sin[:], ALU.mult)
                for n in (1, 2, 4):
                    shape = [P, G, n]
                    lo_r, lo_i = pw_r[:, :, 1:1 + n], pw_i[:, :, 1:1 + n]
                    top_r, top_i = pw_r[:, :, n:n + 1].broadcast_to(shape), pw_i[:, :, n:n + 1].broadcast_to(shape)
                    tt(tmp_p[:, :, 0:n], lo_r, top_r, ALU.mult)
                    tt(tmp_q[:, :, 0:n], lo_i, top_i, ALU.mult)
                    tt(pw_r[:, :, 1 + n:1 + 2 * n], tmp_p[:, :, 0:n], tmp_q[:, :, 0:n], ALU.subtract)
                    tt(tmp_p[:, :, 0:n], lo_r, top_i, ALU.mult)
                    tt(tmp_q[:, :, 0:n], lo_i, top_r, ALU.mult)
                    tt(pw_i[:, :, 1 + n:1 + 2 * n], tmp_p[:, :, 0:n], tmp_q[:, :, 0:n], ALU.add)
                for s in range(LC):
                    ts(rev_r[:, :, s], pw_r[:, :, LC - 1 - s], 1.0, None, ALU.mult)
                    ts(rev_i[:, :, s], pw_i[:, :, LC - 1 - s], 1.0, None, ALU.mult)
                ts(t1[:], pw_r[:, :, 1], -1.0, None, ALU.add)
                tt(den[:], a_re[:], a_re[:], ALU.mult)
                tt(t2[:], a_im[:], a_im[:], ALU.mult)
                tt(den[:], den[:], t2[:], ALU.add)
                step(dve.reciprocal(den[:], den[:]))
                tt(c_re[:], t1[:], a_re[:], ALU.mult)
                tt(t2[:], pw_i[:, :, 1], a_im[:], ALU.mult)
                tt(c_re[:], c_re[:], t2[:], ALU.add)
                tt(c_re[:], c_re[:], den[:], ALU.mult)
                tt(c_im[:], pw_i[:, :, 1], a_re[:], ALU.mult)
                tt(t2[:], t1[:], a_im[:], ALU.mult)
                tt(c_im[:], c_im[:], t2[:], ALU.subtract)
                tt(c_im[:], c_im[:], den[:], ALU.mult)
                dve.wait_ge(b_in, 64)
                full = [P, G, CG]
                ts(bb_i, bb_i, sgn[:, 0:1], None, ALU.mult)
                ts(c_x, c_x, sgn[:, 1:2], None, ALU.mult)
                w1 = local[:, 0:CG // 2].rearrange("p k x g -> p (k x g)").rearrange("p (g c) -> p g c", g=G)
                w2 = local[:, CG // 2:CG].rearrange("p k x g -> p (k x g)").rearrange("p (g c) -> p g c", g=G)
                tt(w1, bb_i, bc(c_im[:], 2, full), ALU.mult)
                tt(w2, bb, bc(c_im[:], 2, full), ALU.mult)
                tt(bb, bb, bc(c_re[:], 2, full), ALU.mult)
                tt(bb_i, bb_i, bc(c_re[:], 2, full), ALU.mult)
                tt(bb, bb, w1, ALU.add)
                dve.tensor_tensor(bb_i, bb_i, w2, ALU.subtract).then_inc(coef_done, 1)
                dve.wait_ge(coef_done, 1)
                with dve.Fori(0, NGB) as cb:
                    step.loop(cb, 2)
                    g8 = bass.ds(GB * cb, GB)
                    full = [P, GB, LC + 1, CG]
                    cx, cy = bc(c_x[:, g8, :], 2, full), bc(c_y[:, g8, :], 2, full)
                    pr, pi = bc(pw_r[:, g8, :], 3, full), bc(pw_i[:, g8, :], 3, full)
                    dve.wait_ge(m_done, cb)
                    dve.wait_ge(o_out, 16 * cb)
                    step.mark(dve.tensor_tensor(o_tmp[:], cy, pi, ALU.mult))
                    step(dve.tensor_tensor(o_pad[:, :, LC - 1:2 * LC, :], cx, pr, ALU.mult))
                    dve.tensor_tensor(o_pad[:, :, LC - 1:2 * LC, :], o_pad[:, :, LC - 1:2 * LC, :], o_tmp[:],
                                      ALU.subtract).then_inc(pads_done, 1)
                    dve.tensor_copy(b_pad[:, :, LC - 1, :], bb[:, g8, :]).then_inc(pads_done, 1)
                    dve.wait_ge(m_done, cb + 1)
                    dve.wait_ge(yl_done, cb)
                    for g in range(GB):
                        dve.scalar_tensor_tensor(m_rows[:, g, :], C["ident"][:], d_col[:, bass.ds(GB * cb + g, 1)],
                                                 ps_m[:, g // 4, (g % 4) * P:(g % 4 + 1) * P], ALU.mult, ALU.add
                                                 ).then_inc(m_copied, 1)
                    for x, (bank, done) in enumerate(((ps_b, hs_done), (ps_e, ht_done))):
                        dve.wait_ge(done, cb + 1)
                        for r in range(2):
                            ins = dve.tensor_copy(local[:, :, x, bass.ds(GB * cb + 4 * r, 4)].rearrange("p k g -> p g k"),
                                                  bank[:, r, 0:4 * CK].rearrange("p (g k) -> p g k", g=4))
                        ins.then_inc(h_copied, 1)
                    step.end_loop(NGB)

        ctx = ExitStack()
        sb = lambda n, s, d=F32: ctx.enter_context(nc.sbuf_tensor(n, s, d))
        ps = lambda n, s, d=F32: ctx.enter_context(nc.psum_tensor(n, s, d))
        with ctx:
            state = [sb(f"state{j}", [P, 2, G]) for j in range(2)]
            a8_r, a8_i = sb("a8_r", [P, 2, G]), sb("a8_i", [P, 2, G])
            m1, m2 = sb("rec_m1", [P, 2, G]), sb("rec_m2", [P, 2, G])
            h0_t = sb("h0_t", [P, DB, G])
            end_s = sb("end_s", [P, DB, G])
            end_m = sb("end_m", [P, DB, G])
            sgn = sb("sgn2", [P, 2])
            b_glu = sb("b_glu", [P, NGB])
            o_st = [sb(f"o_st{u}", [P, GB, P]) for u in range(2)]
            prev_st = [sb(f"prev_st{u}", [P, GB, CK]) for u in range(2)]
            y = [sb(f"y{u}", [CK, GB, P]) for u in range(2)]
            z_tok = [sb(f"z_tok{u}", [CK, LC, P]) for u in range(2)]
            w_glu = sb("w_glu", [P, NGB, SW])
            gate = [sb(f"glu_gate{u}", [P, T]) for u in range(2)]
            ps_y = ps("ps_y", [P, 2, 512])
            ps_z = ps("ps_z", [P, 2, 512])
            ps_g = [ps(f"ps_g{u}", [P, 2, 512]) for u in range(2)]
            ssm = free[:, CK * 2 * G:CK * 2 * G + NGB * T].rearrange("p (c t) -> p c t", c=NGB)

            consts_in, w_in = sem("s5b_consts"), sem("w_glu_in")
            o_in = [sem(f"o_in{u}") for u in range(2)]
            state_done, prev_done, final_done, ends_out = (sem(n) for n in ("state_done", "prev_done", "final_done",
                                                                           "ends_out"))
            prev_staged, y_done, y_added, z_done, z_turned, z_copied = (
                sem(n) for n in ("prev_staged", "y_done", "y_added", "z_done", "z_turned", "z_copied"))
            glu_sum, glu_gated, glu_done = sem("glu_sum"), sem("glu_gated"), sem("glu_done")
            v_step = sem("s5b_v_step")
            block = ctx.enter_context(nc.Block())

            @block.sync
            def _(sp):
                sp.dma_start(h0_t[:], I["h0_ir"].rearrange("p (b g) -> p b g", b=DB)).then_inc(consts_in, 16)
                sp.dma_start(sgn[:], I["sgn"]).then_inc(consts_in, 16)
                sp.dma_start(b_glu[:], I["b_gluT"]).then_inc(consts_in, 16)
                sp.dma_start(w_glu[:], I["w_glu"].rearrange("(k p) n -> p k n", p=P)).then_inc(w_in, 16)
                for u in range(2):
                    sp.dma_start(o_st[u][:].rearrange("p g x -> p (g x)"), o_dram[u]).then_inc(o_in[u], 16)
                with sp.Fori(1, NGB // 2) as i:
                    for u in range(2):
                        sp.wait_ge(y_done, 2 * i + u - 1)
                        sp.dma_start(o_st[u][:].rearrange("p g x -> p (g x)"),
                                     o_dram[bass.ds(2 * i + u, 1)].rearrange("a p n -> (a p) n")).then_inc(o_in[u], 16)
                sp.wait_ge(final_done, 1)
                sp.wait_ge(state_done, NCK + 1)
                sp.dma_start(O["end_prompt"], state[NCK % 2][:, 0, :]).then_inc(ends_out, 16)
                sp.dma_start(O["end_sample"].rearrange("p (b g) -> p b g", b=DB), end_s[:]).then_inc(ends_out, 16)
                sp.wait_ge(glu_done, NGB)
                sp.dma_start(S["ssm_dram"].rearrange("(c p) t -> p c t", p=P), ssm).then_inc(ends_out, 16)
                sp.wait_ge(ends_out, 48)

            @block.scalar
            def _(act):
                with act.Fori(0, NCK // 2) as i:
                    for u in range(2):
                        act.wait_ge(state_done, 2 * i + u + 1)
                        act.activation(prev[:, bass.ds(2 * i + u, 1), :].rearrange("p k g -> p (k g)"),
                                       state[u][:, 0, :], ACT.Copy).then_inc(prev_done, 1)
                act.wait_ge(prev_done, NCK)
                with act.Fori(0, NGB // 2) as i:
                    for u in range(2):
                        cb = 2 * i + u
                        act.activation(prev_st[u][:].rearrange("p g k -> p k g"), prev[:, :, bass.ds(GB * cb, GB)],
                                       ACT.Copy).then_inc(prev_staged, 1)
                        act.wait_ge(y_added, cb + 1)
                        act.wait_ge(z_turned, cb)
                        act.activation(z_tok[u][:].rearrange("k t (g c) -> k g t c", g=GB),
                                       y[u][:].rearrange("k g (t c) -> k g t c", t=LC), ACT.Gelu_apprx_tanh
                                       ).then_inc(z_done, 1)
                for n in range(NGB):
                    act.wait_ge(glu_sum, n + 1)
                    if n >= 2:
                        act.wait_ge(glu_done, n - 1)
                    act.activation(halves(gate[n % 2][:]), fold(ps_g[n % 2]), ACT.Sigmoid, bias=b_glu[:, n:n + 1]
                                   ).then_inc(glu_gated, 1)

            @block.tensor
            def _(pe):
                with pe.Fori(0, NGB // 2) as i:
                    for u in range(2):
                        cb = 2 * i + u
                        pe.wait_ge(prev_staged, cb + 1)
                        pe.wait_ge(o_in[u], 16 * i + 16)
                        pe.wait_ge(y_added, cb)
                        for g in range(GB):
                            mm = pe.matmul(ps_y[0:CK, g // 4, (g % 4) * P:(g % 4 + 1) * P], prev_st[u][:, g, :],
                                           o_st[u][:, g, :], start=True, stop=True)
                        mm.then_inc(y_done, 1)
                        pe.wait_ge(z_done, cb + 1)
                        pe.wait_ge(z_copied, cb)
                        for t in range(LC):
                            mm = pe.transpose(ps_z[:, t // 4, (t % 4) * CK:(t % 4 + 1) * CK], z_tok[u][:, t, :],
                                              C["ident"][0:CK, 0:CK])
                        mm.then_inc(z_turned, 1)
                pe.wait_ge(z_copied, NGB)
                pe.wait_ge(w_in, 16)
                for n in range(NGB):
                    if n >= 2:
                        pe.wait_ge(glu_gated, n - 1)
                    for k in range(NGB):
                        for a in range(2):
                            mm = pe.matmul(ps_g[n % 2][:, a, 0:HT], w_glu[:, k, n * P:(n + 1) * P],
                                           u_all[:, k, a * HT:(a + 1) * HT], start=(k == 0), stop=(k == NGB - 1))
                    mm.then_inc(glu_sum, 1)

            @block.vector
            def _(dve):
                step = Chain(dve, v_step)
                dve.wait_ge(consts_in, 48)
                for x in range(2):
                    step.mark(dve.tensor_copy(a8_r[:, x, :], pw_r[:, :, LC]))
                step.mark(dve.tensor_copy(a8_i[:, 0, :], pw_i[:, :, LC]))
                step.mark(dve.tensor_scalar(a8_i[:, 1, :], pw_i[:, :, LC], -1.0, None, ALU.mult))
                step(dve.tensor_scalar(h0_t[:], h0_t[:], sgn[:, 0:1], None, ALU.mult))
                full = [P, DB, G]
                step.mark(dve.tensor_tensor(end_m[:], h0_t[:], bc(pw_i[:, :, LC], 1, full), ALU.mult))
                step(dve.tensor_tensor(end_s[:], prev[:, NCK:CK, :], bc(pw_r[:, :, LC], 1, full), ALU.mult))
                step(dve.tensor_tensor(end_s[:], end_s[:], end_m[:], ALU.add))
                dve.tensor_tensor(end_s[:], end_s[:], local[:, NCK:CK, 0, :], ALU.add).then_inc(final_done, 1)
                dve.memset(state[0][:], 0.0).then_inc(state_done, 1)
                with dve.Fori(0, NCK // 2) as i:
                    step.loop(i, 8)
                    for u in range(2):
                        old, new = state[u], state[1 - u]
                        dve.wait_ge(state_done, 2 * i + u + 1)
                        step.mark(dve.tensor_tensor(m1[:], a8_r[:], old[:], ALU.mult))
                        step.mark(dve.tensor_tensor(m2[:, 0, :], a8_i[:, 0, :], old[:, 1, :], ALU.mult))
                        step(dve.tensor_tensor(m2[:, 1, :], a8_i[:, 1, :], old[:, 0, :], ALU.mult))
                        step(dve.tensor_tensor(m1[:], m1[:], m2[:], ALU.add))
                        dve.wait_ge(prev_done, 2 * i + u)
                        dve.tensor_tensor(new[:], m1[:],
                                          local[:, bass.ds(2 * i + u, 1), :, :].rearrange("p k x g -> p (k x) g"),
                                          ALU.add).then_inc(state_done, 1)
                    step.end_loop(NCK // 2)
                dve.wait_ge(state_done, NCK + 1)
                with dve.Fori(0, NGB // 2) as i:
                    for u in range(2):
                        cb = 2 * i + u
                        dve.wait_ge(y_done, cb + 1)
                        dve.tensor_tensor(y[u][:].rearrange("k (r g) q -> k r (g q)", r=2), ps_y[0:CK, :, :],
                                          y_loc[:, bass.ds(GB * cb, GB), :].rearrange("k (r g) q -> k r (g q)", r=2),
                                          ALU.add).then_inc(y_added, 1)
                        dve.wait_ge(z_turned, cb + 1)
                        for r in range(2):
                            ins = dve.tensor_copy(
                                u_all[:, bass.ds(cb, 1), :].rearrange("p c (k t) -> p t (c k)", t=LC)[:, 4 * r:4 * r + 4],
                                ps_z[:, r, 0:4 * CK].rearrange("p (t k) -> p t k", t=4))
                        ins.then_inc(z_copied, 1)
                dve.wait_ge(z_copied, NGB)
                for n in range(NGB):
                    dve.wait_ge(glu_gated, n + 1)
                    dve.tensor_tensor(ssm[:, n, :], u_all[:, n, :], gate[n % 2][:], ALU.mult).then_inc(glu_done, 1)


def merge_and_query(nc, I, O, S, C, sem):
    ctx = ExitStack()
    sb = lambda n, s, d=F32: ctx.enter_context(nc.sbuf_tensor(n, s, d))
    ps = lambda n, s, d=F32: ctx.enter_context(nc.psum_tensor(n, s, d))
    with ctx:
        mod, h2, q_t = S["mod"], S["h2"], S["q_t"]
        mix = h2
        x = sb("x1", [P, KC, T])
        ring = [sb(f"wo_ring{u}", [P, KC, WB]) for u in range(2)]
        sq = [sb(f"sq2_{u}", [P, T]) for u in range(2)]
        std = sb("std2", [P, T])
        rstd = [sb(f"rstd2_{n}", [P, T]) for n in range(2)]
        g_mix, g2 = sb("g_mix", [P, KC]), sb("g2", [P, KC])
        scale2 = sb("scale2", [P, KC, NC_])
        gated = sb("gated", [P, NSM])
        ps_norm = ps("ps_norm2", [P, 2, 512])
        ps_out = [ps(f"ps_out{q}", [P, 2, 512]) for q in range(2)]

        mix_in, x_in, g_in = sem("mix_in"), sem("x1_in"), sem("g_mix_in")
        w_full = [sem(f"wo_full{u}") for u in range(2)]
        sq_done, sq_used, std_done = (sem(n) for n in ("sq2_done", "sq2_used", "std2_done"))
        mix_done, scale_done = sem("mix_done"), sem("scale2_done")
        out_done, out_read = [sem(f"wo_done{q}") for q in range(2)], [sem(f"wo_read{q}") for q in range(2)]
        q_copied = [sem(f"q_copied{q}") for q in range(2)]
        xn_done, h_prompt, h_sample, x_out = (sem(n) for n in ("xn2_done", "h2_prompt", "h2_sample", "x1_out"))
        q_pad = sem("q_pad")
        v_step = sem("merge_v_step")
        NW = D // WB // 2
        block = ctx.enter_context(nc.Block())

        @block.sync
        def _(sp):
            w_out = I["w_out"].rearrange("(k p) (b c) -> b p k c", p=P, c=WB)
            w_q = I["w_q"].rearrange("(k p) (b c) -> b p k c", p=P, c=WB)
            sp.dma_start(mix[:, 0:H, :], S["att_dram"].rearrange("(c p) t -> p c t", p=P)).then_inc(mix_in, 16)
            sp.dma_start(mix[:, H:KC, :], S["ssm_dram"].rearrange("(c p) t -> p c t", p=P)).then_inc(mix_in, 16)
            sp.dma_start(g_mix[:], I["g_mixT"]).then_inc(g_in, 16)
            sp.dma_start(g2[:], I["g2T"]).then_inc(g_in, 16)
            for u in range(2):
                sp.dma_start(ring[u][:], w_out[u]).then_inc(w_full[u], 16)
            sp.dma_start(x[:], I["xT"].rearrange("(k p) t -> p k t", p=P)).then_inc(x_in, 16)
            for b in range(2, 4 * NW):
                sp.wait_ge(out_done[1], 2 * (b - 1))
                w, n = (w_out, b) if b < 2 * NW else (w_q, b - 2 * NW)
                sp.dma_start(ring[b % 2][:], w[n]).then_inc(w_full[b % 2], 16)
            sp.wait_ge(out_read[1], 4 * NW)
            sp.wait_ge(out_read[0], 4 * NW)
            sp.dma_start(S["x1_dram"].rearrange("(k p) t -> p k t", p=P), x[:]).then_inc(x_out, 16)
            sp.wait_ge(x_out, 16)

        @block.scalar
        def _(act):
            for part in range(2):
                act.wait_ge(mix_in, 32)
                for c in range(H):
                    n = part * H + c
                    if n >= 2:
                        act.wait_ge(sq_used, n - 1)
                    act.activation(sq[n % 2][:], mix[:, n, :], ACT.Square).then_inc(sq_done, 1)
                act.wait_ge(sq_used, H * (part + 1))
                if part:
                    act.wait_ge(mix_done, 1)
                act.activation(halves(std[:]), fold(ps_norm), ACT.Sqrt, scale=1.0 / FW, bias=C["eps"][:, 0:1]
                               ).then_inc(std_done, 1)
            for c in range(KC):
                act.wait_ge(out_read[c % 2], c // 2 + 1)
                act.wait_ge(sq_used, KC + max(c - 1, 0))
                act.activation(sq[c % 2][:], x[:, c, :], ACT.Square).then_inc(sq_done, 1)
            act.wait_ge(sq_used, 2 * KC)
            act.wait_ge(mix_done, 2)
            act.activation(halves(std[:]), fold(ps_norm), ACT.Sqrt, scale=1.0 / D, bias=C["eps"][:, 0:1]
                           ).then_inc(std_done, 1)
            act.wait_ge(scale_done, 1)
            for c in range(KC):
                act.wait_ge(xn_done, c + 1)
                act.activation(h2[:, c, 0:NPR], h2[:, c, 0:NPR], ACT.Identity, scale=scale2[:, c, 0:1],
                               bias=mod[:, 3 * KC + c, 0:1]).then_inc(h_prompt, 1)
            with act.Fori(0, 2 * NW) as i:
                for m in range(2):
                    act.wait_ge(out_done[1], 4 * NW + 2 * i + m + 1)
                    act.activation(q_t[:, bass.ds(4 * i + 2 * m + 1, 1), 0:T].rearrange("p c (a t) -> p (c a) t", a=2),
                                   fold(ps_out[1]), ACT.Copy).then_inc(q_copied[1], 1)

        @block.tensor
        def _(pe):
            def add_squares(n0, n):
                for c in range(n):
                    pe.wait_ge(sq_done, n0 + c + 1)
                    for a in range(2):
                        mm = pe.matmul(ps_norm[:, a, 0:HT], C["ones"][:], sq[(n0 + c) % 2][:, a * HT:(a + 1) * HT],
                                       start=(c == 0), stop=(c == n - 1))
                    mm.then_inc(sq_used, 1)

            add_squares(0, H)
            pe.wait_ge(std_done, 1)
            add_squares(H, H)
            pe.wait_ge(mix_done, 2)

            def project(base, copied):
                with pe.Fori(0, NW) as i:
                    for u in range(2):
                        pe.wait_ge(w_full[u], 16 * (base // 4) + 16 * i + 16)
                        for m in range(4):
                            q = m % 2
                            pe.wait_ge(copied[q], 4 * i + 2 * u + m // 2)
                            for k in range(KC):
                                for a in range(2):
                                    mm = pe.matmul(ps_out[q][:, a, 0:HT], ring[u][:, k, m * P:(m + 1) * P],
                                                   h2[:, k, a * HT:(a + 1) * HT], start=(k == 0), stop=(k == KC - 1))
                            mm.then_inc(out_done[q], 1)

            project(0, out_read)
            add_squares(KC, KC)
            pe.wait_ge(h_prompt, KC)
            pe.wait_ge(h_sample, 1)
            project(4 * NW, q_copied)

        @block.gpsimd
        def _(pool):
            pool.memset(q_t[:, :, T:NTT * P], 0.0).then_inc(q_pad, 1)

        @block.vector
        def _(dve):
            step = Chain(dve, v_step)
            dve.wait_ge(g_in, 32)
            step(dve.tensor_scalar(scale2[:], mod[:, 4 * KC:5 * KC, :], 1.0, None, ALU.add))
            dve.tensor_tensor(scale2[:], scale2[:], bc(g2[:], 2, [P, KC, NC_]), ALU.mult).then_inc(scale_done, 1)
            dve.wait_ge(scale_done, 1)
            for part in range(2):
                dve.wait_ge(std_done, part + 1)
                step(dve.reciprocal(rstd[part][:], std[:]))
                for c in range(part * H, part * H + H):
                    ins = dve.scalar_tensor_tensor(mix[:, c, :], mix[:, c, :], g_mix[:, c:c + 1], rstd[part][:],
                                                   ALU.mult, ALU.mult)
                    step.mark(ins) if c % H < H - 1 else ins.then_inc(mix_done, 1)
            dve.wait_ge(x_in, 16)
            with dve.Fori(0, KC // 2) as i:
                step.loop(i, 6)
                for q in range(2):
                    dve.wait_ge(out_done[q], i + 1)
                    c = bass.ds(2 * i + q, 1)
                    gate = mod[:, bass.ds(2 * KC + 2 * i + q, 1), :].rearrange("p c r -> p (c r)")
                    xc = x[:, c, :].rearrange("p c t -> p (c t)")
                    xs = xc[:, NPR:T].rearrange("p (b t) -> p b t", b=DB)
                    step.mark(dve.scalar_tensor_tensor(xc[:, 0:HT], ps_out[q][:, 0, 0:HT], gate[:, 0:1],
                                                       xc[:, 0:HT], ALU.mult, ALU.add))
                    step.mark(dve.scalar_tensor_tensor(xc[:, HT:NPR], ps_out[q][:, 1, 0:NPR - HT], gate[:, 0:1],
                                                       xc[:, HT:NPR], ALU.mult, ALU.add))
                    step(dve.tensor_tensor(gated[:].rearrange("p (b t) -> p b t", b=DB),
                                           ps_out[q][:, 1, NPR - HT:HT].rearrange("p (b t) -> p b t", b=DB),
                                           bc(gate[:, 1:NC_], 2, [P, DB, DS]), ALU.mult))
                    dve.tensor_tensor(xs, xs, gated[:].rearrange("p (b t) -> p b t", b=DB), ALU.add
                                      ).then_inc(out_read[q], 1)
                    dve.wait_ge(out_read[q], i + 1)
                step.end_loop(KC // 2)
            dve.wait_ge(std_done, 3)
            step(dve.reciprocal(rstd[0][:], std[:]))
            for c in range(KC):
                dve.tensor_tensor(h2[:, c, :], x[:, c, :], rstd[0][:], ALU.mult).then_inc(xn_done, 1)
            dve.wait_ge(xn_done, KC)
            hs = h2[:, :, NPR:T].rearrange("p c (b t) -> p c b t", b=DB)
            step(dve.tensor_tensor(hs, hs, bc(scale2[:, :, 1:NC_], 3, [P, KC, DB, DS]), ALU.mult))
            dve.tensor_tensor(hs, hs, bc(mod[:, 3 * KC:4 * KC, 1:NC_], 3, [P, KC, DB, DS]), ALU.add
                              ).then_inc(h_sample, 1)
            with dve.Fori(0, 2 * NW) as i:
                for m in range(2):
                    dve.wait_ge(out_done[0], 4 * NW + 2 * i + m + 1)
                    dve.tensor_copy(q_t[:, bass.ds(4 * i + 2 * m, 1), 0:T].rearrange("p c (a t) -> p (c a) t", a=2),
                                    fold(ps_out[0])).then_inc(q_copied[0], 1)


def select_experts(nc, I, O, S, C, sem):
    ctx = ExitStack()
    sb = lambda n, s, d=F32: ctx.enter_context(nc.sbuf_tensor(n, s, d))
    ps = lambda n, s, d=F32: ctx.enter_context(nc.psum_tensor(n, s, d))
    HX = 2 * PH
    with ctx:
        q_t, out_t = S["q_t"], S["sel_t"]
        keys = sb("keys_sel", [P, HX, NK])
        q_st = sb("q_tile", [P, HX, P])
        s = sb("s_sel", [P, HX, NK])
        val = sb("val_sel", [P, HX, TK])
        idx = sb("idx_sel", [P, HX, TK], U32)
        idx_f = sb("idx_f_sel", [P, HX, TK])
        cand = sb("cand_sel", [P, PH, TK * TK])
        top = sb("top_sel", [P, PH, TK])
        pos = sb("pos_sel", [P, PH, TK], U32)
        half = [sb(f"half{x}", [P, PH, TK], U32) for x in range(2)]
        half_f = [sb(f"half_f{x}", [P, PH, TK]) for x in range(2)]
        number = sb("number_sel", [P, TK])
        hit = [sb(f"hit{x}", [P, PH, TK, TK]) for x in range(2)]
        res = [sb(f"res{n}", [P, PH, TK]) for n in range(3)]
        diff, e = sb("diff_sel", [P, PH, TK]), sb("e_sel", [P, PH, TK])
        tot = sb("tot_sel", [P, PH])
        ps_s = [ps(f"ps_sc{j}", [P, 512]) for j in range(4)]
        ps_t = ps("ps_sel_t", [P, 512])
        keys_in, q_staged, s_done, s_copied = (sem(n) for n in ("keys_in", "q_tile_staged", "sc_done", "sc_copied"))
        top_done, e_done, res_part, t_done, t_copied = (sem(n) for n in ("top_done", "e_sel_done", "res_part", "sel_turned",
                                                                         "sel_copied"))
        hits_found, hits_done, hits_used = sem("hits_found"), sem("hits_done"), sem("hits_used")
        v_step = sem("sel_v_step")
        held = sem("sel_held")
        block = ctx.enter_context(nc.Block())

        @block.sync
        def _(sp):
            sp.dma_start(keys[:], I["subkeysT"].rearrange("p (x n) -> p x n", x=HX)).then_inc(keys_in, 16)
            sp.dma_start(number[:], I["number"]).then_inc(keys_in, 16)

        @block.scalar
        def _(act):
            with act.Fori(0, NTT) as i:
                act.wait_ge(s_done, 4 * i)
                act.activation(q_st[:], q_t[:, :, bass.ds(P * i, P)], ACT.Copy).then_inc(q_staged, 1)
                for j in range(4):
                    act.wait_ge(s_done, 4 * i + j + 1)
                    act.wait_ge(top_done, i)
                    act.activation(s[:, 4 * j:4 * j + 4, :], ps_s[j][:].rearrange("p (x n) -> p x n", x=4), ACT.Copy
                                   ).then_inc(s_copied, 1)
                act.wait_ge(top_done, i + 1)
                act.activation(e[:], diff[:], ACT.Exp).then_inc(e_done, 1)
                act.wait_ge(t_done, i + 1)
                act.activation(out_t[:, :, bass.ds(P * i, P)], ps_t[:, 0:3 * P].rearrange("p (n t) -> p n t", n=3),
                               ACT.Copy).then_inc(t_copied, 1)

        @block.tensor
        def _(pe):
            pe.wait_ge(keys_in, 32)

            def scores(i):
                pe.wait_ge(q_staged, i + 1)
                for j in range(4):
                    pe.wait_ge(s_copied, 4 * i)
                    for x in range(4 * j, 4 * j + 4):
                        mm = pe.matmul(ps_s[j][:, (x % 4) * P:(x % 4 + 1) * P], q_st[:, x, :], keys[:, x, :],
                                       start=True, stop=True)
                    mm.then_inc(s_done, 1)

            with pe.Fori(0, NTT) as i:
                scores(i)
                pe.wait_ge(res_part, 2 * i + 2)
                pe.wait_ge(hits_used, i + 1)
                pe.wait_ge(t_copied, i)
                for n in range(3):
                    mm = pe.transpose(ps_t[:, n * P:(n + 1) * P], res[n][:].rearrange("p h k -> p (h k)"), C["ident"][:])
                mm.then_inc(t_done, 1)

        @block.gpsimd
        def _(pool):
            with pool.Fori(0, NTT) as i:
                full = [P, PH, TK, TK]
                pool.wait_ge(hits_found, i + 1)
                pool.tensor_tensor(hit[1][:], hit[1][:], bc(idx_f[:, 1:HX:2, :], 2, full), ALU.mult
                                   ).then_inc(hits_done, 1)

        @block.vector
        def _(dve):
            step = Chain(dve, v_step)
            dve.wait_ge(keys_in, 32)

            def settle():
                step.settle()
                dve.sem_inc(held, 1)

            def two_rounds(get, n, values, places):
                for x in range(n):
                    step.mark(dve.max(values[:, x, 0:8], get(x)))
                settle()
                for x in range(n):
                    step.mark(dve.max_index(places[:, x, 0:8], values[:, x, 0:8], get(x)))
                settle()
                for x in range(n):
                    step.mark(dve.match_replace(get(x), values[:, x, 0:8], get(x), 3 * NEG))
                settle()
                for x in range(n):
                    step.mark(dve.max(values[:, x, 8:16], get(x)))
                settle()
                for x in range(n):
                    step.mark(dve.max_index(places[:, x, 8:16], values[:, x, 8:16], get(x)))
                settle()

            with dve.Fori(0, NTT) as i:
                step.loop(i, 5 * HX + 2 + 5 * PH + 4 + 2 + 2)
                dve.wait_ge(s_copied, 4 * i + 4)
                dve.sem_inc(held, 1)
                two_rounds(lambda x: s[:, x, :], HX, val, idx)
                dve.wait_ge(hits_done, i)
                step.mark(dve.tensor_copy(idx_f[:], idx[:]))
                full = [P, PH, TK, TK]
                step.mark(dve.tensor_tensor(cand[:].rearrange("p h (a b) -> p h a b", a=TK),
                                            bc(val[:, 0:HX:2, :], 3, full), bc(val[:, 1:HX:2, :], 2, full), ALU.add))
                settle()
                two_rounds(lambda x: cand[:, x, :], PH, top, pos)
                step.mark(dve.tensor_scalar(half[0][:], pos[:], 4, None, ALU.logical_shift_right))
                step(dve.tensor_scalar(half[1][:], pos[:], TK - 1, None, ALU.bitwise_and))
                step.mark(dve.tensor_copy(half_f[0][:], half[0][:]))
                step(dve.tensor_copy(half_f[1][:], half[1][:]))
                dve.tensor_tensor(diff[:], top[:], top[:, :, 0:1].broadcast_to([P, PH, TK]), ALU.subtract
                                  ).then_inc(top_done, 1)
                dve.tensor_tensor(hit[1][:], bc(half_f[1][:], 3, full),
                                  number[:].unsqueeze(1).unsqueeze(1).broadcast_to(full), ALU.is_equal
                                  ).then_inc(hits_found, 1)
                step(dve.tensor_tensor(hit[0][:], bc(half_f[0][:], 3, full),
                                       number[:].unsqueeze(1).unsqueeze(1).broadcast_to(full), ALU.is_equal))
                step(dve.tensor_tensor(hit[0][:], hit[0][:], bc(idx_f[:, 0:HX:2, :], 2, full), ALU.mult))
                dve.wait_ge(t_done, i)
                dve.tensor_reduce(res[0][:], hit[0][:], AX, ALU.add).then_inc(res_part, 1)
                dve.wait_ge(e_done, i + 1)
                step(dve.tensor_reduce(tot[:], e[:], AX, ALU.add))
                step(dve.reciprocal(tot[:], tot[:]))
                dve.tensor_tensor(res[2][:], e[:], bc(tot[:], 2, [P, PH, TK]), ALU.mult).then_inc(res_part, 1)
                dve.wait_ge(hits_done, i + 1)
                dve.tensor_reduce(res[1][:], hit[1][:], AX, ALU.add).then_inc(hits_used, 1)
                step.end_loop(NTT)


def spread_gates(nc, I, O, S, C, sem):
    ctx = ExitStack()
    sb = lambda n, s, d=F32: ctx.enter_context(nc.sbuf_tensor(n, s, d))
    ps = lambda n, s, d=F32: ctx.enter_context(nc.psum_tensor(n, s, d))
    NB, Q = 4, 4
    with ctx:
        sel = S["sel_t"]
        count = sb("count", [P, P])
        rows = [sb(f"hot_rows{b}", [P, Q, P]) for b in range(NB)]
        colm = [sb(f"hot_cols{b}", [P, Q, P]) for b in range(NB)]
        out = [sb(f"gate_blk{x}", [P, NK, TB]) for x in range(2)]
        ps_g = [ps(f"ps_gate{b}", [P, 512]) for b in range(NB)]
        count_in = sem("count_in")
        rows_done, cols_done = [sem(f"rows_done{b}") for b in range(NB)], [sem(f"cols_done{b}") for b in range(NB)]
        g_sum, g_copied = [sem(f"g_sum{b}") for b in range(NB)], sem("g_copied")
        g_out = [sem(f"g_out{x}") for x in range(2)]
        block = ctx.enter_context(nc.Block())
        turns = TB // (NB * Q)

        @block.sync
        def _(sp):
            sp.dma_start(count[:], I["count"]).then_inc(count_in, 16)
            for k in range(NTB):
                sp.wait_ge(g_copied, NB * turns * (k + 1))
                sp.dma_start(S["gates_dram"][k], out[k % 2][:].rearrange("p j t -> p (j t)")).then_inc(g_out[k % 2], 16)
            for x in range(2):
                sp.wait_ge(g_out[x], 16 * ((NTB + 1 - x) // 2))

        @block.vector
        def _(dve):
            dve.wait_ge(count_in, 16)
            with dve.Fori(0, NTB * turns) as i:
                for b in range(NB):
                    dve.wait_ge(g_sum[b], i)
                    t = bass.ds((i * NB + b) * Q, Q)
                    dve.tensor_tensor(rows[b][:], bc(sel[:, 0, t], 2, [P, Q, P]), bc(count[:], 1, [P, Q, P]),
                                      ALU.is_equal).then_inc(rows_done[b], 1)
                    for j in range(Q):
                        t = bass.ds((i * NB + b) * Q + j, 1)
                        dve.tensor_scalar(colm[b][:, j, :], count[:], sel[:, 1, t], sel[:, 2, t], ALU.is_equal,
                                          ALU.mult).then_inc(cols_done[b], 1)

        @block.tensor
        def _(pe):
            with pe.Fori(0, NTB * turns) as i:
                for b in range(NB):
                    pe.wait_ge(rows_done[b], i + 1)
                    pe.wait_ge(cols_done[b], Q * i + Q)
                    if b == 0:
                        pe.wait_ge(g_copied, NB * i)
                    for j in range(Q):
                        mm = pe.matmul(ps_g[b][:, j * P:(j + 1) * P], rows[b][:, j, :], colm[b][:, j, :],
                                       start=True, stop=True)
                    mm.then_inc(g_sum[b], 1)

        @block.scalar
        def _(act):
            for k in range(NTB):
                if k >= 2:
                    act.wait_ge(g_out[k % 2], 16 * (k // 2))
                with act.Fori(0, turns) as i:
                    for b in range(NB):
                        act.wait_ge(g_sum[b], i + (turns * k + 1))
                        act.activation(out[k % 2][:, :, bass.ds((i * NB + b) * Q, Q)].rearrange("p j t -> p t j"),
                                       ps_g[b][:].rearrange("p (t j) -> p t j", t=Q), ACT.Copy).then_inc(g_copied, 1)


def experts(nc, I, O, S, C, sem):
    ctx = ExitStack()
    sb = lambda n, s, d=F32: ctx.enter_context(nc.sbuf_tensor(n, s, d))
    ps = lambda n, s, d=F32: ctx.enter_context(nc.psum_tensor(n, s, d))
    HC = KC // 2
    HW = D // 2
    with ctx:
        acc = S["acc"]
        h_hi, h_lo = sb("h_hi", [P, KC, T], F32R), sb("h_lo", [P, KC, T], F32R)
        w_hi = [sb(f"w_hi{n}", [P, T], F32R) for n in range(4)]
        w_lo = [sb(f"w_lo{n}", [P, T], F32R) for n in range(4)]
        gates = [sb(f"gates{n}", [P, NTB, 2, TB]) for n in range(2)]
        wt = [sb(f"wt{n}", [P, T]) for n in range(2)]
        raw_u = [sb(f"raw_u{n}", [P, HW]) for n in range(2)]
        raw_v = [sb(f"raw_v{n}", [P, HW]) for n in range(2)]
        u_hi = [sb(f"u_hi{n}", [P, HW], F32R) for n in range(2)]
        u_lo = [sb(f"u_lo{n}", [P, HW], F32R) for n in range(2)]
        v_hi = [[sb(f"v_hi{b}{x}", [P, HW], F32R) for x in range(2)] for b in range(2)]
        v_lo = [[sb(f"v_lo{b}{x}", [P, HW], F32R) for x in range(2)] for b in range(2)]
        ps_u = [ps(f"ps_u{n}", [P, 2, 512]) for n in range(2)]
        ps_v = [ps(f"ps_v{n}", [P, 2, 512]) for n in range(2)]

        u_in, v_in, gates_in = ([sem(f"{n}{x}") for x in range(2)] for n in ("raw_u_in", "raw_v_in", "gates_in"))
        u_hi_done, u_lo_done, u_used = ([sem(f"{n}{x}") for x in range(2)] for n in ("u_hi_done", "u_lo_done", "u_used"))
        v_hi_done, v_lo_done = ([sem(f"{n}{x}") for x in range(2)] for n in ("v_hi_done", "v_lo_done"))
        v_chunk, acc_done = ([sem(f"{n}{x}") for x in range(2)] for n in ("v_chunk", "acc_done"))
        h_hi_done, h_lo_done, acc_clear = sem("h_hi_done"), sem("h_lo_done"), sem("acc_clear")
        a_done, gm_done, w_hi_done, w_lo_done = (sem(n) for n in ("a_done", "gm_done", "w_hi_done", "w_lo_done"))
        block = ctx.enter_context(nc.Block())
        NS = NK

        def run(eng, step):
            step(0, 0), step(1, 1)
            with eng.Fori(0, (NS - 4) // 4) as i:
                for u in range(4):
                    step(4 * i + (2 + u), 2 + u)
            for s in range(NS - 2, NS + 2):
                step(s, s)

        first = lambda s: isinstance(s, int) and s < 2
        last = lambda s, n: isinstance(s, int) and s + n > NS - 1

        @block.sync
        def _(sp):
            def load_u(s, h):
                src = I["uT"][bass.ds(s, 1)].rearrange("a p n -> (a p) n")
                sp.dma_start(raw_u[h][:], src[:, h * HW:(h + 1) * HW]).then_inc(u_in[h], 16)

            def load_gates(g, par):
                sp.dma_start(gates[par][:].rearrange("p b j t -> p b (j t)"),
                             S["gates_dram"].rearrange("b p (g n) -> g p b n", g=NK // 2)[bass.ds(g, 1)]
                             .rearrange("a p b n -> (a p) b n")).then_inc(gates_in[par], 16)

            v_rows = I["peer_v"].rearrange("(i j) d -> j i d", j=NK)

            def step(s, m):
                v = s - 1
                if not (isinstance(s, int) and not 0 <= v < NS):
                    for x in range(2):
                        sp.wait_ge(v_lo_done[x], v)
                        e = bass.ds(v - (m - 1) % 2 + x, 1)
                        sp.dma_start(raw_v[x][:], v_rows[e].rearrange("a p n -> (a p) n")[
                            :, ((m - 1) % 2) * HW:((m - 1) % 2 + 1) * HW]).then_inc(v_in[x], 16)
                if m % 2 == 0 and not last(s, 3):
                    sp.wait_ge(gm_done, s)
                    load_gates(s // 2 + 1 if isinstance(s, int) else half_of(s) + 1, (m // 2 + 1) % 2)
                if not last(s, 2):
                    for h in range(2):
                        sp.wait_ge(u_lo_done[h], s + 2)
                        load_u(s + 2, h)

            load_u(0, 0)
            load_u(0, 1)
            load_gates(0, 0)
            for h in range(2):
                sp.wait_ge(u_lo_done[h], 1)
                load_u(1, h)
            step(0, 0), step(1, 1)
            with sp.Fori(0, (NS - 4) // 4) as i:
                for u in range(4):
                    half_of = lambda s, u=u: 2 * i + (2 + u) // 2
                    step(4 * i + (2 + u), 2 + u)
            for s in range(NS - 2, NS + 2):
                step(s, s)

        @block.scalar
        def _(act):
            def split_u(s, h):
                act.wait_ge(u_in[h], 16 * s + 16)
                act.wait_ge(u_used[h], s)
                act.activation(u_hi[h][:], raw_u[h][:], ACT.Copy).then_inc(u_hi_done[h], 1)

            def step(s, m):
                v = s - 2
                if not first(s):
                    if last(s, -1):
                        act.wait_ge(v_chunk[1], (HC // 2) * (v - 1))
                    else:
                        act.wait_ge(u_used[1], s)
                    for x in range(2):
                        act.wait_ge(v_in[x], 16 * v + 16)
                        act.activation(v_hi[m % 2][x][:], raw_v[x][:], ACT.Copy).then_inc(v_hi_done[x], 1)
                if not last(s, 1):
                    split_u(s + 1, 0)
                if not last(s, 0):
                    act.wait_ge(u_used[1], s + 1)
                    if not first(s):
                        act.wait_ge(w_lo_done, s - 1)
                    act.activation(halves(wt[m % 2][:]), fold(ps_u[m % 2]), ACT.Gelu_apprx_tanh).then_inc(a_done, 1)
                if not last(s, 1):
                    split_u(s + 1, 1)
                if not last(s, 0):
                    act.wait_ge(gm_done, s + 1)
                    if not first(s):
                        act.wait_ge(v_chunk[1], (HC // 2) * (s - 2 - m % 2))
                    act.activation(w_hi[m % 4][:], wt[m % 2][:], ACT.Copy).then_inc(w_hi_done, 1)

            for c in range(KC):
                act.activation(h_hi[:, c, :], acc[:, c, :], ACT.Copy).then_inc(h_hi_done, 1)
            split_u(0, 0)
            split_u(0, 1)
            run(act, step)

        @block.vector
        def _(dve):
            def split_u(s, h):
                dve.wait_ge(u_hi_done[h], s + 1)
                dve.tensor_tensor(u_lo[h][:], raw_u[h][:], u_hi[h][:].bitcast(F32), ALU.subtract
                                  ).then_inc(u_lo_done[h], 1)

            def add(v, c, b):
                q = c % 2
                dve.wait_ge(v_chunk[q], (HC // 2) * v + c // 2 + 1)
                dve.wait_ge(acc_done[q], (HC // 2) * v + c // 2)
                dst = halves(acc[:, b * HC + c, :])
                dve.tensor_tensor(dst, fold(ps_v[q]), dst, ALU.add).then_inc(acc_done[q], 1)

            def step(s, m):
                v = s - 2
                if not first(s):
                    for x in range(2):
                        dve.wait_ge(v_hi_done[x], v + 1)
                        dve.tensor_tensor(v_lo[m % 2][x][:], raw_v[x][:], v_hi[m % 2][x][:].bitcast(F32),
                                          ALU.subtract).then_inc(v_lo_done[x], 1)
                if not last(s, 1):
                    split_u(s + 1, 0)
                if not first(s):
                    add(v, 0, m % 2)
                if not last(s, 1):
                    split_u(s + 1, 1)
                if not first(s):
                    add(v, 1, m % 2)
                if not last(s, 0):
                    dve.wait_ge(a_done, s + 1)
                    par = (m // 2) % 2
                    dve.wait_ge(gates_in[par], 16 * turns_of(s, m) + 16)
                    w = wt[m % 2][:].rearrange("p (b t) -> p b t", t=TB)
                    dve.tensor_tensor(w, w, gates[par][:, :, m % 2, :], ALU.mult).then_inc(gm_done, 1)
                if not first(s):
                    add(v, 2, m % 2)
                if not last(s, 0):
                    dve.wait_ge(w_hi_done, s + 1)
                    dve.tensor_tensor(w_lo[m % 4][:], wt[m % 2][:], w_hi[m % 4][:].bitcast(F32), ALU.subtract
                                      ).then_inc(w_lo_done, 1)
                if not first(s):
                    for c in range(3, HC):
                        add(v, c, m % 2)

            for c in range(KC):
                dve.wait_ge(h_hi_done, c + 1)
                dve.tensor_tensor(h_lo[:, c, :], acc[:, c, :], h_hi[:, c, :].bitcast(F32), ALU.subtract
                                  ).then_inc(h_lo_done, 1)
            split_u(0, 0)
            split_u(0, 1)
            dve.wait_ge(h_lo_done, KC)
            dve.memset(acc[:], 0.0).then_inc(acc_clear, 1)
            dve.wait_ge(acc_clear, 1)
            turns_of = lambda s, m: s // 4
            step(0, 0), step(1, 1)
            with dve.Fori(0, (NS - 4) // 4) as i:
                turns_of = lambda s, m: i + m // 4
                for u in range(4):
                    step(4 * i + (2 + u), 2 + u)
            turns_of = lambda s, m: s // 4
            for s in range(NS - 2, NS + 2):
                step(s, s)

        @block.tensor
        def _(pe):
            def product(out, pairs, start, stop):
                n = 0
                for (hi, lo), (m_hi, m_lo) in pairs:
                    for w, mv in ((hi, m_hi), (hi, m_lo), (lo, m_hi)):
                        n += 1
                        for a in range(2):
                            mm = pe.matmul(out[:, a, 0:HT], w, mv[:, a * HT:(a + 1) * HT],
                                           start=(start and n == 1), stop=(stop and n == 3 * len(pairs)))
                return mm

            def step(s, m):
                v = s - 2
                if not last(s, 0):
                    if not first(s):
                        pe.wait_ge(a_done, s - 1)
                    for h in range(2):
                        pe.wait_ge(u_lo_done[h], s + 1)
                        for k in range(HC):
                            c = h * HC + k
                            cols = slice(k * P, (k + 1) * P)
                            mm = product(ps_u[m % 2], [((u_hi[h][:, cols], u_lo[h][:, cols]), (h_hi[:, c, :], h_lo[:, c, :]))],
                                         c == 0, c == KC - 1)
                        mm.then_inc(u_used[h], 1)
                if not first(s):
                    b = m % 2
                    for x in range(2):
                        pe.wait_ge(v_lo_done[x], v + 1)
                    pe.wait_ge(w_lo_done, s - m % 2)
                    for c in range(HC):
                        q = c % 2
                        pe.wait_ge(acc_done[q], (HC // 2) * v + c // 2)
                        cols = slice(c * P, (c + 1) * P)
                        pair = [((v_hi[b][x][:, cols], v_lo[b][x][:, cols]),
                                 (w_hi[(m - 2 - b + x) % 4][:], w_lo[(m - 2 - b + x) % 4][:])) for x in range(2)]
                        product(ps_v[q], pair, True, True).then_inc(v_chunk[q], 1)

            pe.wait_ge(h_lo_done, KC)
            run(pe, step)


def finish(nc, I, O, S, C, sem):
    ctx = ExitStack()
    sb = lambda n, s, d=F32: ctx.enter_context(nc.sbuf_tensor(n, s, d))
    ps = lambda n, s, d=F32: ctx.enter_context(nc.psum_tensor(n, s, d))
    with ctx:
        acc, mod = S["acc"], S["mod"]
        x = sb("x2", [P, KC, T])
        sq = [sb(f"sq3_{u}", [P, T]) for u in range(2)]
        std, rstd, g_f = sb("std3", [P, T]), sb("rstd3", [P, T]), sb("g_f", [P, KC])
        ps_norm = ps("ps_norm3", [P, 2, 512])
        x_in, g_in, added = sem("x2_in"), sem("g_f_in"), sem("x2_added")
        scaled, sq_done, sq_used, std_done, y_done, y_out = (sem(n) for n in ("acc_scaled", "sq3_done", "sq3_used",
                                                                             "std3_done", "y_done_f", "y_out"))
        v_step = sem("fin_v_step")
        block = ctx.enter_context(nc.Block())

        @block.sync
        def _(sp):
            x_v = S["x1_dram"].rearrange("(k p) t -> p k t", p=P)
            y_v = O["yT"].rearrange("(k p) t -> p k t", p=P)
            sp.dma_start(g_f[:], I["gfT"]).then_inc(g_in, 16)
            for n in range(4):
                sp.dma_start(x[:, 4 * n:4 * n + 4, :], x_v[:, 4 * n:4 * n + 4, :]).then_inc(x_in, 16)
            for n in range(4):
                sp.wait_ge(y_done, 4 * n + 4)
                sp.dma_start(y_v[:, 4 * n:4 * n + 4, :], x[:, 4 * n:4 * n + 4, :]).then_inc(y_out, 16)
            sp.wait_ge(y_out, 64)

        @block.scalar
        def _(act):
            for c in range(KC):
                act.wait_ge(added, c + 1)
                if c >= 2:
                    act.wait_ge(sq_used, c - 1)
                act.activation(sq[c % 2][:], x[:, c, :], ACT.Square).then_inc(sq_done, 1)
            act.wait_ge(sq_used, KC)
            act.activation(halves(std[:]), fold(ps_norm), ACT.Sqrt, scale=1.0 / D, bias=C["eps"][:, 0:1]
                           ).then_inc(std_done, 1)

        @block.tensor
        def _(pe):
            for c in range(KC):
                pe.wait_ge(sq_done, c + 1)
                for a in range(2):
                    mm = pe.matmul(ps_norm[:, a, 0:HT], C["ones"][:], sq[c % 2][:, a * HT:(a + 1) * HT],
                                   start=(c == 0), stop=(c == KC - 1))
                mm.then_inc(sq_used, 1)

        @block.vector
        def _(dve):
            step = Chain(dve, v_step)
            dve.wait_ge(x_in, 64)
            gate = mod[:, 5 * KC:6 * KC, :]
            acc_s = acc[:, :, NPR:T].rearrange("p c (b t) -> p c b t", b=DB)
            step(dve.tensor_tensor(acc_s, acc_s, bc(gate[:, :, 1:NC_], 3, [P, KC, DB, DS]), ALU.mult))
            step(dve.tensor_tensor(x[:, :, NPR:T], x[:, :, NPR:T], acc[:, :, NPR:T], ALU.add))
            for c in range(KC):
                dve.scalar_tensor_tensor(x[:, c, 0:NPR], acc[:, c, 0:NPR], gate[:, c, 0:1], x[:, c, 0:NPR],
                                         ALU.mult, ALU.add).then_inc(added, 1)
            dve.wait_ge(std_done, 1)
            dve.wait_ge(g_in, 16)
            dve.wait_ge(added, KC)
            step(dve.reciprocal(rstd[:], std[:]))
            for c in range(KC):
                dve.scalar_tensor_tensor(x[:, c, :], x[:, c, :], g_f[:, c:c + 1], rstd[:], ALU.mult, ALU.mult
                                         ).then_inc(y_done, 1)


def spill_attention(nc, I, O, S, C, sem):
    done = sem("att_out")
    with nc.Block() as block:
        @block.sync
        def _(sp):
            sp.dma_start(S["att_dram"].rearrange("(c p) t -> p c t", p=P), S["att"][:]).then_inc(done, 16)
            sp.wait_ge(done, 16)


def set_constants(nc, I, O, S, C, sem):
    ready = sem(f"{C["ident"].name}_ready")
    with nc.Block() as block:
        @block.gpsimd
        def _(pool):
            pool.memset(C["eps"][:], EPS).then_inc(ready, 1)
            pool.memset(C["ones"][:], 1.0).then_inc(ready, 1)
            pool.memset(C["ident"][:], 0.0).then_inc(ready, 1)
            pool.wait_ge(ready, 3)
            pool.affine_select(out=C["ident"][:], in_=C["ident"][:], compare_op=ALU.not_equal, fill=1.0,
                               base=0, pattern=[[-1, P]], channel_multiplier=1).then_inc(ready, 1)
            pool.wait_ge(ready, 4)


def stage(nc, program, *args):
    used = []

    def sem(name):
        used.append(nc.alloc_semaphore(name=name))
        return used[-1]

    program(nc, *args, sem)
    nc.clear_and_free_semaphores(used)
    nc.all_engine_barrier()


def build(nc, I, O):
    tile = lambda n, s: nc.sbuf_tensor(n, s, F32)
    scratch = lambda n, s: nc.dram_tensor(n, s, F32).ap()
    S = {"att_dram": scratch("att_scratch", [FW, T]), "ssm_dram": scratch("ssm_scratch", [SW, T]),
         "x1_dram": scratch("x1_scratch", [D, T]), "gates_dram": scratch("gates_scratch", [NTB, P, NK * TB])}
    C = {}
    args = (I, O, S, C)
    with tile("eps", [P, 1]) as C["eps"], tile("ones", [P, P]) as C["ones"], tile("mod", [P, NMOD, NC_]) as S["mod"]:
        with tile("ident_a", [P, P]) as C["ident"], tile("qkvu", [P, 4 * H, T]) as S["qkvu"], \
                tile("logf", [H, T]) as S["logf"]:
            stage(nc, set_constants, *args)
            stage(nc, project_inputs, *args)
            with tile("att", [P, H, T]) as S["att"]:
                stage(nc, attend_prompt, *args)
                stage(nc, attend_sample, *args)
                stage(nc, spill_attention, *args)
            stage(nc, s5_layer, *args)
        with tile("h2_acc", [P, KC, T]) as S["h2"]:
            S["acc"] = S["h2"]
            with tile("ident_b", [P, P]) as C["ident"], tile("sel_t", [P, 3, NTT * P]) as S["sel_t"]:
                stage(nc, set_constants, *args)
                with tile("q_t", [P, KC, NTT * P]) as S["q_t"]:
                    stage(nc, merge_and_query, *args)
                    stage(nc, select_experts, *args)
                stage(nc, spread_gates, *args)
            stage(nc, experts, *args)
            stage(nc, finish, *args)


def layout(inputs):
    import numpy as np
    f = {n: np.asarray(a) for n, a in inputs.items()}
    cols = lambda v, n: np.ascontiguousarray(v.reshape(n, P).T)
    a = {}
    a["xT"] = np.concatenate([f["x_prompt"].reshape(NPR, D), f["x_sample"].reshape(NSM, D)]).T
    a["cT"] = np.concatenate([f["c_prompt"], f["c_sample"]]).T
    a["w_ada"] = f["w_ada"][0]
    a["b_adaT"] = cols(f["b_ada"][0], NMOD)
    a["g1T"] = cols(f["g_norm1"][0], KC)
    w_in = f["w_in"][0]
    a["w_in"] = np.concatenate([w_in[:, :3 * FW], w_in[:, 3 * FW + H:]], axis=1)
    a["w_fg"] = w_in[:, 3 * FW:3 * FW + H]
    a["b_fg"] = f["b_forget"][0].reshape(H, 1)
    a["pages"] = f["page_table"].reshape(1, DB * NPG)
    a["cache_k"] = f["cache_k"][0].reshape(-1, PAGE, FW)
    a["cache_v"] = f["cache_v"][0].reshape(-1, PAGE, FW)
    a["cache_lfT"] = f["cache_logf"][0].transpose(0, 2, 1)
    g_ = lambda v: v.reshape(G, NST, -1).transpose(1, 0, 2).reshape(NST, -1)
    two = lambda x, y: np.concatenate([g_(x), g_(y)])
    a["a_re"], a["a_im"] = two(f["ssm_a_re"], f["ssm_a_re"]), two(f["ssm_a_im"], f["ssm_a_im"])
    a["log_dt"] = np.broadcast_to(f["ssm_log_dt"], (P, G))
    br, bi = f["ssm_b_re"], f["ssm_b_im"]
    cr, ci = f["ssm_c_re"][0].transpose(0, 2, 1), f["ssm_c_im"][0].transpose(0, 2, 1)
    a["b_ri"], a["b_ir"], a["c_ri"], a["c_ir"] = two(br, bi), two(bi, br), two(cr, ci), two(ci, cr)
    hr, hi = (f[n][0].transpose(2, 0, 1).reshape(NST, DB * G) for n in ("state_ssm_re", "state_ssm_im"))
    a["h0_ri"], a["h0_ir"] = np.concatenate([hr, hi]), np.concatenate([hi, hr])
    a["d_col"] = np.tile(f["ssm_d"][0].reshape(G, CG).T, (LC, 1))
    a["w_glu"], a["b_gluT"] = f["w_glu"][0], cols(f["b_glu"][0], NGB)
    a["w_out"], a["w_q"] = f["w_out"][0], f["peer_w_q"][0]
    a["g_mixT"] = cols(np.concatenate([f["g_attn_out"][0], f["g_ssm_out"][0]]), KC)
    a["g2T"], a["gfT"] = cols(f["g_norm2"][0], KC), cols(f["g_final"], KC)
    a["subkeysT"] = f["peer_subkeys"][0].transpose(3, 0, 1, 2).reshape(P, 2 * PH * NK)
    a["uT"] = f["peer_u"][0].reshape(NK, NK, KC, P).transpose(1, 3, 2, 0).reshape(NK, P, D)
    a["peer_v"] = f["peer_v"][0]
    a["tri"] = np.where(np.tril(np.ones((P, P))) > 0, 0, NEG).astype(np.float32)
    own = np.eye(H, dtype=np.float32)
    a["sel_neg"] = np.repeat(own[:, :, None] * np.float32(-1 / SCALE), P, axis=2)
    a["sel_pos_s"] = np.repeat(own, DS, axis=1)
    a["sel_neg_s"] = a["sel_pos_s"] * np.float32(-1 / SCALE)
    a["own_q"] = np.tile(np.eye(DS, dtype=np.float32), (H, 1))
    b_, q_, t_ = np.arange(DB), np.tile(np.arange(DS), H), np.arange(DS)
    seen = (b_[None, :, None, None] == b_[None, None, :, None]) & (t_[None, None, None, :] <= q_[:, None, None, None])
    a["mask_s"] = np.where(seen, 0, NEG).astype(np.float32).reshape(H * DS, DB, NSM)
    a["number"] = np.broadcast_to(np.arange(TK, dtype=np.float32), (P, TK))
    a["count"] = np.broadcast_to(np.arange(P, dtype=np.float32), (P, P))
    a["sgn"] = np.repeat(np.array([[-1, 1], [1, -1]], np.float32), NST, axis=0)
    return {n: np.ascontiguousarray(v) for n, v in a.items()}


OUTS = {"kvT": (2 * FW, T), "logfT": (H, T), "yT": (D, T), "end_prompt": (P, G), "end_sample": (P, DB * G)}


def kernel(**inputs):
    import numpy as np
    import concourse.bacc as bacc
    from concourse.bass_utils import run_bass_kernel_spmd

    nc = bacc.Bacc("TRN2", target_bir_lowering=False, num_devices=1)
    arrays, I, O = {}, {}, {}
    for name, a in layout(inputs).items():
        arrays["in_" + name] = a
        I[name] = nc.dram_tensor("in_" + name, a.shape, mybir.dt.from_np(a.dtype), kind="ExternalInput").ap()
    for name, shape in OUTS.items():
        O[name] = nc.dram_tensor("out_" + name, shape, F32, kind="ExternalOutput").ap()
    build(nc, I, O)
    r = run_bass_kernel_spmd(nc, [arrays], core_ids=[0]).results[0]
    out = {n: np.asarray(r["out_" + n]) for n in OUTS}
    y, kv, lf = out["yT"].T, out["kvT"].T, out["logfT"].T
    k, v = kv[:, :FW], kv[:, FW:]
    ep = out["end_prompt"].reshape(2, NST, G).transpose(0, 2, 1)
    es = out["end_sample"].reshape(2, NST, DB, G).transpose(0, 2, 3, 1)
    pr = lambda a, *s: np.ascontiguousarray(a[:NPR]).reshape(1, 1, NPR, *s)
    sm = lambda a, *s: np.ascontiguousarray(a[NPR:]).reshape(1, DB, DS, *s)
    one = lambda a, *s: np.ascontiguousarray(a).reshape(1, *s)
    return (one(y[:NPR], NPR, D), np.ascontiguousarray(y[NPR:]).reshape(DB, DS, D),
            pr(k, H, DH), pr(v, H, DH), pr(lf, H), one(ep[0], 1, G, NST), one(ep[1], 1, G, NST),
            sm(k, H, DH), sm(v, H, DH), sm(lf, H), one(es[0], DB, G, NST), one(es[1], DB, G, NST))
```

```python
import math
from contextlib import ExitStack

import concourse.bass as bass
import concourse.mybir as mybir
from concourse.alu_op_type import AluOpType as ALU

F32 = mybir.dt.float32
F32R = mybir.dt.float32r
BF16 = mybir.dt.bfloat16
I32 = mybir.dt.int32
U32 = mybir.dt.uint32
ACT = mybir.ActivationFunctionType
AX = mybir.AxisListType.X

P = 128
D = 2048
KC = D // P
NPR = 512
DB, DS = 8, 8
NSM = DB * DS
T = NPR + NSM
HT = T // 2
NC_ = 1 + DB
MODS = 6
NMOD = MODS * KC
H = 8
DH = 128
SCALE = DH ** -0.5
FW = H * DH
PAST, PAGE = 256, 128
NPG = PAST // PAGE
G, NST, CG = 64, 64, 16
SW = G * CG
LC = 8
NCK = NPR // LC
CK = NCK + DB
GB = P // CG
NGB = G // GB
PH, NK, TK = 8, 128, 16
EPS = 1e-6
NEG = -1e30
WB = 512
TB = 32
NTB = T // TB
NTT = -(-T // P)


class Chain:

    def __init__(self, eng, sem):
        self.eng, self.sem, self.n, self.base = eng, sem, 0, 0

    def __call__(self, ins):
        ins.then_inc(self.sem, 1)
        self.n += 1
        self.eng.wait_ge(self.sem, self.base + self.n)

    def mark(self, ins):
        ins.then_inc(self.sem, 1)
        self.n += 1

    def settle(self):
        self.eng.wait_ge(self.sem, self.base + self.n)

    def loop(self, i, per):
        self.start, self.per = self.n, per
        self.base = i * per

    def end_loop(self, count):
        assert self.n - self.start == self.per, (self.n - self.start, self.per)
        self.base = 0
        self.n = self.start + count * self.per


def fold(psum, n=HT):
    return psum[:, :, 0:n]


def halves(ap):
    return ap.rearrange("p (a t) -> p a t", a=2)


def bc(ap, axis, shape):
    return ap.unsqueeze(axis).broadcast_to(shape)


def product(pe, out, pairs, start=True, stop=True):
    n = 0
    for (w_hi, w_lo), (m_hi, m_lo) in pairs:
        for w, mv in ((w_hi, m_hi), (w_hi, m_lo), (w_lo, m_hi)):
            n += 1
            for a in range(2):
                mm = pe.matmul(out[:, a, 0:HT], w, mv[:, a * HT:(a + 1) * HT],
                               start=(start and n == 1), stop=(stop and n == 3 * len(pairs)))
    return mm


def modulate(nc, I, O, S, C, sem):
    ctx = ExitStack()
    sb = lambda n, s, d=F32: ctx.enter_context(nc.sbuf_tensor(n, s, d))
    ps = lambda n, s, d=F32: ctx.enter_context(nc.psum_tensor(n, s, d))
    KH = KC // 2
    with ctx:
        x, mod = sb("x", [P, KC, T]), S["mod"]
        h_hi, h_lo = S["h_hi"], S["h_lo"]
        free = S["qkvu"][:].rearrange("p c t -> p (c t)")
        raw = [free[:, u * KC * WB:(u + 1) * KC * WB].rearrange("p (k c) -> p k c", k=KC) for u in range(2)]
        w_hi, w_lo = ([part[:].rearrange("p c t -> p (c t)")[:, f * KH * WB:(f + 1) * KH * WB]
                       .rearrange("p (k c) -> p k c", k=KH) for f in range(2)] for part in (h_hi, h_lo))
        sq = [sb(f"sq{u}", [P, T]) for u in range(2)]
        std = sb("std", [P, T])
        rstd = sb("rstd", [P, T])
        c_in = sb("c_in", [P, KC, NC_])
        c_silu = sb("c_silu", [P, KC, NC_])
        c_two = sb("c_two", [P, KC, 2 * NC_], F32R)
        b_ada = sb("b_ada", [P, NMOD])
        g1 = sb("g1", [P, KC])
        scale1 = sb("scale1", [P, KC, NC_])
        row = [sb(f"row{u}", [2 * NC_, WB]) for u in range(2)]
        ps_norm = ps("ps_norm", [P, 2, 512])
        ps_row = [ps(f"ps_row{u}", [P, 512]) for u in range(2)]
        ps_mod = [ps(f"ps_mod{u}", [P, 512]) for u in range(2)]

        x_in, small_in, w_full = sem("x_in"), sem("small_in"), [[sem(f"ada_full{u}{f}") for f in range(2)]
                                                                        for u in range(2)]
        silu_done, c_hi_done, c_lo_done = sem("silu_done"), sem("c_hi_done"), sem("c_lo_done")
        sq_done, sq_used, norm_sum, std_done = (sem(n) for n in ("sq_done", "sq_used", "norm_sum", "std_done"))
        hi_done = [sem(f"ada_hi_done{f}") for f in range(2)]
        lo_done = [sem(f"ada_lo_done{f}") for f in range(2)]
        used = [sem(f"ada_used{f}") for f in range(2)]
        row_copied = [sem(f"row_copied{u}") for u in range(2)]
        mod_t = [sem(f"mod_t{u}") for u in range(2)]
        mod_part, mod_done = ([sem(f"{n}{u}") for u in range(2)] for n in ("mod_part", "mod_done"))
        xn_done, scale_done, h_prompt, h_sample = (sem(n) for n in ("xn_done", "scale_done", "h_prompt", "h_sample"))
        hin_done = sem("hin_hi_done"), sem("hin_lo_done")
        held = sem("ada_held")
        v_step = sem("mod_v_step")
        NA = NMOD * P // WB // 2
        block = ctx.enter_context(nc.Block())

        def lagging(eng, work, after, between):
            work(0, 0, 0)
            work(0, 0, 1)
            between()
            with eng.Fori(0, NA - 1) as i:
                work(2 * i + 1, 1, 0)
                after(i, 0)
                work(2 * i + 1, 1, 1)
                work(2 * i + 2, 0, 0)
                after(i, 1)
                work(2 * i + 2, 0, 1)
            work(2 * NA - 1, 1, 0)
            after(NA - 1, 0)
            work(2 * NA - 1, 1, 1)
            after(NA - 1, 1)

        @block.sync
        def _(sp):
            w_ada = I["w_ada"].rearrange("b p (f n) -> b f p n", f=2)

            def load(n, u):
                for f in range(2):
                    if not isinstance(n, int):
                        sp.wait_ge(lo_done[f], n - 1)
                    sp.dma_start(raw[u][:, f * KH:(f + 1) * KH, :].rearrange("p k c -> p (k c)"),
                                 w_ada[bass.ds(n, 1), f].rearrange("b p n -> (b p) n")).then_inc(w_full[u][f], 16)

            load(0, 0)
            sp.dma_start(x[:], I["xT"].rearrange("(k p) t -> p k t", p=P)).then_inc(x_in, 16)
            load(1, 1)
            with sp.Fori(1, NA) as i:
                for u in range(2):
                    load(2 * i + u, u)

        @block.scalar
        def _(act):
            act.dma_start(c_in[:], I["cT"].rearrange("(k p) r -> p k r", p=P)).then_inc(small_in, 16)
            act.dma_start(b_ada[:], I["b_adaT"]).then_inc(small_in, 16)
            act.dma_start(g1[:], I["g1T"]).then_inc(small_in, 16)
            act.wait_ge(small_in, 48)
            act.activation(c_silu[:], c_in[:], ACT.Silu).then_inc(silu_done, 1)
            act.wait_ge(silu_done, 1)
            act.activation(c_two[:, :, 0:NC_], c_silu[:], ACT.Copy).then_inc(c_hi_done, 1)

            def norm():
                act.wait_ge(x_in, 16)
                for c in range(KC):
                    if c >= 2:
                        act.wait_ge(sq_used, c - 1)
                    act.activation(sq[c % 2][:], x[:, c, :], ACT.Square).then_inc(sq_done, 1)
                act.wait_ge(norm_sum, 1)
                act.activation(halves(std[:]), fold(ps_norm), ACT.Sqrt, scale=1.0 / D, bias=C["eps"][:, 0:1]
                               ).then_inc(std_done, 1)

            def high_parts(n, u, f):
                act.wait_ge(w_full[u][f], 8 * (n - u) + 16)
                act.wait_ge(used[f], n)
                act.activation(w_hi[f], raw[u][:, f * KH:(f + 1) * KH, :], ACT.Copy).then_inc(hi_done[f], 1)

            def copy_row(i, u):
                act.wait_ge(used[1], 2 * i + u + 1)
                act.wait_ge(mod_t[u], i)
                act.activation(row[u][:], ps_row[u][0:2 * NC_, :], ACT.Copy).then_inc(row_copied[u], 1)

            lagging(act, high_parts, copy_row, norm)
            act.wait_ge(scale_done, 1)
            act.wait_ge(xn_done, 1)
            for c in range(KC):
                act.activation(x[:, c, 0:NPR], x[:, c, 0:NPR], ACT.Identity, scale=scale1[:, c, 0:1],
                               bias=mod[:, c, 0:1]).then_inc(h_prompt, 1)
            act.wait_ge(h_sample, 1)
            act.wait_ge(used[0], 2 * NA)
            act.wait_ge(used[1], 2 * NA)
            for c in range(KC):
                act.wait_ge(h_prompt, c + 1)
                act.activation(h_hi[:, c, :], x[:, c, :], ACT.Copy).then_inc(hin_done[0], 1)

        @block.tensor
        def _(pe):
            def norm():
                for c in range(KC):
                    pe.wait_ge(sq_done, c + 1)
                    for a in range(2):
                        mm = pe.matmul(ps_norm[:, a, 0:HT], C["ones"][:], sq[c % 2][:, a * HT:(a + 1) * HT],
                                       start=(c == 0), stop=(c == KC - 1))
                    if c < KC - 1:
                        mm.then_inc(sq_used, 1)
                mm.then_inc(norm_sum, 1)

            pe.wait_ge(c_hi_done, 1)
            pe.wait_ge(c_lo_done, 1)

            def rows(n, u):
                pe.wait_ge(row_copied[u], (n - u) // 2 if isinstance(n, int) else before(u))
                for f in range(2):
                    pe.wait_ge(lo_done[f], n + 1)
                    for k in range(KH):
                        for w in (w_hi, w_lo):
                            mm = pe.matmul(ps_row[u][0:2 * NC_, :], c_two[:, f * KH + k, :], w[f][:, k, :],
                                           start=(f == 0 and k == 0 and w is w_hi),
                                           stop=(f == 1 and k == KH - 1 and w is w_lo))
                    mm.then_inc(used[f], 1)

            def turn(i, u):
                pe.wait_ge(row_copied[u], i + 1)
                pe.wait_ge(mod_done[u], i)
                pe.sem_inc(held, 1)
                for j in range(WB // P):
                    mm = pe.transpose(ps_mod[u][:, 2 * j * NC_:2 * (j + 1) * NC_], row[u][:, j * P:(j + 1) * P],
                                      C["ident"][0:2 * NC_, 0:2 * NC_])
                mm.then_inc(mod_t[u], 1)

            rows(0, 0)
            norm()
            with pe.Fori(0, NA - 1) as i:
                before = lambda u: i + (1 - u)
                turn(i, 0)
                rows(2 * i + 1, 1)
                turn(i, 1)
                rows(2 * i + 2, 0)
            turn(NA - 1, 0)
            rows(2 * NA - 1, 1)
            turn(NA - 1, 1)

        @block.vector
        def _(dve):
            step = Chain(dve, v_step)
            dve.wait_ge(c_hi_done, 1)
            dve.tensor_tensor(c_two[:, :, NC_:2 * NC_], c_silu[:], c_two[:, :, 0:NC_].bitcast(F32), ALU.subtract
                              ).then_inc(c_lo_done, 1)

            def low_parts(n, u, f):
                dve.wait_ge(hi_done[f], n + 1)
                dve.tensor_tensor(w_lo[f], raw[u][:, f * KH:(f + 1) * KH, :], w_hi[f].bitcast(F32),
                                  ALU.subtract).then_inc(lo_done[f], 1)

            def keep(i, u):
                dve.wait_ge(mod_t[u], i + 1)
                dst = mod[:, bass.ds((2 * i + u) * 4, 4), :]
                src = ps_mod[u][:, 0:8 * NC_].rearrange("p (j x r) -> p j x r", j=4, x=2)
                dve.tensor_tensor(dst, src[:, :, 0, :], bc(b_ada[:, bass.ds((2 * i + u) * 4, 4)], 2, [P, 4, NC_]),
                                  ALU.add).then_inc(mod_part[u], 1)
                dve.wait_ge(mod_part[u], i + 1)
                dve.tensor_tensor(dst, src[:, :, 1, :], dst, ALU.add).then_inc(mod_done[u], 1)

            def norm():
                dve.wait_ge(std_done, 1)
                step(dve.reciprocal(rstd[:], std[:]))
                for c in range(KC):
                    ins = dve.tensor_tensor(x[:, c, :], x[:, c, :], rstd[:], ALU.mult)
                    if c == KC - 1:
                        ins.then_inc(xn_done, 1)
                    else:
                        step.mark(ins)
                dve.wait_ge(small_in, 48)

            lagging(dve, low_parts, keep, norm)
            for u in range(2):
                dve.wait_ge(mod_done[u], NA)
            dve.wait_ge(xn_done, 1)
            step.settle()
            step(dve.tensor_scalar(scale1[:], mod[:, KC:2 * KC, :], 1.0, None, ALU.add))
            dve.tensor_tensor(scale1[:], scale1[:], bc(g1[:], 2, [P, KC, NC_]), ALU.mult).then_inc(scale_done, 1)
            dve.wait_ge(scale_done, 1)
            xs = x[:, :, NPR:T].rearrange("p c (b t) -> p c b t", b=DB)
            step(dve.tensor_tensor(xs, xs, bc(scale1[:, :, 1:NC_], 3, [P, KC, DB, DS]), ALU.mult))
            dve.tensor_tensor(xs, xs, bc(mod[:, 0:KC, 1:NC_], 3, [P, KC, DB, DS]), ALU.add).then_inc(h_sample, 1)
            for c in range(KC):
                dve.wait_ge(hin_done[0], c + 1)
                dve.tensor_tensor(h_lo[:, c, :], x[:, c, :], h_hi[:, c, :].bitcast(F32), ALU.subtract
                                  ).then_inc(hin_done[1], 1)


def project_inputs(nc, I, O, S, C, sem):
    ctx = ExitStack()
    sb = lambda n, s, d=F32: ctx.enter_context(nc.sbuf_tensor(n, s, d))
    ps = lambda n, s, d=F32: ctx.enter_context(nc.psum_tensor(n, s, d))
    with ctx:
        h_hi, h_lo, qkvu, logf = S["h_hi"], S["h_lo"], S["qkvu"], S["logf"]
        raw = [sb(f"w_raw{u}", [P, KC, P]) for u in range(2)]
        w_hi = [sb(f"w_hi_in{u}", [P, KC, P], F32R) for u in range(2)]
        w_lo = [sb(f"w_lo_in{u}", [P, KC, P], F32R) for u in range(2)]
        w_fg = sb("w_fg", [P, KC, H])
        w_fg_hi, w_fg_lo = sb("w_fg_hi", [P, KC, H], F32R), sb("w_fg_lo", [P, KC, H], F32R)
        b_fg = sb("b_fg", [H, 1])
        fg, fg_abs, fg_e = (sb(n, [H, T])[:] for n in ("fg", "fg_abs", "fg_e"))
        fg_s, fg_acc, fg_s2 = fg_abs, fg_e, logf[:]
        ps_fg = ps("ps_fg", [P, 2, 512])
        ps_out = [ps(f"ps_proj{q}", [P, 2, 512]) for q in range(2)]
        w_full = [sem(f"w_full{u}") for u in range(2)]
        hi_done, lo_done, proj_done, proj_copied = ([sem(f"{n}{u}") for u in range(2)] for n in (
            "w_hi_done", "w_lo_done", "proj_done", "proj_copied"))
        fg_in, w_fg_done = sem("fg_in"), sem("w_fg_done")
        fg_done, fg_copied, fg_abs_done, fg_exp_done, logf_done = (
            sem(n) for n in ("fg_done", "fg_copied", "fg_abs_done", "fg_exp_done", "logf_done"))
        kv_out = sem("kv_out")
        v_step = sem("proj_v_step")
        NW = 4 * H // 2
        block = ctx.enter_context(nc.Block())

        @block.sync
        def _(sp):
            for u in range(2):
                sp.dma_start(raw[u][:].rearrange("p k c -> p (k c)"), I["w_in"][u]).then_inc(w_full[u], 16)
            with sp.Fori(1, NW) as i:
                for u in range(2):
                    sp.wait_ge(lo_done[u], i)
                    sp.dma_start(raw[u][:].rearrange("p k c -> p (k c)"),
                                 I["w_in"][bass.ds(2 * i + u, 1)].rearrange("b p n -> p (b n)")
                                 ).then_inc(w_full[u], 16)
            for u in range(2):
                sp.wait_ge(proj_copied[u], 3 * H // 2)
            sp.dma_start(O["kvT"].rearrange("(c p) t -> p c t", p=P), qkvu[:, H:3 * H, :]).then_inc(kv_out, 16)
            sp.wait_ge(logf_done, 1)
            sp.dma_start(O["logfT"], logf[:]).then_inc(kv_out, 16)
            sp.wait_ge(kv_out, 32)

        @block.scalar
        def _(act):
            act.dma_start(w_fg[:], I["w_fg"].rearrange("(k p) h -> p k h", p=P)).then_inc(fg_in, 16)
            act.dma_start(b_fg[:], I["b_fg"]).then_inc(fg_in, 16)

            def high_parts(i, u):
                act.wait_ge(w_full[u], 16 * i + 16)
                act.wait_ge(proj_done[u], i)
                act.activation(w_hi[u][:], raw[u][:], ACT.Copy).then_inc(hi_done[u], 1)

            high_parts(0, 0)
            high_parts(0, 1)
            act.wait_ge(fg_copied, 1)
            act.activation(fg_abs, fg, ACT.Abs).then_inc(fg_abs_done, 1)
            act.wait_ge(fg_abs_done, 1)
            act.activation(fg_e, fg_abs, ACT.Exp, scale=-1.0).then_inc(fg_exp_done, 1)

            def copy_out(i):
                act.wait_ge(proj_done[1], i + 1)
                act.activation(qkvu[:, bass.ds(2 * i + 1, 1), :].rearrange("p c (a t) -> p (c a) t", a=2),
                               fold(ps_out[1]), ACT.Copy).then_inc(proj_copied[1], 1)

            with act.Fori(0, NW - 1) as i:
                high_parts(i + 1, 0)
                copy_out(i)
                high_parts(i + 1, 1)
            copy_out(NW - 1)

        @block.tensor
        def _(pe):
            pe.wait_ge(w_fg_done, 2)
            for k in range(KC):
                mm = product(pe, ps_fg[0:H], [((w_fg_hi[:, k, :], w_fg_lo[:, k, :]), (h_hi[:, k, :], h_lo[:, k, :]))],
                             k == 0, k == KC - 1)
            mm.then_inc(fg_done, 1)
            with pe.Fori(0, NW) as i:
                for u in range(2):
                    pe.wait_ge(lo_done[u], i + 1)
                    pe.wait_ge(proj_copied[u], i)
                    for k in range(KC):
                        mm = product(pe, ps_out[u], [((w_hi[u][:, k, :], w_lo[u][:, k, :]),
                                                      (h_hi[:, k, :], h_lo[:, k, :]))], k == 0, k == KC - 1)
                    mm.then_inc(proj_done[u], 1)

        @block.vector
        def _(dve):
            step = Chain(dve, v_step)

            def low_parts(i, u):
                dve.wait_ge(hi_done[u], i + 1)
                dve.tensor_tensor(w_lo[u][:], raw[u][:], w_hi[u][:].bitcast(F32), ALU.subtract
                                  ).then_inc(lo_done[u], 1)

            dve.wait_ge(fg_in, 32)
            dve.tensor_copy(w_fg_hi[:], w_fg[:]).then_inc(w_fg_done, 1)
            dve.wait_ge(w_fg_done, 1)
            dve.tensor_tensor(w_fg_lo[:], w_fg[:], w_fg_hi[:].bitcast(F32), ALU.subtract).then_inc(w_fg_done, 1)
            low_parts(0, 0)
            low_parts(0, 1)

            dve.wait_ge(fg_done, 1)
            dve.tensor_scalar(halves(fg), ps_fg[0:H, :, 0:HT], b_fg[:, 0:1], None, ALU.add
                              ).then_inc(fg_copied, 1)
            dve.wait_ge(fg_exp_done, 1)
            step(dve.tensor_scalar(fg, fg, 0.0, None, ALU.min))
            step(dve.tensor_scalar(fg_s, fg_e, 2.0, None, ALU.add))
            step(dve.reciprocal(fg_s, fg_s))
            step(dve.tensor_tensor(fg_s, fg_s, fg_e, ALU.mult))
            step(dve.tensor_tensor(fg_s2, fg_s, fg_s, ALU.mult))
            step(dve.tensor_scalar(fg_acc, fg_s2, 1.0 / 17, None, ALU.mult))
            for n in (15, 13, 11, 9, 7, 5, 3):
                step(dve.scalar_tensor_tensor(fg_acc, fg_acc, 1.0 / n, fg_s2, ALU.add, ALU.mult))
            step(dve.scalar_tensor_tensor(fg_acc, fg_acc, 1.0, fg_s, ALU.add, ALU.mult))
            dve.scalar_tensor_tensor(logf[:], fg_acc, -2.0, fg, ALU.mult, ALU.add).then_inc(logf_done, 1)

            def copy_out(i):
                dve.wait_ge(proj_done[0], i + 1)
                dve.tensor_copy(qkvu[:, bass.ds(2 * i, 1), :].rearrange("p c (a t) -> p (c a) t", a=2),
                                fold(ps_out[0])).then_inc(proj_copied[0], 1)

            with dve.Fori(0, NW - 1) as i:
                copy_out(i)
                low_parts(i + 1, 0)
                low_parts(i + 1, 1)
            copy_out(NW - 1)


def attend_prompt(nc, I, O, S, C, sem):
    ctx = ExitStack()
    sb = lambda n, s, d=F32: ctx.enter_context(nc.sbuf_tensor(n, s, d))
    ps = lambda n, s, d=F32: ctx.enter_context(nc.psum_tensor(n, s, d))
    NQ = NPR // P
    with ctx:
        qkvu, logf, att = S["qkvu"], S["logf"], S["att"]
        fcum = sb("fcum_p", [H, NPR])
        ones_row = sb("ones_row_p", [H, NPR])
        sel = sb("sel_neg_p", [H, H, P])
        tri = sb("tri", [P, P])
        fk = sb("fk", [P, H, NPR])
        fk_diag = sb("fk_diag", [P, H, NQ, P])
        fq = sb("fq", [P, H, NQ])
        q_st = [sb(f"q_st{u}", [P, NPR]) for u in range(2)]
        v_st = [sb(f"v_st{u}", [P, NPR]) for u in range(2)]
        v_tok = [sb(f"v_tok{u}", [P, NQ, DH]) for u in range(2)]
        s_sb = sb("s_sb", [P, NQ, NPR])
        prob = sb("prob", [P, NQ, NPR])
        p_t = [sb(f"p_t{j}", [P, NPR]) for j in range(2)]
        mx, top, bias, rsum, rinv = (sb(n, [P, NQ]) for n in ("mx", "top", "bias", "rsum", "rinv"))
        ps_s = [ps(f"ps_s{j}", [P, 512]) for j in range(NQ)]
        ps_pt = [ps(f"ps_pt{j}", [P, 512]) for j in range(2)]
        ps_o = ps("ps_o", [P, 512])
        ps_v = ps("ps_v", [P, 512])

        masks, masks_in = sem("ones_row_p_ready"), sem("masks_p_in")
        fcum_done, fk_sum, fk_copied = sem("fcum_p_done"), sem("fk_sum"), sem("fk_copied")
        fq_t, fq_done, fkd_done = sem("fq_t"), sem("fq_done"), sem("fkd_done")
        q_staged, v_staged = sem("q_staged"), sem("v_staged")
        v_turned, v_copied = sem("v_turned"), sem("v_copied")
        s_done, s_read = sem("s_done"), sem("s_read")
        bias_done, p_exp, p_norm = sem("bias_done"), sem("p_exp"), sem("p_norm")
        pt_turned, pt_copied = sem("pt_turned"), sem("pt_copied")
        o_done, o_copied = sem("o_done"), sem("o_copied")
        v_step = sem("attp_v_step")

        block = ctx.enter_context(nc.Block())

        @block.gpsimd
        def _(pool):
            pool.memset(ones_row[:], 1.0).then_inc(masks, 1)

        @block.sync
        def _(sp):
            sp.dma_start(sel[:], I["sel_neg"]).then_inc(masks_in, 16)
            sp.dma_start(tri[:], I["tri"]).then_inc(masks_in, 16)

        @block.scalar
        def _(act):
            for h in range(H):
                act.wait_ge(fk_sum, h + 1)
                act.activation(fk[:, h, :], ps_s[h % NQ][:], ACT.Copy).then_inc(fk_copied, 1)

            def stage_q(h, u):
                act.activation(q_st[u][:], qkvu[:, bass.ds(h, 1), 0:NPR].rearrange("p c t -> p (c t)"), ACT.Copy
                               ).then_inc(q_staged, 1)

            def softmax(h):
                act.wait_ge(bias_done, h + 1)
                act.wait_ge(pt_turned, NQ * h)
                for j in range(NQ):
                    n = (j + 1) * P
                    act.activation(prob[:, j, 0:n], s_sb[:, j, 0:n], ACT.Exp, scale=SCALE, bias=bias[:, j:j + 1],
                                   accum_out=rsum[:, j:j + 1]).then_inc(p_exp, 1)

            def copy_turned(h):
                for j in range(NQ):
                    n = (j + 1) * P
                    act.wait_ge(pt_turned, NQ * h + j + 1)
                    if j >= 1:
                        act.wait_ge(o_done, NQ * h + j - 1)
                    act.activation(p_t[j % 2][:, 0:n], ps_pt[j % 2][:, 0:n], ACT.Copy).then_inc(pt_copied, 1)

            stage_q(0, 0)
            stage_q(1, 1)
            with act.Fori(0, H // 2 - 1) as i:
                for u in range(2):
                    softmax(2 * i + u)
                    stage_q(2 * i + u + 2, u)
                    copy_turned(2 * i + u)
            for h in range(H - 2, H):
                softmax(h)
                copy_turned(h)

        @block.tensor
        def _(pe):
            pe.wait_ge(masks_in, 32)
            pe.wait_ge(fcum_done, 1)
            for h in range(H):
                if h >= NQ:
                    pe.wait_ge(fk_copied, h - NQ + 1)
                pe.matmul(ps_s[h % NQ][:], sel[:, h, :], fcum[:], start=True, stop=True).then_inc(fk_sum, 1)
            for j in range(NQ):
                mm = pe.transpose(ps_o[:, j * H:(j + 1) * H], fcum[:, j * P:(j + 1) * P], C["ident"][0:H, 0:H])
            mm.then_inc(fq_t, 1)
            pe.wait_ge(fk_copied, H)
            pe.wait_ge(fq_done, 1)

            def scores(h, u):
                pe.wait_ge(q_staged, h + 1)
                pe.wait_ge(s_read, NQ * h)
                for j in range(NQ):
                    pe.matmul(ps_s[j][:, 0:(j + 1) * P], q_st[u][:, j * P:(j + 1) * P],
                              qkvu[:, bass.ds(H + h, 1), 0:(j + 1) * P].rearrange("p c t -> p (c t)"),
                              start=True, stop=True).then_inc(s_done, 1)
                pe.wait_ge(v_staged, h + 1)
                pe.wait_ge(v_copied, h)
                for j in range(NQ):
                    mm = pe.transpose(ps_v[:, j * P:(j + 1) * P], v_st[u][:, j * P:(j + 1) * P], C["ident"][:])
                mm.then_inc(v_turned, 1)

            def values(h, u):
                pe.wait_ge(v_copied, h + 1)
                pe.wait_ge(p_norm, h + 1)
                pe.wait_ge(o_copied, h)

                def turn(j):
                    if j >= 2:
                        pe.wait_ge(pt_copied, NQ * h + j - 1)
                    else:
                        pe.wait_ge(pt_copied, NQ * h)
                    for b in range(j + 1):
                        mm = pe.transpose(ps_pt[j % 2][:, b * P:(b + 1) * P], prob[:, j, b * P:(b + 1) * P],
                                          C["ident"][:])
                    mm.then_inc(pt_turned, 1)

                turn(0)
                for j in range(NQ):
                    if j + 1 < NQ:
                        turn(j + 1)
                    pe.wait_ge(pt_copied, NQ * h + j + 1)
                    for b in range(j + 1):
                        mm = pe.matmul(ps_o[:, j * P:(j + 1) * P], v_tok[u][:, b, :],
                                       p_t[j % 2][:, b * P:(b + 1) * P], start=(b == 0), stop=(b == j))
                    mm.then_inc(o_done, 1)

            scores(0, 0)
            with pe.Fori(0, H // 2 - 1) as i:
                for u in range(2):
                    scores(2 * i + u + 1, 1 - u)
                    values(2 * i + u, u)
            scores(H - 1, 1)
            values(H - 2, 0)
            values(H - 1, 1)

        @block.vector
        def _(dve):
            step = Chain(dve, v_step)
            dve.wait_ge(masks, 1)
            dve.wait_ge(masks_in, 32)
            dve.tensor_tensor_scan(fcum[:], ones_row[:], logf[:, 0:NPR], 0.0, ALU.mult, ALU.add
                                   ).then_inc(fcum_done, 1)
            dve.wait_ge(fq_t, 1)
            dve.tensor_copy(fq[:].rearrange("p h j -> p j h"), ps_o[:, 0:NQ * H].rearrange("p (j h) -> p j h", j=NQ)
                            ).then_inc(fq_done, 1)
            dve.wait_ge(fk_copied, H)
            for h in range(H):
                dve.tensor_tensor(fk_diag[:, h], fk[:, h, :].rearrange("p (j k) -> p j k", j=NQ),
                                  bc(tri[:], 1, [P, NQ, P]), ALU.add).then_inc(fkd_done, 1)
            dve.wait_ge(fkd_done, H)
            dve.wait_ge(fq_done, 1)

            def stage_v(h, u):
                dve.tensor_copy(v_st[u][:], qkvu[:, bass.ds(2 * H + h, 1), 0:NPR].rearrange("p c t -> p (c t)")
                                ).then_inc(v_staged, 1)

            def maxima(h):
                dve.wait_ge(p_exp, NQ * h)
                for j in range(NQ):
                    dve.wait_ge(s_done, NQ * h + j + 1)
                    n = j * P
                    if j:
                        step.mark(dve.tensor_tensor(s_sb[:, j, 0:n], ps_s[j][:, 0:n],
                                                    fk[:, bass.ds(h, 1), 0:n].rearrange("p c t -> p (c t)"), ALU.add))
                    dve.tensor_tensor(s_sb[:, j, n:n + P], ps_s[j][:, n:n + P],
                                      fk_diag[:, bass.ds(h, 1), j, :].rearrange("p c t -> p (c t)"), ALU.add
                                      ).then_inc(s_read, 1)
                step.settle()
                dve.wait_ge(s_read, NQ * h + NQ)
                for j in range(NQ):
                    step.mark(dve.tensor_reduce(mx[:, j:j + 1], s_sb[:, j, 0:(j + 1) * P], AX, ALU.max))
                step.settle()
                fq_h = fq[:, bass.ds(h, 1), :].rearrange("p c j -> p (c j)")
                step(dve.scalar_tensor_tensor(top[:], mx[:], SCALE, fq_h, ALU.mult, ALU.add))
                dve.scalar_tensor_tensor(bias[:], top[:], -1.0, fq_h, ALU.mult, ALU.add).then_inc(bias_done, 1)

            def copy_v(h, u):
                dve.wait_ge(v_turned, h + 1)
                dve.tensor_copy(v_tok[u][:].rearrange("p j d -> p (j d)"), ps_v[:]).then_inc(v_copied, 1)

            def normalise(h):
                dve.wait_ge(p_exp, NQ * h + NQ)
                step(dve.reciprocal(rinv[:], rsum[:]))
                for j in range(NQ):
                    n = (j + 1) * P
                    ins = dve.tensor_scalar(prob[:, j, 0:n], prob[:, j, 0:n], rinv[:, j:j + 1], None, ALU.mult)
                    step.mark(ins) if j < NQ - 1 else ins.then_inc(p_norm, 1)

            def copy_out(h):
                dve.wait_ge(o_done, NQ * h + NQ)
                dve.tensor_copy(att[:, bass.ds(h, 1), 0:NPR].rearrange("p c t -> p (c t)"), ps_o[:]
                                ).then_inc(o_copied, 1)

            stage_v(0, 0)
            stage_v(1, 1)
            maxima(0)
            copy_v(0, 0)
            with dve.Fori(0, H // 2 - 1) as i:
                step.loop(i, 2 * (NQ + NQ + NQ))
                for u in range(2):
                    normalise(2 * i + u)
                    stage_v(2 * i + u + 2, u)
                    maxima(2 * i + u + 1)
                    copy_out(2 * i + u)
                    copy_v(2 * i + u + 1, 1 - u)
                step.end_loop(H // 2 - 1)
            normalise(H - 2)
            maxima(H - 1)
            copy_out(H - 2)
            copy_v(H - 1, 1)
            normalise(H - 1)
            copy_out(H - 1)


def attend_sample(nc, I, O, S, C, sem):
    ctx = ExitStack()
    sb = lambda n, s, d=F32: ctx.enter_context(nc.sbuf_tensor(n, s, d))
    ps = lambda n, s, d=F32: ctx.enter_context(nc.psum_tensor(n, s, d))
    R = H * DS
    KW = PAST + NSM
    with ctx:
        qkvu, logf, att = S["qkvu"], S["logf"], S["att"]
        pages = sb("pages", [1, DB * NPG], I32)
        lf_past = sb("lf_past", [H, DB, PAST])
        fc_past = sb("fc_past", [H, DB, PAST])
        fc_new = sb("fc_new", [H, NSM])
        ones_row = sb("ones_row_s", [H, PAST])
        sel_neg = sb("sel_neg_s", [H, R])
        sel_pos = sb("sel_pos_s", [H, R])
        mask = sb("mask_s", [R, DB, NSM])
        own_q = sb("own_q", [R, DS])
        fk = sb("fk_s", [R, DB, KW])
        fq_all = sb("fq_all", [R, DB, DS])
        fq = sb("fq_s", [R, DB])
        k_pg = [sb(f"k_pg{u}", [P, NPG, FW]) for u in range(2)]
        v_pg = [sb(f"v_pg{u}", [P, NPG, FW]) for u in range(2)]
        k_t = sb("k_t", [P, H, KW])
        q_blk = [sb(f"q_blk{u}", [P, H * (R + DS)]) for u in range(2)]
        v_new = sb("v_new", [NSM, FW])
        s_sb = sb("s_sb_s", [R, KW])
        prob = sb("prob_s", [R, KW])
        p_t = sb("p_t_s", [P, 3 * R])
        mx, top, bias, rsum, rinv = (sb(n, [R, 1]) for n in ("mx_s", "top_s", "bias_s", "rsum_s", "rinv_s"))
        ps_k = ps("ps_k", [P, 4, 512])
        ps_s = ps("ps_s_s", [P, 512])
        ps_t = ps("ps_t_s", [P, 512])
        ps_o = ps("ps_o_s", [P, 512])
        ps_fk = [ps_s, ps("ps_x_s", [P, 512])]

        pages_in, consts_in, lf_in = sem("pages_in"), sem("consts_s_in"), sem("lf_in")
        k_in = [sem(f"k_in{u}") for u in range(2)]
        v_in = [sem(f"v_in{u}") for u in range(2)]
        cleared, fc_done = sem("cleared"), sem("fc_s_done")
        fk_sum, fk_done, fq_sum, fq_done = sem("fk_s_sum"), sem("fk_s_done"), sem("fq_s_sum"), sem("fq_s_done")
        vn_turned, vn_copied = sem("vn_turned"), sem("vn_copied")
        kt_turned, kt_copied_a, kt_copied_v = sem("kt_turned"), sem("kt_copied_a"), sem("kt_copied_v")
        q_done, s_done, bias_done, p_exp, p_norm = (sem(n) for n in ("q_blk_done", "s_s_done", "bias_s_done",
                                                                   "p_s_exp", "p_s_norm"))
        pt_turned, pt_copied, o_done, o_copied = (sem(n) for n in ("pt_s_turned", "pt_s_copied", "o_s_done",
                                                                 "o_s_copied"))
        v_step = sem("atts_v_step")
        k_new_done, att_out = sem("k_new_done"), sem("att_out")
        held, held_sp = sem("atts_held"), sem("atts_held_sp")

        block = ctx.enter_context(nc.Block())

        @block.sync
        def _(sp):
            sp.dma_start(pages[:], I["pages"]).then_inc(pages_in, 16)
            sp.dma_start(sel_neg[:], I["sel_neg_s"]).then_inc(consts_in, 16)
            sp.dma_start(sel_pos[:], I["sel_pos_s"]).then_inc(consts_in, 16)
            sp.dma_start(mask[:], I["mask_s"]).then_inc(consts_in, 16)
            sp.dma_start(own_q[:], I["own_q"]).then_inc(consts_in, 16)
            sp.wait_ge(pages_in, 16)

            def load(b, u, slots, cache, full):
                for g in range(NPG):
                    page = sp.value_load(pages[0:1, bass.ds(b * NPG + g, 1)], min_val=0, max_val=I["cache_k"].shape[0] - 1)
                    sp.dma_start(slots[u][:, g, :], I[cache][bass.ds(page, 1)].rearrange("a t n -> t (a n)")
                                 ).then_inc(full[u], 16)

            for b in range(2):
                load(b, b, k_pg, "cache_k", k_in)
                load(b, b, v_pg, "cache_v", v_in)
            att_rows = S["att_dram"].rearrange("(c p) t -> p c t", p=P)
            sp.dma_start(att_rows[:, :, 0:NPR], att[:, :, 0:NPR]).then_inc(att_out, 16)
            with sp.Fori(1, DB // 2) as i:
                for u in range(2):
                    sp.wait_ge(kt_turned, 2 * i + u - 1)
                    sp.sem_inc(held_sp, 1)
                    load(2 * i + u, u, k_pg, "cache_k", k_in)
                    sp.wait_ge(o_done, 2 * i + u - 1)
                    sp.sem_inc(held_sp, 1)
                    load(2 * i + u, u, v_pg, "cache_v", v_in)
            sp.wait_ge(o_copied, DB)
            sp.dma_start(att_rows[:, :, NPR:T], att[:, :, NPR:T]).then_inc(att_out, 16)
            sp.wait_ge(att_out, 32)

        @block.gpsimd
        def _(pool):
            pool.memset(ones_row[:], 1.0).then_inc(cleared, 1)
            for u in range(2):
                pool.memset(q_blk[u][:], 0.0).then_inc(cleared, 1)
            pool.wait_ge(pages_in, 16)
            for b in range(DB):
                for g in range(NPG):
                    page = pool.value_load(pages[0:1, b * NPG + g:b * NPG + g + 1], min_val=0,
                                           max_val=I["cache_k"].shape[0] - 1)
                    pool.dma_start(lf_past[:, b, g * PAGE:(g + 1) * PAGE],
                                   I["cache_lfT"][bass.ds(page, 1)].rearrange("a h t -> (a h) t")).then_inc(lf_in, 16)

        @block.scalar
        def _(act):
            act.wait_ge(vn_turned, 1)
            act.activation(v_new[:].rearrange("p (a n) -> p a n", a=2), ps_k[0:NSM, 0:2, :], ACT.Copy
                           ).then_inc(vn_copied, 1)

            def copy_keys(b):
                act.wait_ge(kt_turned, b + 1)
                act.wait_ge(s_done, b)
                act.activation(k_t[:, 0:4, 0:PAST].rearrange("p (a h) k -> p a h k", a=2),
                               ps_k[:, 0:2, :].rearrange("p a (h k) -> p a h k", h=2), ACT.Copy
                               ).then_inc(kt_copied_a, 1)

            def softmax(b):
                act.wait_ge(bias_done, b + 1)
                act.wait_ge(pt_turned, b)
                act.activation(prob[:], s_sb[:], ACT.Exp, scale=SCALE, bias=bias[:], accum_out=rsum[:]
                               ).then_inc(p_exp, 1)

            def copy_turned(b):
                act.wait_ge(pt_turned, b + 1)
                act.wait_ge(o_done, b)
                act.activation(p_t[:, 0:2 * R], ps_t[:, 0:2 * R], ACT.Copy).then_inc(pt_copied, 1)
                act.activation(p_t[0:NSM, 2 * R:3 * R], ps_t[0:NSM, 2 * R:3 * R], ACT.Copy).then_inc(pt_copied, 1)

            copy_keys(0)
            with act.Fori(0, DB - 1) as b:
                softmax(b)
                copy_keys(b + 1)
                copy_turned(b)
            softmax(DB - 1)
            copy_turned(DB - 1)

        @block.tensor
        def _(pe):
            for h in range(H):
                mm = pe.transpose(ps_k[0:NSM, h // 4, (h % 4) * P:(h % 4 + 1) * P], qkvu[:, 2 * H + h, NPR:T],
                                  C["ident"][:])
            mm.then_inc(vn_turned, 1)
            pe.wait_ge(consts_in, 64)
            pe.wait_ge(fc_done, 2 * DB)
            pe.matmul(ps_o[0:R, 0:NSM], sel_pos[:], fc_new[:], start=True, stop=True).then_inc(fq_sum, 1)
            for b in range(DB):
                if b >= 2:
                    pe.wait_ge(fk_done, 2 * (b - 1))
                pe.matmul(ps_fk[b % 2][0:R, 0:PAST], sel_neg[:], fc_past[:, b, :], start=True, stop=True)
                pe.matmul(ps_fk[b % 2][0:R, PAST:KW], sel_neg[:], fc_new[:], start=True, stop=True
                          ).then_inc(fk_sum, 1)
            pe.wait_ge(vn_copied, 1)
            pe.wait_ge(fk_done, 2 * DB)
            pe.wait_ge(fq_done, 2)
            pe.wait_ge(k_new_done, 1)

            def turn_keys(b, u, turn):
                pe.wait_ge(k_in[u], 32 * turn)
                pe.wait_ge(kt_copied_a, b)
                pe.wait_ge(kt_copied_v, b)
                for h in range(H):
                    for g in range(NPG):
                        mm = pe.transpose(ps_k[:, h // 2, (h % 2) * PAST + g * P:(h % 2) * PAST + (g + 1) * P],
                                          k_pg[u][:, g, h * DH:(h + 1) * DH], C["ident"][:])
                mm.then_inc(kt_turned, 1)

            def scores(b, u):
                pe.wait_ge(kt_copied_a, b + 1)
                pe.wait_ge(kt_copied_v, b + 1)
                pe.wait_ge(q_done, b + 1)
                for h in range(H):
                    mm = pe.matmul(ps_s[0:R, 0:KW], q_blk[u][:, h * R:(h + 1) * R], k_t[:, h, :],
                                   start=(h == 0), stop=(h == H - 1))
                mm.then_inc(s_done, 1)

            def values(b, u, turn):
                pe.wait_ge(p_norm, b + 1)
                pe.wait_ge(pt_copied, 2 * b)
                pe.sem_inc(held, 1)
                pe.transpose(ps_t[:, 0:R], prob[:, 0:P], C["ident"][0:R, 0:R])
                pe.transpose(ps_t[:, R:2 * R], prob[:, P:2 * P], C["ident"][0:R, 0:R])
                pe.transpose(ps_t[0:NSM, 2 * R:3 * R], prob[:, PAST:KW], C["ident"][0:R, 0:R]).then_inc(pt_turned, 1)
                pe.wait_ge(pt_copied, 2 * b + 2)
                pe.wait_ge(v_in[u], 32 * turn)
                pe.wait_ge(o_copied, b)
                for h in range(H):
                    q = slice(h * DS, (h + 1) * DS)
                    for g in range(NPG):
                        pe.matmul(ps_o[:, q], v_pg[u][:, g, h * DH:(h + 1) * DH],
                                  p_t[:, g * R + h * DS:g * R + (h + 1) * DS], start=(g == 0), stop=False)
                    mm = pe.matmul(ps_o[:, q], v_new[:, h * DH:(h + 1) * DH],
                                   p_t[0:NSM, 2 * R + h * DS:2 * R + (h + 1) * DS], start=False, stop=True)
                mm.then_inc(o_done, 1)

            turn_keys(0, 0, 1)
            with pe.Fori(0, DB // 2 - 1) as i:
                for u in range(2):
                    b = 2 * i + u
                    scores(b, u)
                    turn_keys(b + 1, 1 - u, i + 1 + u)
                    values(b, u, i + 1)
            scores(DB - 2, 0)
            turn_keys(DB - 1, 1, DB // 2)
            values(DB - 2, 0, DB // 2)
            scores(DB - 1, 1)
            values(DB - 1, 1, DB // 2)

        @block.vector
        def _(dve):
            step = Chain(dve, v_step)
            dve.wait_ge(cleared, 3)
            dve.wait_ge(lf_in, 16 * DB * NPG)
            for b in range(DB):
                dve.tensor_tensor_scan(fc_past[:, b, :], ones_row[:], lf_past[:, b, :], 0.0, ALU.mult, ALU.add
                                       ).then_inc(fc_done, 1)
            dve.wait_ge(fc_done, DB)
            for b in range(DB):
                dve.tensor_tensor_scan(fc_new[:, b * DS:(b + 1) * DS], ones_row[:, 0:DS],
                                       logf[:, NPR + b * DS:NPR + (b + 1) * DS], fc_past[:, b, PAST - 1:PAST],
                                       ALU.mult, ALU.add).then_inc(fc_done, 1)
            dve.wait_ge(consts_in, 64)
            dve.wait_ge(fq_sum, 1)
            dve.tensor_tensor(fq_all[:], ps_o[0:R, 0:NSM].rearrange("p (b t) -> p b t", b=DB),
                              bc(own_q[:], 1, [R, DB, DS]), ALU.mult).then_inc(fq_done, 1)
            dve.wait_ge(fq_done, 1)
            dve.tensor_reduce(fq[:], fq_all[:], AX, ALU.add).then_inc(fq_done, 1)
            for b in range(DB):
                dve.wait_ge(fk_sum, b + 1)
                dve.tensor_copy(fk[:, b, 0:PAST], ps_fk[b % 2][0:R, 0:PAST]).then_inc(fk_done, 1)
                dve.tensor_tensor(fk[:, b, PAST:KW], ps_fk[b % 2][0:R, PAST:KW], mask[:, b, :], ALU.add).then_inc(fk_done, 1)
            dve.wait_ge(fk_done, 2 * DB)
            dve.wait_ge(fq_done, 2)

            def spread_queries(b, u):
                dve.tensor_copy(q_blk[u][:].rearrange("p (h x) -> p h x", h=H)[:, :, 0:DS],
                                qkvu[:, 0:H, bass.ds(NPR + b * DS, DS)]).then_inc(q_done, 1)

            def copy_keys(b):
                dve.wait_ge(kt_turned, b + 1)
                dve.wait_ge(s_done, b)
                dve.tensor_copy(k_t[:, 4:8, 0:PAST].rearrange("p (a h) k -> p a h k", a=2),
                                ps_k[:, 2:4, :].rearrange("p a (h k) -> p a h k", h=2)).then_inc(kt_copied_v, 1)

            def maxima(b):
                dve.wait_ge(s_done, b + 1)
                dve.wait_ge(p_exp, b)
                step(dve.tensor_tensor(s_sb[:], ps_s[0:R, 0:KW],
                                       fk[:, bass.ds(b, 1), :].rearrange("p c t -> p (c t)"), ALU.add))
                step(dve.tensor_reduce(mx[:], s_sb[:], AX, ALU.max))
                step(dve.scalar_tensor_tensor(top[:], mx[:], SCALE, fq[:, bass.ds(b, 1)], ALU.mult, ALU.add))
                dve.scalar_tensor_tensor(bias[:], top[:], -1.0, fq[:, bass.ds(b, 1)], ALU.mult, ALU.add
                                         ).then_inc(bias_done, 1)

            def normalise(b):
                dve.wait_ge(p_exp, b + 1)
                step(dve.reciprocal(rinv[:], rsum[:]))
                dve.tensor_scalar(prob[:], prob[:], rinv[:, 0:1], None, ALU.mult).then_inc(p_norm, 1)

            def copy_out(b):
                dve.wait_ge(o_done, b + 1)
                dve.tensor_copy(att[:, :, bass.ds(NPR + b * DS, DS)],
                                ps_o[:, 0:R].rearrange("p (h q) -> p h q", h=H)).then_inc(o_copied, 1)

            dve.tensor_copy(k_t[:, :, PAST:KW], qkvu[:, H:2 * H, NPR:T]).then_inc(k_new_done, 1)
            spread_queries(0, 0)
            spread_queries(1, 1)
            copy_keys(0)
            with dve.Fori(0, DB // 2 - 1) as i:
                step.loop(i, 8)
                for u in range(2):
                    b = 2 * i + u
                    maxima(b)
                    spread_queries(b + 2, u)
                    copy_keys(b + 1)
                    normalise(b)
                    copy_out(b)
                step.end_loop(DB // 2 - 1)
            maxima(DB - 2)
            copy_keys(DB - 1)
            normalise(DB - 2)
            copy_out(DB - 2)
            maxima(DB - 1)
            normalise(DB - 1)
            copy_out(DB - 1)


def s5_layer(nc, I, O, S, C, sem):
    qkvu = S["qkvu"]
    free = qkvu[:, 0:3 * H, :].rearrange("p c t -> p (c t)")
    u_all = qkvu[:, 3 * H:4 * H, :]
    at = [0]

    def carve(n):
        at[0] += n
        assert at[0] <= 3 * H * T
        return free[:, at[0] - n:at[0]]

    local = carve(CK * 2 * G).rearrange("p (k x g) -> p k x g", x=2, g=G)
    bb = carve(G * CG).rearrange("p (g c) -> p g c", g=G)
    bb_i = carve(G * CG).rearrange("p (g c) -> p g c", g=G)
    c_x = carve(G * CG).rearrange("p (g c) -> p g c", g=G)
    c_y = carve(G * CG).rearrange("p (g c) -> p g c", g=G)
    o_dram = nc.dram_tensor("o_scratch", [NGB, P, GB * P], F32).ap()
    outer = ExitStack()
    with outer:
        osb = lambda n, s, d=F32: outer.enter_context(nc.sbuf_tensor(n, s, d))
        prev = osb("prev", [P, CK, G])
        y_loc = osb("y_loc", [CK, G, P])
        pw_r = osb("pw_r", [P, G, LC + 1])
        pw_i = osb("pw_i", [P, G, LC + 1])

        ctx = ExitStack()
        sb = lambda n, s, d=F32: ctx.enter_context(nc.sbuf_tensor(n, s, d))
        ps = lambda n, s, d=F32: ctx.enter_context(nc.psum_tensor(n, s, d))
        with ctx:
            rev_r, rev_i = sb("rev_r", [P, G, LC]), sb("rev_i", [P, G, LC])
            a_re, a_im, log_dt = (sb(n, [P, G]) for n in ("a_re", "a_im", "log_dt"))
            dt, mag, ang, turns, sin, cos, c_re, c_im, t1, t2, den = (
                sb(n, [P, G]) for n in ("dt", "mag", "ang", "turns", "sin", "cos", "c_re", "c_im", "t1", "t2", "den"))
            sgn = sb("sgn", [P, 2])
            half_pi = sb("half_pi", [P, 1])
            d_col = sb("d_col", [P, G])
            tmp_p, tmp_q = sb("tmp_p", [P, G, 4]), sb("tmp_q", [P, G, 4])
            u_st = sb("u_st", [P, LC, CK])
            u_tok = sb("u_tok", [CK, GB, LC, CG])
            u_lhs = sb("u_lhs", [P, GB, CK])
            o_pow = sb("o_pow", [P, GB, LC + 1, CG])
            b_st = sb("b_st", [P, GB, CG])
            taps = sb("taps", [CG, GB, 2 * LC - 1, CG])
            m_raw = sb("m_raw", [P, GB, P])
            o_tmp = sb("o_tmp", [P, GB, LC + 1, CG])
            e_s, e_t = (sb(n, [P, GB, LC, CG]) for n in ("e_s", "e_t"))
            e_tmp = sb("e_tmp", [P, GB, LC, CG])
            e_rows = sb("e_rows", [P, GB, 2, P])
            m_rows = sb("m_rows", [P, GB, P])
            ps_a, ps_b, ps_m, ps_e = (ps(n, [P, 2, 512]) for n in ("ps_a", "ps_b", "ps_m", "ps_e"))

            par_in, b_in, h0_in = sem("par_in"), sem("b_in"), sem("h0_in")
            cleared = sem("s5_cleared")
            dt_done, arg_done, trig_done, coef_done = (sem(n) for n in ("dt_done", "arg_done", "trig_done",
                                                                        "coef_done"))
            u_staged, a_turned, u_tok_done, b_turned, u_lhs_done = (
                sem(n) for n in ("u_staged", "a_turned", "u_tok_done", "b_turned", "u_lhs_done"))
            taps_done, taps_copied, m_in = sem("taps_done"), sem("taps_copied"), sem("m_in")
            pows_done, m_copied, e_done, e_turned, e_copied = (
                sem(n) for n in ("pows_done", "m_copied", "e_done", "e_turned", "e_copied"))
            yl_done, yl_copied, hs_done, ht_done, h_copied, o_out = (
                sem(n) for n in ("yl_done", "yl_copied", "hs_done", "ht_done", "h_copied", "o_out"))
            v_step, g_step = sem("s5_v_step"), sem("s5_g_step")
            held, held_sp = sem("s5_held"), sem("s5_held_sp")

            block = ctx.enter_context(nc.Block())

            @block.sync
            def _(sp):
                for dst, n in ((a_re, "a_re"), (a_im, "a_im"), (log_dt, "log_dt"), (sgn, "sgn"), (d_col, "d_col")):
                    sp.dma_start(dst[:], I[n]).then_inc(par_in, 16)
                for dst, n in ((bb, "b_ri"), (bb_i, "b_ir"), (c_x, "c_ri"), (c_y, "c_ir")):
                    sp.dma_start(dst, I[n].rearrange("p (g c) -> p g c", g=G)).then_inc(b_in, 16)
                sp.dma_start(prev[:, NCK:CK, :], I["h0_ri"].rearrange("p (b g) -> p b g", b=DB)).then_inc(h0_in, 16)
                with sp.Fori(0, NGB) as cb:
                    sp.wait_ge(pows_done, 2 * cb + 2)
                    sp.dma_start(o_dram[bass.ds(cb, 1)].rearrange("a p (g x) -> (a p) g x", g=GB),
                                 o_pow[:, :, 1:LC + 1, :].rearrange("p g b c -> p g (b c)")).then_inc(o_out, 16)
                    sp.wait_ge(taps_copied, cb + 1)
                    sp.sem_inc(held_sp, 1)
                    sp.wait_ge(m_copied, GB * cb)
                    for s in range(LC):
                        sp.dma_start(m_raw[s * CG:(s + 1) * CG],
                                     taps[:, :, LC - 1 - s:2 * LC - 1 - s, :].rearrange("p g b c -> p g (b c)")
                                     ).then_inc(m_in, 16)
                sp.wait_ge(o_out, 16 * NGB)
                sp.wait_ge(h0_in, 16)

            @block.scalar
            def _(act):
                act.wait_ge(par_in, 80)
                act.activation(dt[:], log_dt[:], ACT.Exp).then_inc(dt_done, 1)
                act.wait_ge(arg_done, 1)
                act.activation(mag[:], t1[:], ACT.Exp).then_inc(trig_done, 1)
                act.activation(sin[:], ang[:], ACT.Sin).then_inc(trig_done, 1)
                act.wait_ge(cleared, 3)
                act.activation(cos[:], t2[:], ACT.Sin, scale=-1.0, bias=half_pi[:, 0:1]).then_inc(trig_done, 1)
                with act.Fori(0, NGB) as cb:
                    act.wait_ge(a_turned, cb)
                    act.activation(u_st[:], u_all[:, bass.ds(cb, 1), :].rearrange("p c (k s) -> p s (c k)", s=LC),
                                   ACT.Copy).then_inc(u_staged, 1)
                    act.wait_ge(a_turned, cb + 1)
                    act.wait_ge(b_turned, cb)
                    for r in range(2):
                        act.activation(u_tok[:, :, 4 * r:4 * r + 4, :].rearrange("k g s c -> k s g c"),
                                       ps_a[0:CK, r, :].rearrange("k (s g c) -> k s g c", s=4, g=GB), ACT.Copy
                                       ).then_inc(u_tok_done, 1)
                    act.wait_ge(b_turned, cb + 1)
                    act.wait_ge(ht_done, cb)
                    act.activation(u_lhs[:].rearrange("p (r g) k -> p r (g k)", r=2), ps_b[:, :, 0:4 * CK], ACT.Copy
                                   ).then_inc(u_lhs_done, 1)
                    for r in range(2):
                        act.wait_ge(e_turned, 2 * cb + r + 1)
                        act.activation(e_rows[:, 4 * r:4 * r + 4].rearrange("p g x q -> p x g q"),
                                       ps_e[:].rearrange("p x (g q) -> p x g q", g=4), ACT.Copy).then_inc(e_copied, 1)
                    act.wait_ge(yl_done, cb + 1)
                    act.activation(y_loc[:, bass.ds(GB * cb, GB), :].rearrange("k (r g) q -> k r (g q)", r=2),
                                   ps_a[0:CK, :, :], ACT.Copy).then_inc(yl_copied, 1)

            @block.tensor
            def _(pe):
                ident = C["ident"]

                def find_taps(n):
                    pe.wait_ge(pows_done, 2 * n + 2)
                    pe.wait_ge(taps_copied, n)
                    for g in range(GB):
                        mm = pe.matmul(ps_m[0:CG, g // 4, (g % 4) * P:(g % 4 + 1) * P], b_st[:, g, :],
                                       o_pow[:, g, 0:LC, :].rearrange("p b c -> p (b c)"), start=True, stop=True)
                    mm.then_inc(taps_done, 1)

                def body(cb, more):
                    pe.wait_ge(u_staged, cb + 1)
                    pe.wait_ge(yl_copied, cb)
                    for s in range(LC):
                        mm = pe.transpose(ps_a[0:CK, s // 4, (s % 4) * P:(s % 4 + 1) * P], u_st[:, s, :], ident[:])
                    mm.then_inc(a_turned, 1)
                    pe.wait_ge(u_tok_done, 2 * cb + 2)
                    pe.wait_ge(h_copied, 2 * cb)
                    for g in range(GB):
                        mm = pe.transpose(ps_b[:, g // 4, (g % 4) * CK:(g % 4 + 1) * CK],
                                          u_tok[:, g].rearrange("k s c -> k (s c)"), ident[0:CK, 0:CK])
                    mm.then_inc(b_turned, 1)
                    if more:
                        find_taps(cb + 1)

                    def turn_e(r):
                        pe.wait_ge(e_copied, 2 * cb + r)
                        for g in range(4):
                            for x, e in enumerate((e_s, e_t)):
                                mm = pe.transpose(ps_e[:, x, g * P:(g + 1) * P],
                                                  e[:, 4 * r + g].rearrange("p s c -> p (s c)"), ident[:])
                        mm.then_inc(e_turned, 1)

                    pe.wait_ge(e_done, cb + 1)
                    turn_e(0)
                    pe.wait_ge(u_lhs_done, cb + 1)
                    pe.wait_ge(m_copied, GB * cb + GB)
                    for g in range(GB):
                        mm = pe.matmul(ps_a[0:CK, g // 4, (g % 4) * P:(g % 4 + 1) * P], u_lhs[:, g, :],
                                       m_rows[:, g, :], start=True, stop=True)
                    mm.then_inc(yl_done, 1)
                    turn_e(1)
                    pe.wait_ge(e_copied, 2 * cb + 2)
                    for x, (bank, done) in enumerate(((ps_b, hs_done), (ps_e, ht_done))):
                        for g in range(GB):
                            mm = pe.matmul(bank[:, g // 4, (g % 4) * CK:(g % 4 + 1) * CK], e_rows[:, g, x, :],
                                           u_lhs[:, g, :], start=True, stop=True)
                        mm.then_inc(done, 1)

                find_taps(0)
                with pe.Fori(0, NGB - 1) as cb:
                    body(cb, True)
                body(NGB - 1, False)

            @block.gpsimd
            def _(pool):
                pool.memset(taps[:], 0.0).then_inc(cleared, 1)
                pool.memset(prev[:, 0, :], 0.0).then_inc(cleared, 1)
                pool.memset(half_pi[:], math.pi / 2).then_inc(cleared, 1)
                chain = Chain(pool, g_step)
                pool.wait_ge(coef_done, 1)

                def step(ins):
                    chain(ins)
                    pool.sem_inc(held, 1)

                with pool.Fori(0, NGB) as cb:
                    chain.loop(cb, 5)
                    g8 = bass.ds(GB * cb, GB)
                    full = [P, GB, LC, CG]
                    br, bi = bc(bb[:, g8, :], 2, full), bc(bb_i[:, g8, :], 2, full)
                    pr, pi = bc(rev_r[:, g8, :], 3, full), bc(rev_i[:, g8, :], 3, full)
                    pool.wait_ge(e_turned, 2 * cb)
                    pool.sem_inc(held, 1)
                    step(pool.tensor_tensor(e_tmp[:], pi, bi, ALU.mult))
                    step(pool.tensor_tensor(e_s[:], pr, br, ALU.mult))
                    step(pool.tensor_tensor(e_s[:], e_s[:], e_tmp[:], ALU.add))
                    step(pool.tensor_tensor(e_tmp[:], pi, br, ALU.mult))
                    step(pool.tensor_tensor(e_t[:], pr, bi, ALU.mult))
                    pool.tensor_tensor(e_t[:], e_t[:], e_tmp[:], ALU.subtract).then_inc(e_done, 1)
                    chain.end_loop(NGB)

            @block.vector
            def _(dve):
                step = Chain(dve, v_step)
                tt = lambda o, a, b, op: step(dve.tensor_tensor(o, a, b, op))
                ts = lambda o, a, s1, s2, op0, op1=None: step(dve.tensor_scalar(o, a, s1, s2, op0, op1) if op1
                                                              else dve.tensor_scalar(o, a, s1, s2, op0))
                dve.wait_ge(par_in, 80)
                ts(a_re[:], a_re[:], -1e-4, None, ALU.min)
                dve.wait_ge(dt_done, 1)
                tt(t1[:], a_re[:], dt[:], ALU.mult)
                tt(ang[:], a_im[:], dt[:], ALU.mult)
                ts(turns[:], ang[:], 1 / (2 * math.pi), None, ALU.mult)
                ts(turns[:], turns[:], 12582912.0, None, ALU.add)
                ts(turns[:], turns[:], 12582912.0, None, ALU.subtract)
                for part in (6.28125, 0.0019350051879882812, 3.0199159819e-07):
                    step(dve.scalar_tensor_tensor(ang[:], turns[:], -part, ang[:], ALU.mult, ALU.add))
                ts(ang[:], ang[:], 3.1415925, -3.1415925, ALU.min, ALU.max)
                dve.scalar_tensor_tensor(t2[:], ang[:], -1.0, ang[:], ALU.mult, ALU.max).then_inc(arg_done, 1)
                dve.wait_ge(trig_done, 3)
                dve.wait_ge(arg_done, 1)
                dve.wait_ge(cleared, 3)
                ts(pw_r[:, :, 0], a_re[:], 0.0, 1.0, ALU.mult, ALU.add)
                ts(pw_i[:, :, 0], a_re[:], 0.0, None, ALU.mult)
                tt(pw_r[:, :, 1], mag[:], cos[:], ALU.mult)
                tt(pw_i[:, :, 1], mag[:], sin[:], ALU.mult)
                for n in (1, 2, 4):
                    shape = [P, G, n]
                    lo_r, lo_i = pw_r[:, :, 1:1 + n], pw_i[:, :, 1:1 + n]
                    top_r, top_i = pw_r[:, :, n:n + 1].broadcast_to(shape), pw_i[:, :, n:n + 1].broadcast_to(shape)
                    tt(tmp_p[:, :, 0:n], lo_r, top_r, ALU.mult)
                    tt(tmp_q[:, :, 0:n], lo_i, top_i, ALU.mult)
                    tt(pw_r[:, :, 1 + n:1 + 2 * n], tmp_p[:, :, 0:n], tmp_q[:, :, 0:n], ALU.subtract)
                    tt(tmp_p[:, :, 0:n], lo_r, top_i, ALU.mult)
                    tt(tmp_q[:, :, 0:n], lo_i, top_r, ALU.mult)
                    tt(pw_i[:, :, 1 + n:1 + 2 * n], tmp_p[:, :, 0:n], tmp_q[:, :, 0:n], ALU.add)
                for s in range(LC):
                    ts(rev_r[:, :, s], pw_r[:, :, LC - 1 - s], 1.0, None, ALU.mult)
                    ts(rev_i[:, :, s], pw_i[:, :, LC - 1 - s], 1.0, None, ALU.mult)
                ts(t1[:], pw_r[:, :, 1], -1.0, None, ALU.add)
                tt(den[:], a_re[:], a_re[:], ALU.mult)
                tt(t2[:], a_im[:], a_im[:], ALU.mult)
                tt(den[:], den[:], t2[:], ALU.add)
                step(dve.reciprocal(den[:], den[:]))
                tt(c_re[:], t1[:], a_re[:], ALU.mult)
                tt(t2[:], pw_i[:, :, 1], a_im[:], ALU.mult)
                tt(c_re[:], c_re[:], t2[:], ALU.add)
                tt(c_re[:], c_re[:], den[:], ALU.mult)
                tt(c_im[:], pw_i[:, :, 1], a_re[:], ALU.mult)
                tt(t2[:], t1[:], a_im[:], ALU.mult)
                tt(c_im[:], c_im[:], t2[:], ALU.subtract)
                tt(c_im[:], c_im[:], den[:], ALU.mult)
                dve.wait_ge(b_in, 64)
                full = [P, G, CG]
                ts(bb_i, bb_i, sgn[:, 0:1], None, ALU.mult)
                ts(c_x, c_x, sgn[:, 1:2], None, ALU.mult)
                w1 = local[:, 0:CG // 2].rearrange("p k x g -> p (k x g)").rearrange("p (g c) -> p g c", g=G)
                w2 = local[:, CG // 2:CG].rearrange("p k x g -> p (k x g)").rearrange("p (g c) -> p g c", g=G)
                tt(w1, bb_i, bc(c_im[:], 2, full), ALU.mult)
                tt(w2, bb, bc(c_im[:], 2, full), ALU.mult)
                tt(bb, bb, bc(c_re[:], 2, full), ALU.mult)
                tt(bb_i, bb_i, bc(c_re[:], 2, full), ALU.mult)
                tt(bb, bb, w1, ALU.add)
                dve.tensor_tensor(bb_i, bb_i, w2, ALU.subtract).then_inc(coef_done, 1)
                dve.wait_ge(coef_done, 1)

                def fill_powers(n):
                    g8 = bass.ds(GB * n, GB)
                    full = [P, GB, LC + 1, CG]
                    cx, cy = bc(c_x[:, g8, :], 2, full), bc(c_y[:, g8, :], 2, full)
                    pr, pi = bc(pw_r[:, g8, :], 3, full), bc(pw_i[:, g8, :], 3, full)
                    dve.wait_ge(taps_done, n)
                    dve.wait_ge(o_out, 16 * n)
                    step.mark(dve.tensor_tensor(o_tmp[:], cy, pi, ALU.mult))
                    step(dve.tensor_tensor(o_pow[:], cx, pr, ALU.mult))
                    dve.tensor_tensor(o_pow[:], o_pow[:], o_tmp[:], ALU.subtract).then_inc(pows_done, 1)
                    dve.tensor_copy(b_st[:], bb[:, g8, :]).then_inc(pows_done, 1)

                def copy_taps(n):
                    dve.wait_ge(taps_done, n + 1)
                    dve.tensor_copy(taps[:, :, LC - 1:2 * LC - 1, :].rearrange("p g b c -> p g (b c)"),
                                    ps_m[0:CG].rearrange("p r (g x) -> p (r g) x", g=4)).then_inc(taps_copied, 1)

                def copy_m(cb):
                    dve.wait_ge(m_in, 16 * LC * cb + 16 * LC)
                    dve.wait_ge(yl_done, cb)
                    for g in range(GB):
                        dve.scalar_tensor_tensor(m_rows[:, g, :], C["ident"][:], d_col[:, bass.ds(GB * cb + g, 1)],
                                                 m_raw[:, g, :], ALU.mult, ALU.add).then_inc(m_copied, 1)

                def copy_ends(cb):
                    for x, (bank, done) in enumerate(((ps_b, hs_done), (ps_e, ht_done))):
                        dve.wait_ge(done, cb + 1)
                        for r in range(2):
                            ins = dve.tensor_copy(local[:, :, x, bass.ds(GB * cb + 4 * r, 4)].rearrange("p k g -> p g k"),
                                                  bank[:, r, 0:4 * CK].rearrange("p (g k) -> p g k", g=4))
                        ins.then_inc(h_copied, 1)

                fill_powers(0)
                copy_taps(0)
                with dve.Fori(0, NGB - 1) as cb:
                    step.loop(cb, 2)
                    fill_powers(cb + 1)
                    copy_m(cb)
                    copy_taps(cb + 1)
                    copy_ends(cb)
                    step.end_loop(NGB - 1)
                copy_m(NGB - 1)
                copy_ends(NGB - 1)

        ctx = ExitStack()
        sb = lambda n, s, d=F32: ctx.enter_context(nc.sbuf_tensor(n, s, d))
        ps = lambda n, s, d=F32: ctx.enter_context(nc.psum_tensor(n, s, d))
        with ctx:
            state = [sb(f"state{j}", [P, 2, G]) for j in range(2)]
            a8_r, a8_i = sb("a8_r", [P, 2, G]), sb("a8_i", [P, 2, G])
            m1, m2 = sb("rec_m1", [P, 2, G]), sb("rec_m2", [P, 2, G])
            h0_t = sb("h0_t", [P, DB, G])
            end_s = sb("end_s", [P, DB, G])
            end_m = sb("end_m", [P, DB, G])
            sgn = sb("sgn2", [P, 2])
            b_glu = sb("b_glu", [P, NGB])
            o_st = [sb(f"o_st{u}", [P, GB, P]) for u in range(2)]
            prev_st = [sb(f"prev_st{u}", [P, GB, CK]) for u in range(2)]
            y = [sb(f"y{u}", [CK, GB, P]) for u in range(2)]
            z_tok = [sb(f"z_tok{u}", [CK, LC, P]) for u in range(2)]
            w_glu = sb("w_glu", [P, NGB, SW])
            gate = [sb(f"glu_gate{u}", [P, T]) for u in range(2)]
            ps_y = ps("ps_y", [P, 2, 512])
            ps_z = ps("ps_z", [P, 2, 512])
            ps_g = [ps(f"ps_g{u}", [P, 2, 512]) for u in range(2)]
            ssm = free[:, CK * 2 * G:CK * 2 * G + NGB * T].rearrange("p (c t) -> p c t", c=NGB)

            consts_in, w_in = sem("s5b_consts"), sem("w_glu_in")
            o_in = [sem(f"o_in{u}") for u in range(2)]
            state_done, terms_done, moved = ([sem(f"{n}{f}") for f in range(2)] for n in (
                "state_done", "terms_done", "moved"))
            prev_done, final_done, ends_out = (sem(n) for n in ("prev_done", "final_done", "ends_out"))
            halves_of_groups = (slice(0, G // 2), slice(G // 2, G))
            prev_staged, y_done, y_added, z_done, z_turned, z_copied = (
                sem(n) for n in ("prev_staged", "y_done", "y_added", "z_done", "z_turned", "z_copied"))
            glu_sum, glu_gated, glu_done = sem("glu_sum"), sem("glu_gated"), sem("glu_done")
            v_step = sem("s5b_v_step")
            block = ctx.enter_context(nc.Block())

            @block.sync
            def _(sp):
                sp.dma_start(h0_t[:], I["h0_ir"].rearrange("p (b g) -> p b g", b=DB)).then_inc(consts_in, 16)
                sp.dma_start(sgn[:], I["sgn"]).then_inc(consts_in, 16)
                sp.dma_start(b_glu[:], I["b_gluT"]).then_inc(consts_in, 16)
                sp.dma_start(w_glu[:], I["w_glu"].rearrange("(k p) n -> p k n", p=P)).then_inc(w_in, 16)
                for u in range(2):
                    sp.dma_start(o_st[u][:].rearrange("p g x -> p (g x)"), o_dram[u]).then_inc(o_in[u], 16)
                with sp.Fori(1, NGB // 2) as i:
                    for u in range(2):
                        sp.wait_ge(y_done, 2 * i + u - 1)
                        sp.dma_start(o_st[u][:].rearrange("p g x -> p (g x)"),
                                     o_dram[bass.ds(2 * i + u, 1)].rearrange("a p n -> (a p) n")).then_inc(o_in[u], 16)
                sp.wait_ge(final_done, 1)
                for f in range(2):
                    sp.wait_ge(state_done[f], NCK + 1)
                sp.dma_start(O["end_prompt"], state[NCK % 2][:, 0, :]).then_inc(ends_out, 16)
                sp.dma_start(O["end_sample"].rearrange("p (b g) -> p b g", b=DB), end_s[:]).then_inc(ends_out, 16)
                ssm_rows = S["ssm_dram"].rearrange("(c p) t -> p c t", p=P)
                for n in range(0, NGB, 2):
                    sp.wait_ge(glu_done, n + 2)
                    sp.dma_start(ssm_rows[:, n:n + 2, :], ssm[:, n:n + 2, :]).then_inc(ends_out, 16)
                sp.wait_ge(ends_out, 16 * (2 + NGB // 2))

            @block.scalar
            def _(act):
                with act.Fori(0, NCK // 2) as i:
                    for u in range(2):
                        for f in range(2):
                            act.wait_ge(state_done[f], 2 * i + u + 1)
                        act.activation(prev[:, bass.ds(2 * i + u, 1), :].rearrange("p k g -> p (k g)"),
                                       state[u][:, 0, :], ACT.Copy).then_inc(prev_done, 1)
                act.wait_ge(prev_done, NCK)

                def stage_prev(cb, u):
                    act.activation(prev_st[u][:].rearrange("p g k -> p k g"), prev[:, :, bass.ds(GB * cb, GB)],
                                   ACT.Copy).then_inc(prev_staged, 1)

                def gelu(cb, u):
                    act.wait_ge(y_added, cb + 1)
                    act.wait_ge(z_turned, cb)
                    act.activation(z_tok[u][:].rearrange("k t (g c) -> k g t c", g=GB),
                                   y[u][:].rearrange("k g (t c) -> k g t c", t=LC), ACT.Gelu_apprx_tanh
                                   ).then_inc(z_done, 1)

                stage_prev(0, 0)
                with act.Fori(0, NGB // 2 - 1) as i:
                    stage_prev(2 * i + 1, 1)
                    gelu(2 * i, 0)
                    stage_prev(2 * i + 2, 0)
                    gelu(2 * i + 1, 1)
                stage_prev(NGB - 1, 1)
                gelu(NGB - 2, 0)
                gelu(NGB - 1, 1)
                for n in range(NGB):
                    act.wait_ge(glu_sum, n + 1)
                    if n >= 2:
                        act.wait_ge(glu_done, n - 1)
                    act.activation(halves(gate[n % 2][:]), fold(ps_g[n % 2]), ACT.Sigmoid, bias=b_glu[:, n:n + 1]
                                   ).then_inc(glu_gated, 1)

            @block.tensor
            def _(pe):
                def carry(cb, u, turn):
                    pe.wait_ge(prev_staged, cb + 1)
                    pe.wait_ge(o_in[u], 16 * turn)
                    pe.wait_ge(y_added, cb)
                    for g in range(GB):
                        mm = pe.matmul(ps_y[0:CK, g // 4, (g % 4) * P:(g % 4 + 1) * P], prev_st[u][:, g, :],
                                       o_st[u][:, g, :], start=True, stop=True)
                    mm.then_inc(y_done, 1)

                def turn_z(cb, u):
                    pe.wait_ge(z_done, cb + 1)
                    pe.wait_ge(z_copied, cb)
                    for t in range(LC):
                        mm = pe.transpose(ps_z[:, t // 4, (t % 4) * CK:(t % 4 + 1) * CK], z_tok[u][:, t, :],
                                          C["ident"][0:CK, 0:CK])
                    mm.then_inc(z_turned, 1)

                carry(0, 0, 1)
                with pe.Fori(0, NGB // 2 - 1) as i:
                    carry(2 * i + 1, 1, i + 1)
                    turn_z(2 * i, 0)
                    carry(2 * i + 2, 0, i + 2)
                    turn_z(2 * i + 1, 1)
                carry(NGB - 1, 1, NGB // 2)
                turn_z(NGB - 2, 0)
                turn_z(NGB - 1, 1)
                pe.wait_ge(z_copied, NGB)
                pe.wait_ge(w_in, 16)
                for n in range(NGB):
                    if n >= 2:
                        pe.wait_ge(glu_gated, n - 1)
                    for k in range(NGB):
                        for a in range(2):
                            mm = pe.matmul(ps_g[n % 2][:, a, 0:HT], w_glu[:, k, n * P:(n + 1) * P],
                                           u_all[:, k, a * HT:(a + 1) * HT], start=(k == 0), stop=(k == NGB - 1))
                    mm.then_inc(glu_sum, 1)

            @block.vector
            def _(dve):
                step = Chain(dve, v_step)
                dve.wait_ge(consts_in, 48)
                for x in range(2):
                    step.mark(dve.tensor_copy(a8_r[:, x, :], pw_r[:, :, LC]))
                step.mark(dve.tensor_copy(a8_i[:, 0, :], pw_i[:, :, LC]))
                step.mark(dve.tensor_scalar(a8_i[:, 1, :], pw_i[:, :, LC], -1.0, None, ALU.mult))
                step(dve.tensor_scalar(h0_t[:], h0_t[:], sgn[:, 0:1], None, ALU.mult))
                full = [P, DB, G]
                step.mark(dve.tensor_tensor(end_m[:], h0_t[:], bc(pw_i[:, :, LC], 1, full), ALU.mult))
                step(dve.tensor_tensor(end_s[:], prev[:, NCK:CK, :], bc(pw_r[:, :, LC], 1, full), ALU.mult))
                step(dve.tensor_tensor(end_s[:], end_s[:], end_m[:], ALU.add))
                dve.tensor_tensor(end_s[:], end_s[:], local[:, NCK:CK, 0, :], ALU.add).then_inc(final_done, 1)
                step.settle()
                for f, half in enumerate(halves_of_groups):
                    dve.memset(state[0][:, :, half], 0.0).then_inc(state_done[f], 1)
                with dve.Fori(0, NCK // 2) as i:
                    for u in range(2):
                        k, old, new = 2 * i + u, state[u], state[1 - u]
                        for f, half in enumerate(halves_of_groups):
                            dve.wait_ge(state_done[f], k + 1)
                            dve.tensor_tensor(m1[:, :, half], a8_r[:, :, half], old[:, :, half], ALU.mult
                                              ).then_inc(terms_done[f], 1)
                            for x in range(2):
                                dve.tensor_tensor(m2[:, x, half], a8_i[:, x, half], old[:, 1 - x, half], ALU.mult
                                                  ).then_inc(terms_done[f], 1)
                        for f, half in enumerate(halves_of_groups):
                            dve.wait_ge(terms_done[f], 3 * k + 3)
                            dve.tensor_tensor(m1[:, :, half], m1[:, :, half], m2[:, :, half], ALU.add
                                              ).then_inc(moved[f], 1)
                        for f, half in enumerate(halves_of_groups):
                            dve.wait_ge(moved[f], k + 1)
                            if f == 0:
                                dve.wait_ge(prev_done, k)
                            dve.tensor_tensor(new[:, :, half], m1[:, :, half],
                                              local[:, bass.ds(k, 1), :, half].rearrange("p k x g -> p (k x) g"),
                                              ALU.add).then_inc(state_done[f], 1)

                def add_carried(cb, u):
                    dve.wait_ge(y_done, cb + 1)
                    if not (isinstance(cb, int) and cb < 2):
                        dve.wait_ge(z_done, cb - 1)
                    dve.tensor_tensor(y[u][:].rearrange("k (r g) q -> k r (g q)", r=2), ps_y[0:CK, :, :],
                                      y_loc[:, bass.ds(GB * cb, GB), :].rearrange("k (r g) q -> k r (g q)", r=2),
                                      ALU.add).then_inc(y_added, 1)

                def copy_z(cb):
                    dve.wait_ge(z_turned, cb + 1)
                    for r in range(2):
                        ins = dve.tensor_copy(
                            u_all[:, bass.ds(cb, 1), :].rearrange("p c (k t) -> p t (c k)", t=LC)[:, 4 * r:4 * r + 4],
                            ps_z[:, r, 0:4 * CK].rearrange("p (t k) -> p t k", t=4))
                    ins.then_inc(z_copied, 1)

                add_carried(0, 0)
                with dve.Fori(0, NGB // 2 - 1) as i:
                    add_carried(2 * i + 1, 1)
                    copy_z(2 * i)
                    add_carried(2 * i + 2, 0)
                    copy_z(2 * i + 1)
                add_carried(NGB - 1, 1)
                copy_z(NGB - 2)
                copy_z(NGB - 1)
                dve.wait_ge(z_copied, NGB)
                for n in range(NGB):
                    dve.wait_ge(glu_gated, n + 1)
                    dve.tensor_tensor(ssm[:, n, :], u_all[:, n, :], gate[n % 2][:], ALU.mult).then_inc(glu_done, 1)


def merge_and_query(nc, I, O, S, C, sem):
    ctx = ExitStack()
    sb = lambda n, s, d=F32: ctx.enter_context(nc.sbuf_tensor(n, s, d))
    ps = lambda n, s, d=F32: ctx.enter_context(nc.psum_tensor(n, s, d))
    with ctx:
        mod, h_hi, h_lo = S["mod"], S["h_hi"], S["h_lo"]
        h = sb("mix_h2", [P, KC, T])
        x = sb("x1", [P, KC, T])
        raw = [sb(f"wo_raw{u}", [P, KC, P]) for u in range(2)]
        w_hi = [sb(f"wo_hi{u}", [P, KC, P], F32R) for u in range(2)]
        w_lo = [sb(f"wo_lo{u}", [P, KC, P], F32R) for u in range(2)]
        rstd = sb("rstd2", [P, T])
        g_mix, g2 = sb("g_mix", [P, KC]), sb("g2", [P, KC])
        scale2 = sb("scale2", [P, KC, NC_])
        gated = sb("gated", [P, NSM])
        q_st = [sb(f"q_store{u}", [P, NTT * P]) for u in range(2)]
        sq = [q_st[u][:, 0:T] for u in range(2)]
        ps_norm = ps("ps_norm2", [P, 2, 512])
        ps_out = [ps(f"ps_out{q}", [P, 2, 512]) for q in range(2)]

        mix_in, x_in, g_in = sem("mix_in"), sem("x1_in"), sem("g_mix_in")
        w_full, hi_done, lo_done, out_done, out_read = ([sem(f"{n}{u}") for u in range(2)] for n in (
            "wo_full", "wo_hi_done", "wo_lo_done", "wo_done", "wo_read"))
        sq_done, sq_used, std_done, rstd_done = (sem(n) for n in ("sq2_done", "sq2_used", "std2_done", "rstd2_done"))
        mixed, m_hi_done, m_lo_done = sem("mixed"), sem("m_hi_done"), sem("m_lo_done")
        scale_done, xn_done, h_prompt, h_sample, x_out = (
            sem(n) for n in ("scale2_done", "xn2_done", "h2_prompt", "h2_sample", "x1_out"))
        h_hi_done, h_lo_done = sem("h2_hi_done"), sem("h2_lo_done")
        q_pad, q_out = sem("q_pad"), [sem(f"q_out{u}") for u in range(2)]
        v_step = sem("merge_v_step")
        NW = KC // 2
        block = ctx.enter_context(nc.Block())

        @block.sync
        def _(sp):
            sp.dma_start(h[:, 0:H, :], S["att_dram"].rearrange("(c p) t -> p c t", p=P)).then_inc(mix_in, 16)
            sp.dma_start(h[:, H:KC, :], S["ssm_dram"].rearrange("(c p) t -> p c t", p=P)).then_inc(mix_in, 16)
            sp.dma_start(g_mix[:], I["g_mixT"]).then_inc(g_in, 16)
            sp.dma_start(g2[:], I["g2T"]).then_inc(g_in, 16)
            for u in range(2):
                sp.dma_start(raw[u][:].rearrange("p k c -> p (k c)"), I["w_out_q"][u]).then_inc(w_full[u], 16)
            sp.dma_start(x[:], I["xT"].rearrange("(k p) t -> p k t", p=P)).then_inc(x_in, 16)
            def load(i, u):
                sp.wait_ge(lo_done[u], i)
                sp.dma_start(raw[u][:].rearrange("p k c -> p (k c)"),
                             I["w_out_q"][bass.ds(2 * i + u, 1)].rearrange("b p n -> p (b n)")
                             ).then_inc(w_full[u], 16)

            def store_queries(i, u):
                sp.wait_ge(out_read[u], i + NW + 1)
                sp.dma_start(q_rows[bass.ds(2 * i + u, 1)].rearrange("c p t -> (c p) t"), q_st[u][:]
                             ).then_inc(q_out[u], 16)

            q_rows = S["q_dram"].rearrange("(c p) t -> c p t", p=P)
            with sp.Fori(1, NW + 1) as i:
                for u in range(2):
                    load(i, u)
            for q in range(2):
                sp.wait_ge(out_read[q], NW)
            sp.dma_start(S["x1_dram"].rearrange("(k p) t -> p k t", p=P), x[:]).then_inc(x_out, 16)
            sp.wait_ge(q_pad, 2)
            with sp.Fori(0, NW - 1) as i:
                for u in range(2):
                    load(i + NW + 1, u)
                    store_queries(i, u)
            for u in range(2):
                store_queries(NW - 1, u)
            sp.wait_ge(x_out, 16)
            for u in range(2):
                sp.wait_ge(q_out[u], 16 * NW)

        @block.scalar
        def _(act):
            for part in range(2):
                act.wait_ge(mix_in, 32)
                for c in range(H):
                    n = part * H + c
                    if n >= 2:
                        act.wait_ge(sq_used, n - 1)
                    act.activation(sq[n % 2], h[:, n, :], ACT.Square).then_inc(sq_done, 1)
                act.wait_ge(sq_used, H * (part + 1))
                if part:
                    act.wait_ge(mixed, H)
                act.activation(halves(rstd[:]), fold(ps_norm), ACT.Sqrt, scale=1.0 / FW, bias=C["eps"][:, 0:1]
                               ).then_inc(std_done, 1)

            def high_parts(i, u):
                act.wait_ge(w_full[u], 16 * i + 16)
                act.wait_ge(out_done[u], i)
                act.activation(w_hi[u][:], raw[u][:], ACT.Copy).then_inc(hi_done[u], 1)

            high_parts(0, 0)
            high_parts(0, 1)
            for c in range(KC):
                act.wait_ge(mixed, c + 1)
                act.activation(h_hi[:, c, :], h[:, c, :], ACT.Copy).then_inc(m_hi_done, 1)
            with act.Fori(0, NW) as i:
                for u in range(2):
                    high_parts(i + 1, u)
            for c in range(KC):
                act.wait_ge(out_read[c % 2], NW)
                act.wait_ge(sq_used, KC + max(c - 1, 0))
                act.activation(sq[c % 2], x[:, c, :], ACT.Square).then_inc(sq_done, 1)
            act.wait_ge(sq_used, 2 * KC)
            act.wait_ge(mixed, KC)
            act.activation(halves(rstd[:]), fold(ps_norm), ACT.Sqrt, scale=1.0 / D, bias=C["eps"][:, 0:1]
                           ).then_inc(std_done, 1)
            act.wait_ge(scale_done, 1)
            for c in range(KC):
                act.wait_ge(xn_done, c + 1)
                act.activation(h[:, c, 0:NPR], h[:, c, 0:NPR], ACT.Identity, scale=scale2[:, c, 0:1],
                               bias=mod[:, 3 * KC + c, 0:1]).then_inc(h_prompt, 1)
            act.wait_ge(h_prompt, KC)
            act.wait_ge(h_sample, 1)
            for c in range(KC):
                act.activation(h_hi[:, c, :], h[:, c, :], ACT.Copy).then_inc(h_hi_done, 1)

            def copy_out(i):
                act.wait_ge(out_done[1], NW + i + 1)
                act.wait_ge(q_out[1], 16 * i)
                act.activation(halves(q_st[1][:, 0:T]), fold(ps_out[1]), ACT.Copy).then_inc(out_read[1], 1)

            with act.Fori(0, NW - 1) as i:
                high_parts(i + NW + 1, 0)
                copy_out(i)
                high_parts(i + NW + 1, 1)
            copy_out(NW - 1)

        @block.tensor
        def _(pe):
            def add_squares(n0, n):
                for c in range(n):
                    pe.wait_ge(sq_done, n0 + c + 1)
                    for a in range(2):
                        mm = pe.matmul(ps_norm[:, a, 0:HT], C["ones"][:], sq[(n0 + c) % 2][:, a * HT:(a + 1) * HT],
                                       start=(c == 0), stop=(c == n - 1))
                    mm.then_inc(sq_used, 1)

            def project(first, parts_done):
                with pe.Fori(0, NW) as i:
                    for u in range(2):
                        pe.wait_ge(lo_done[u], i + first + 1)
                        pe.wait_ge(out_read[u], i + first)
                        for k in range(KC):
                            if u == 0:
                                pe.wait_ge(parts_done, k + 1)
                            mm = product(pe, ps_out[u], [((w_hi[u][:, k, :], w_lo[u][:, k, :]),
                                                          (h_hi[:, k, :], h_lo[:, k, :]))], k == 0, k == KC - 1)
                        mm.then_inc(out_done[u], 1)

            add_squares(0, H)
            pe.wait_ge(std_done, 1)
            add_squares(H, H)
            project(0, m_lo_done)
            pe.wait_ge(std_done, 2)
            add_squares(KC, KC)
            project(NW, h_lo_done)

        @block.gpsimd
        def _(pool):
            for u in range(2):
                pool.memset(q_st[u][:, T:NTT * P], 0.0).then_inc(q_pad, 1)

        @block.vector
        def _(dve):
            step = Chain(dve, v_step)

            def low_parts(i, u):
                dve.wait_ge(hi_done[u], i + 1)
                dve.tensor_tensor(w_lo[u][:], raw[u][:], w_hi[u][:].bitcast(F32), ALU.subtract
                                  ).then_inc(lo_done[u], 1)

            dve.wait_ge(g_in, 32)
            step(dve.tensor_scalar(scale2[:], mod[:, 4 * KC:5 * KC, :], 1.0, None, ALU.add))
            dve.tensor_tensor(scale2[:], scale2[:], bc(g2[:], 2, [P, KC, NC_]), ALU.mult).then_inc(scale_done, 1)
            for part in range(2):
                dve.wait_ge(std_done, part + 1)
                dve.reciprocal(rstd[:], rstd[:]).then_inc(rstd_done, 1)
                dve.wait_ge(rstd_done, part + 1)
                for c in range(part * H, part * H + H):
                    dve.scalar_tensor_tensor(h[:, c, :], h[:, c, :], g_mix[:, c:c + 1], rstd[:], ALU.mult, ALU.mult
                                             ).then_inc(mixed, 1)
            low_parts(0, 0)
            low_parts(0, 1)
            for c in range(KC):
                dve.wait_ge(m_hi_done, c + 1)
                dve.tensor_tensor(h_lo[:, c, :], h[:, c, :], h_hi[:, c, :].bitcast(F32), ALU.subtract
                                  ).then_inc(m_lo_done, 1)
            dve.wait_ge(x_in, 16)
            with dve.Fori(0, NW) as i:
                step.loop(i, 6)
                for q in range(2):
                    dve.wait_ge(out_done[q], i + 1)
                    c = bass.ds(2 * i + q, 1)
                    gate = mod[:, bass.ds(2 * KC + 2 * i + q, 1), :].rearrange("p c r -> p (c r)")
                    xc = x[:, c, :].rearrange("p c t -> p (c t)")
                    xs = xc[:, NPR:T].rearrange("p (b t) -> p b t", b=DB)
                    step.mark(dve.scalar_tensor_tensor(xc[:, 0:HT], ps_out[q][:, 0, 0:HT], gate[:, 0:1],
                                                       xc[:, 0:HT], ALU.mult, ALU.add))
                    step.mark(dve.scalar_tensor_tensor(xc[:, HT:NPR], ps_out[q][:, 1, 0:NPR - HT], gate[:, 0:1],
                                                       xc[:, HT:NPR], ALU.mult, ALU.add))
                    step(dve.tensor_tensor(gated[:].rearrange("p (b t) -> p b t", b=DB),
                                           ps_out[q][:, 1, NPR - HT:HT].rearrange("p (b t) -> p b t", b=DB),
                                           bc(gate[:, 1:NC_], 2, [P, DB, DS]), ALU.mult))
                    dve.tensor_tensor(xs, xs, gated[:].rearrange("p (b t) -> p b t", b=DB), ALU.add
                                      ).then_inc(out_read[q], 1)
                    dve.wait_ge(out_read[q], i + 1)
                    low_parts(i + 1, q)
                step.end_loop(NW)
            dve.wait_ge(std_done, 3)
            dve.reciprocal(rstd[:], rstd[:]).then_inc(rstd_done, 1)
            dve.wait_ge(rstd_done, 3)
            for c in range(KC):
                dve.tensor_tensor(h[:, c, :], x[:, c, :], rstd[:], ALU.mult).then_inc(xn_done, 1)
            dve.wait_ge(xn_done, KC)
            hs = h[:, :, NPR:T].rearrange("p c (b t) -> p c b t", b=DB)
            step(dve.tensor_tensor(hs, hs, bc(scale2[:, :, 1:NC_], 3, [P, KC, DB, DS]), ALU.mult))
            dve.tensor_tensor(hs, hs, bc(mod[:, 3 * KC:4 * KC, 1:NC_], 3, [P, KC, DB, DS]), ALU.add
                              ).then_inc(h_sample, 1)
            for c in range(KC):
                dve.wait_ge(h_hi_done, c + 1)
                dve.tensor_tensor(h_lo[:, c, :], h[:, c, :], h_hi[:, c, :].bitcast(F32), ALU.subtract
                                  ).then_inc(h_lo_done, 1)

            def copy_out(i):
                dve.wait_ge(out_done[0], NW + i + 1)
                dve.wait_ge(q_out[0], 16 * i)
                dve.tensor_copy(halves(q_st[0][:, 0:T]), fold(ps_out[0])).then_inc(out_read[0], 1)

            with dve.Fori(0, NW - 1) as i:
                copy_out(i)
                low_parts(i + NW + 1, 0)
                low_parts(i + NW + 1, 1)
            copy_out(NW - 1)


def select_experts(nc, I, O, S, C, sem):
    ctx = ExitStack()
    sb = lambda n, s, d=F32: ctx.enter_context(nc.sbuf_tensor(n, s, d))
    ps = lambda n, s, d=F32: ctx.enter_context(nc.psum_tensor(n, s, d))
    HX = 2 * PH
    NB, Q = 4, 4
    TURN = NB * Q
    TURNS = P // TURN
    EARLY = 5
    LAST = (T - (NTT - 1) * P) // TURN
    BT = TB // TURN
    with ctx:
        keys = sb("keys_sel", [P, HX, NK])
        q_st = sb("q_tile", [P, HX, P])
        s = sb("s_sel", [P, HX, NK])
        val = sb("val_sel", [P, HX, TK])
        idx = sb("idx_sel", [P, HX, TK], U32)
        idx_f = sb("idx_f_sel", [P, HX, TK])
        cand = sb("cand_sel", [P, PH, TK * TK])
        top = sb("top_sel", [P, PH, TK])
        pos = sb("pos_sel", [P, PH, TK], U32)
        half = [sb(f"half{x}", [P, PH, TK], U32) for x in range(2)]
        half_f = [sb(f"half_f{x}", [P, PH, TK]) for x in range(2)]
        number = sb("number_sel", [P, TK])
        hit = [sb(f"hit{x}", [P, PH, TK, TK]) for x in range(2)]
        res = [sb(f"res{n}", [P, PH, TK]) for n in range(3)]
        diff, e = sb("diff_sel", [P, PH, TK]), sb("e_sel", [P, PH, TK])
        tot = sb("tot_sel", [P, PH])
        sel = sb("sel", [P, 3, NTT * P])
        count = sb("count", [P, P])
        rows = [[sb(f"hot_rows{x}{b}", [P, Q, P]) for b in range(NB)] for x in range(2)]
        colm = [[sb(f"hot_cols{x}{b}", [P, Q, P]) for b in range(NB)] for x in range(2)]
        out = [sb(f"gate_blk{x}", [P, NK, TB]) for x in range(2)]
        ps_s = [ps(f"ps_sc{j}", [P, 512]) for j in range(2)]
        ps_t = ps("ps_sel_t", [P, 512])
        ps_g = [ps(f"ps_gate{b}", [P, 512]) for b in range(NB)]
        keys_in, q_in, count_in = sem("keys_in"), sem("q_tile_in"), sem("count_in")
        s_done, s_copied, s_searched, top_done, e_done = (
            sem(n) for n in ("sc_done", "sc_copied", "sc_searched", "top_done", "e_sel_done"))
        hits_found, hits_done, hits_used, res_part = (
            sem(n) for n in ("hits_found", "hits_done", "hits_used", "res_part"))
        t_done, t_copied = sem("sel_turned"), sem("sel_copied")
        far, far_sq, rows_done, cols_done, g_sum = (
            [sem(f"{n}{b}") for b in range(NB)] for n in ("far", "far_sq", "rows_done", "cols_done", "g_sum"))
        g_copied, g_out = sem("g_copied"), [sem(f"g_out{x}") for x in range(2)]
        v_step, held, held_p = sem("sel_v_step"), sem("sel_held"), sem("sel_held_p")
        block = ctx.enter_context(nc.Block())
        zero = lambda n: isinstance(n, int) and n <= 0

        def run(eng, scores, first, second, spread, loop=None, end_loop=None):
            def body(k):
                scores(k + 1)
                second(k, [(k - 1, t) for t in range(EARLY, TURNS)] if not zero(k) else [])
                first(k + 1, [(k, t) for t in range(EARLY)])

            scores(0)
            first(0, [])
            body(0)
            with eng.Fori(0, NTT - 2) as i:
                if loop:
                    loop(i)
                body(i + 1)
                if loop:
                    end_loop(NTT - 2)
            second(NTT - 1, [(NTT - 2, t) for t in range(EARLY, TURNS)])
            for t in range(LAST):
                spread(NTT - 1, t)

        @block.sync
        def _(sp):
            q_rows = S["q_dram"].rearrange("(c p) t -> p c t", p=P)

            def load_queries(i):
                if i:
                    sp.wait_ge(s_done, 4 * i)
                sp.dma_start(q_st[:], q_rows[:, :, i * P:(i + 1) * P]).then_inc(q_in, 16)

            def store(k):
                sp.wait_ge(g_copied, NB * BT * (k + 1))
                sp.dma_start(S["gates_dram"][k], out[k % 2][:].rearrange("p j t -> p (j t)")
                             ).then_inc(g_out[k % 2], 16)

            load_queries(0)
            sp.dma_start(keys[:], I["subkeysT"].rearrange("p (x n) -> p x n", x=HX)).then_inc(keys_in, 16)
            sp.dma_start(number[:], I["number"]).then_inc(keys_in, 16)
            sp.dma_start(count[:], I["count"]).then_inc(count_in, 16)
            load_queries(1)
            stored = 0
            for i in range(2, NTT):
                load_queries(i)
                whole = ((i - 2) * TURNS + EARLY) // BT
                for k in range(stored, whole):
                    store(k)
                stored = whole
            for k in range(stored, NTB):
                store(k)
            for x in range(2):
                sp.wait_ge(g_out[x], 16 * ((NTB + 1 - x) // 2))

        @block.scalar
        def _(act):
            def scores(i):
                for j in range(4):
                    act.wait_ge(s_done, 4 * i + j + 1)
                    if not zero(i):
                        act.wait_ge(s_searched, i)
                    act.activation(s[:, 4 * j:4 * j + 4, :], ps_s[j % 2][:].rearrange("p (x n) -> p x n", x=4),
                                   ACT.Copy).then_inc(s_copied, 1)

            def copy_gates(k, t):
                n = TURNS * k + t
                slot, before = (t // BT) % 2, TURNS // BT // 2 * k + t // BT // 2
                if t % BT == 0 and not zero(before):
                    act.wait_ge(g_out[slot], 16 * before)
                for b in range(NB):
                    act.wait_ge(g_sum[b], n + 1)
                    at = (t % BT) * TURN + b * Q
                    act.activation(out[slot][:, :, at:at + Q].rearrange("p j t -> p t j"),
                                   ps_g[b][:].rearrange("p (t j) -> p t j", t=Q), ACT.Copy).then_inc(g_copied, 1)

            def spread(k, t):
                n, hot = TURNS * k + t, rows[t % 2]
                for b in range(NB):
                    act.wait_ge(far[b], n + 1)
                    act.activation(hot[b][:], hot[b][:], ACT.Square).then_inc(far_sq[b], 1)
                if not zero(n):
                    copy_gates(*((k, t - 1) if t else (k - 1, TURNS - 1)))
                for b in range(NB):
                    act.wait_ge(far_sq[b], n + 1)
                    act.activation(hot[b][:], hot[b][:], ACT.Relu, scale=-1.0, bias=1.0).then_inc(rows_done[b], 1)

            def first(i, turns):
                for k, t in turns:
                    spread(k, t)

            def second(i, turns):
                for k, t in turns:
                    spread(k, t)
                act.wait_ge(top_done, i + 1)
                act.activation(e[:], diff[:], ACT.Exp).then_inc(e_done, 1)
                act.wait_ge(t_done, i + 1)
                act.activation(sel[:, :, bass.ds(P * i, P)], ps_t[:, 0:3 * P].rearrange("p (n t) -> p n t", n=3),
                               ACT.Copy).then_inc(t_copied, 1)

            run(act, scores, first, second, spread)
            copy_gates(NTT - 1, LAST - 1)

        @block.tensor
        def _(pe):
            pe.wait_ge(keys_in, 32)

            def scores(i):
                pe.wait_ge(q_in, 16 * i + 16)
                for j in range(4):
                    if not zero(4 * i + j - 1):
                        pe.wait_ge(s_copied, 4 * i + j - 1)
                    for x in range(4 * j, 4 * j + 4):
                        mm = pe.matmul(ps_s[j % 2][:, (x % 4) * P:(x % 4 + 1) * P], q_st[:, x, :], keys[:, x, :],
                                       start=True, stop=True)
                    mm.then_inc(s_done, 1)

            def spread(k, t):
                n = TURNS * k + t
                for b in range(NB):
                    pe.wait_ge(rows_done[b], n + 1)
                    pe.wait_ge(cols_done[b], Q * n + Q)
                    if not zero(n):
                        pe.wait_ge(g_copied, NB * n - NB + b + 1)
                    for j in range(Q):
                        mm = pe.matmul(ps_g[b][:, j * P:(j + 1) * P], rows[t % 2][b][:, j, :], colm[t % 2][b][:, j, :],
                                       start=True, stop=True)
                    mm.then_inc(g_sum[b], 1)

            def first(i, turns):
                for k, t in turns:
                    spread(k, t)

            def second(i, turns):
                for k, t in turns:
                    spread(k, t)
                pe.wait_ge(res_part, 2 * i + 2)
                pe.wait_ge(hits_used, i + 1)
                if not zero(i):
                    pe.wait_ge(t_copied, i)
                for n in range(3):
                    mm = pe.transpose(ps_t[:, n * P:(n + 1) * P], res[n][:].rearrange("p h k -> p (h k)"), C["ident"][:])
                mm.then_inc(t_done, 1)

            run(pe, scores, first, second, spread)

        @block.gpsimd
        def _(pool):
            pool.wait_ge(count_in, 16)

            def spread(k, t):
                n = TURNS * k + t
                for b in range(NB):
                    pool.wait_ge(t_copied, k + 1)
                    if not zero(n - 1):
                        pool.wait_ge(g_sum[b], n - 1)
                    pool.sem_inc(held_p, 1)
                    at = bass.ds(P * k + t * TURN + b * Q, Q)
                    pool.tensor_tensor(rows[t % 2][b][:], bc(sel[:, 0, at], 2, [P, Q, P]), bc(count[:], 1, [P, Q, P]),
                                       ALU.subtract).then_inc(far[b], 1)

            def first(i, turns):
                for k, t in turns:
                    spread(k, t)

            def second(i, turns):
                for k, t in turns:
                    spread(k, t)
                pool.wait_ge(hits_found, i + 1)
                pool.tensor_tensor(hit[1][:], hit[1][:], bc(idx_f[:, 1:HX:2, :], 2, [P, PH, TK, TK]), ALU.mult
                                   ).then_inc(hits_done, 1)

            run(pool, lambda i: None, first, second, spread)

        @block.vector
        def _(dve):
            step = Chain(dve, v_step)
            dve.wait_ge(keys_in, 32)
            dve.wait_ge(count_in, 16)

            def spread(k, t):
                n = TURNS * k + t
                dve.wait_ge(t_copied, k + 1)
                for b in range(NB):
                    if not zero(n - 1):
                        dve.wait_ge(g_sum[b], n - 1)
                    for j in range(Q):
                        at = bass.ds(P * k + t * TURN + b * Q + j, 1)
                        dve.tensor_scalar(colm[t % 2][b][:, j, :], count[:], sel[:, 1, at], sel[:, 2, at], ALU.is_equal,
                                          ALU.mult).then_inc(cols_done[b], 1)

            def two_rounds(get, n, values, places, turns):
                phases = (lambda x: dve.max(values[:, x, 0:8], get(x)),
                          lambda x: dve.max_index(places[:, x, 0:8], values[:, x, 0:8], get(x)),
                          lambda x: dve.match_replace(get(x), values[:, x, 0:8], get(x), 3 * NEG),
                          lambda x: dve.max(values[:, x, 8:16], get(x)),
                          lambda x: dve.max_index(places[:, x, 8:16], values[:, x, 8:16], get(x)))
                for phase, search in enumerate(phases):
                    for x in range(n):
                        step.mark(search(x))
                    if phase < len(turns):
                        spread(*turns[phase])
                    step.settle()
                    dve.sem_inc(held, 1)

            def first(i, turns):
                dve.wait_ge(s_copied, 4 * i + 4)
                dve.sem_inc(held, 1)
                two_rounds(lambda x: s[:, x, :], HX, val, idx, turns)
                if not zero(i):
                    dve.wait_ge(hits_done, i)
                dve.tensor_copy(idx_f[:], idx[:]).then_inc(s_searched, 1)

            def second(i, turns):
                full = [P, PH, TK, TK]
                dve.wait_ge(s_searched, i + 1)
                step(dve.tensor_tensor(cand[:].rearrange("p h (a b) -> p h a b", a=TK),
                                       bc(val[:, 0:HX:2, :], 3, full), bc(val[:, 1:HX:2, :], 2, full), ALU.add))
                dve.sem_inc(held, 1)
                two_rounds(lambda x: cand[:, x, :], PH, top, pos, turns)
                step.mark(dve.tensor_scalar(half[0][:], pos[:], 4, None, ALU.logical_shift_right))
                step(dve.tensor_scalar(half[1][:], pos[:], TK - 1, None, ALU.bitwise_and))
                step.mark(dve.tensor_copy(half_f[0][:], half[0][:]))
                step(dve.tensor_copy(half_f[1][:], half[1][:]))
                dve.tensor_tensor(diff[:], top[:], top[:, :, 0:1].broadcast_to([P, PH, TK]), ALU.subtract
                                  ).then_inc(top_done, 1)
                dve.tensor_tensor(hit[1][:], bc(half_f[1][:], 3, full),
                                  number[:].unsqueeze(1).unsqueeze(1).broadcast_to(full), ALU.is_equal
                                  ).then_inc(hits_found, 1)
                step(dve.tensor_tensor(hit[0][:], bc(half_f[0][:], 3, full),
                                       number[:].unsqueeze(1).unsqueeze(1).broadcast_to(full), ALU.is_equal))
                step(dve.tensor_tensor(hit[0][:], hit[0][:], bc(idx_f[:, 0:HX:2, :], 2, full), ALU.mult))
                if not zero(i):
                    dve.wait_ge(t_done, i)
                dve.tensor_reduce(res[0][:], hit[0][:], AX, ALU.add).then_inc(res_part, 1)
                dve.wait_ge(e_done, i + 1)
                step(dve.tensor_reduce(tot[:], e[:], AX, ALU.add))
                step(dve.reciprocal(tot[:], tot[:]))
                dve.tensor_tensor(res[2][:], e[:], bc(tot[:], 2, [P, PH, TK]), ALU.mult).then_inc(res_part, 1)
                dve.wait_ge(hits_done, i + 1)
                dve.tensor_reduce(res[1][:], hit[1][:], AX, ALU.add).then_inc(hits_used, 1)

            per = 5 * HX + 1 + 5 * PH + 4 + 2 + 2
            run(dve, lambda i: None, first, second, spread, lambda i: step.loop(i, per), step.end_loop)


def experts(nc, I, O, S, C, sem):
    ctx = ExitStack()
    sb = lambda n, s, d=F32: ctx.enter_context(nc.sbuf_tensor(n, s, d))
    ps = lambda n, s, d=F32: ctx.enter_context(nc.psum_tensor(n, s, d))
    HC = KC // 2
    HW = D // 2
    with ctx:
        acc, h_hi, h_lo = S["acc"], S["h_hi"], S["h_lo"]
        w_hi = [sb(f"w_hi{n}", [P, T], F32R) for n in range(4)]
        w_lo = [sb(f"w_lo{n}", [P, T], F32R) for n in range(4)]
        gates = [sb(f"gates{n}", [P, NTB, 2, TB]) for n in range(2)]
        wt = [sb(f"wt{n}", [P, T]) for n in range(2)]
        raw_u = [sb(f"raw_u{n}", [P, HW]) for n in range(2)]
        raw_v = [sb(f"raw_v{n}", [P, HW]) for n in range(2)]
        u_hi = [sb(f"u_hi{n}", [P, HW], F32R) for n in range(2)]
        u_lo = [sb(f"u_lo{n}", [P, HW], F32R) for n in range(2)]
        v_hi = [[sb(f"v_hi{b}{x}", [P, HW], F32R) for x in range(2)] for b in range(2)]
        v_lo = [[sb(f"v_lo{b}{x}", [P, HW], F32R) for x in range(2)] for b in range(2)]
        ps_u = [ps(f"ps_u{n}", [P, 2, 512]) for n in range(2)]
        ps_v = [ps(f"ps_v{n}", [P, 2, 512]) for n in range(2)]

        u_in, v_in, gates_in = ([sem(f"{n}{x}") for x in range(2)] for n in ("raw_u_in", "raw_v_in", "gates_in"))
        u_hi_done, u_lo_done, u_used = ([sem(f"{n}{x}") for x in range(2)] for n in ("u_hi_done", "u_lo_done", "u_used"))
        v_hi_done, v_lo_done = ([sem(f"{n}{x}") for x in range(2)] for n in ("v_hi_done", "v_lo_done"))
        v_chunk, acc_done = ([sem(f"{n}{x}") for x in range(2)] for n in ("v_chunk", "acc_done"))
        acc_clear = sem("acc_clear")
        a_done, gm_done, w_hi_done, w_lo_done = (sem(n) for n in ("a_done", "gm_done", "w_hi_done", "w_lo_done"))
        block = ctx.enter_context(nc.Block())
        NS = NK

        def run(eng, step):
            step(0, 0), step(1, 1)
            with eng.Fori(0, (NS - 4) // 4) as i:
                for u in range(4):
                    step(4 * i + (2 + u), 2 + u)
            for s in range(NS - 2, NS + 2):
                step(s, s)

        first = lambda s: isinstance(s, int) and s < 2
        last = lambda s, n: isinstance(s, int) and s + n > NS - 1

        @block.sync
        def _(sp):
            def load_u(s, h):
                src = I["uT"][bass.ds(s, 1)].rearrange("a p n -> (a p) n")
                sp.dma_start(raw_u[h][:], src[:, h * HW:(h + 1) * HW]).then_inc(u_in[h], 16)

            def load_gates(g, par):
                sp.dma_start(gates[par][:].rearrange("p b j t -> p b (j t)"),
                             S["gates_dram"].rearrange("b p (g n) -> g p b n", g=NK // 2)[bass.ds(g, 1)]
                             .rearrange("a p b n -> (a p) b n")).then_inc(gates_in[par], 16)

            v_rows = I["peer_v"].rearrange("(i j) d -> j i d", j=NK)

            def step(s, m):
                v = s - 1
                if not (isinstance(s, int) and not 0 <= v < NS):
                    for x in range(2):
                        sp.wait_ge(v_lo_done[x], v)
                        e = bass.ds(v - (m - 1) % 2 + x, 1)
                        sp.dma_start(raw_v[x][:], v_rows[e].rearrange("a p n -> (a p) n")[
                            :, ((m - 1) % 2) * HW:((m - 1) % 2 + 1) * HW]).then_inc(v_in[x], 16)
                if m % 2 == 0 and not last(s, 3):
                    sp.wait_ge(gm_done, s)
                    load_gates(s // 2 + 1 if isinstance(s, int) else half_of(s) + 1, (m // 2 + 1) % 2)
                if not last(s, 2):
                    for h in range(2):
                        sp.wait_ge(u_lo_done[h], s + 2)
                        load_u(s + 2, h)

            load_u(0, 0)
            load_u(0, 1)
            load_gates(0, 0)
            for h in range(2):
                sp.wait_ge(u_lo_done[h], 1)
                load_u(1, h)
            step(0, 0), step(1, 1)
            with sp.Fori(0, (NS - 4) // 4) as i:
                for u in range(4):
                    half_of = lambda s, u=u: 2 * i + (2 + u) // 2
                    step(4 * i + (2 + u), 2 + u)
            for s in range(NS - 2, NS + 2):
                step(s, s)

        @block.scalar
        def _(act):
            def split_u(s, h):
                act.wait_ge(u_in[h], 16 * s + 16)
                act.wait_ge(u_used[h], s)
                act.activation(u_hi[h][:], raw_u[h][:], ACT.Copy).then_inc(u_hi_done[h], 1)

            def step(s, m):
                v = s - 2
                if not first(s):
                    if last(s, -1):
                        act.wait_ge(v_chunk[1], (HC // 2) * (v - 1))
                    else:
                        act.wait_ge(u_used[1], s)
                    for x in range(2):
                        act.wait_ge(v_in[x], 16 * v + 16)
                        act.activation(v_hi[m % 2][x][:], raw_v[x][:], ACT.Copy).then_inc(v_hi_done[x], 1)
                if not last(s, 1):
                    split_u(s + 1, 0)
                if not last(s, 0):
                    act.wait_ge(u_used[1], s + 1)
                    if not first(s):
                        act.wait_ge(w_lo_done, s - 1)
                    act.activation(halves(wt[m % 2][:]), fold(ps_u[m % 2]), ACT.Gelu_apprx_tanh).then_inc(a_done, 1)
                if not last(s, 1):
                    split_u(s + 1, 1)
                if not last(s, 0):
                    act.wait_ge(gm_done, s + 1)
                    if not first(s):
                        act.wait_ge(v_chunk[1], (HC // 2) * (s - 2 - m % 2))
                    act.activation(w_hi[m % 4][:], wt[m % 2][:], ACT.Copy).then_inc(w_hi_done, 1)

            split_u(0, 0)
            split_u(0, 1)
            run(act, step)

        @block.vector
        def _(dve):
            def split_u(s, h):
                dve.wait_ge(u_hi_done[h], s + 1)
                dve.tensor_tensor(u_lo[h][:], raw_u[h][:], u_hi[h][:].bitcast(F32), ALU.subtract
                                  ).then_inc(u_lo_done[h], 1)

            def add(v, c, b):
                q = c % 2
                dve.wait_ge(v_chunk[q], (HC // 2) * v + c // 2 + 1)
                dve.wait_ge(acc_done[q], (HC // 2) * v + c // 2)
                dst = halves(acc[:, b * HC + c, :])
                dve.tensor_tensor(dst, fold(ps_v[q]), dst, ALU.add).then_inc(acc_done[q], 1)

            def step(s, m):
                v = s - 2
                if not first(s):
                    for x in range(2):
                        dve.wait_ge(v_hi_done[x], v + 1)
                        dve.tensor_tensor(v_lo[m % 2][x][:], raw_v[x][:], v_hi[m % 2][x][:].bitcast(F32),
                                          ALU.subtract).then_inc(v_lo_done[x], 1)
                if not last(s, 1):
                    split_u(s + 1, 0)
                if not first(s):
                    add(v, 0, m % 2)
                if not last(s, 1):
                    split_u(s + 1, 1)
                if not first(s):
                    add(v, 1, m % 2)
                if not last(s, 0):
                    dve.wait_ge(a_done, s + 1)
                    par = (m // 2) % 2
                    dve.wait_ge(gates_in[par], 16 * turns_of(s, m) + 16)
                    w = wt[m % 2][:].rearrange("p (b t) -> p b t", t=TB)
                    dve.tensor_tensor(w, w, gates[par][:, :, m % 2, :], ALU.mult).then_inc(gm_done, 1)
                if not first(s):
                    add(v, 2, m % 2)
                if not last(s, 0):
                    dve.wait_ge(w_hi_done, s + 1)
                    dve.tensor_tensor(w_lo[m % 4][:], wt[m % 2][:], w_hi[m % 4][:].bitcast(F32), ALU.subtract
                                      ).then_inc(w_lo_done, 1)
                if not first(s):
                    for c in range(3, HC):
                        add(v, c, m % 2)

            split_u(0, 0)
            split_u(0, 1)
            dve.memset(acc[:], 0.0).then_inc(acc_clear, 1)
            dve.wait_ge(acc_clear, 1)
            turns_of = lambda s, m: s // 4
            step(0, 0), step(1, 1)
            with dve.Fori(0, (NS - 4) // 4) as i:
                turns_of = lambda s, m: i + m // 4
                for u in range(4):
                    step(4 * i + (2 + u), 2 + u)
            turns_of = lambda s, m: s // 4
            for s in range(NS - 2, NS + 2):
                step(s, s)

        @block.tensor
        def _(pe):
            def step(s, m):
                v = s - 2
                if not last(s, 0):
                    if not first(s):
                        pe.wait_ge(a_done, s - 1)
                    for h in range(2):
                        pe.wait_ge(u_lo_done[h], s + 1)
                        for k in range(HC):
                            c = h * HC + k
                            cols = slice(k * P, (k + 1) * P)
                            mm = product(pe, ps_u[m % 2], [((u_hi[h][:, cols], u_lo[h][:, cols]), (h_hi[:, c, :], h_lo[:, c, :]))],
                                         c == 0, c == KC - 1)
                        mm.then_inc(u_used[h], 1)
                if not first(s):
                    b = m % 2
                    for x in range(2):
                        pe.wait_ge(v_lo_done[x], v + 1)
                    pe.wait_ge(w_lo_done, s - m % 2)
                    for c in range(HC):
                        q = c % 2
                        pe.wait_ge(acc_done[q], (HC // 2) * v + c // 2)
                        cols = slice(c * P, (c + 1) * P)
                        pair = [((v_hi[b][x][:, cols], v_lo[b][x][:, cols]),
                                 (w_hi[(m - 2 - b + x) % 4][:], w_lo[(m - 2 - b + x) % 4][:])) for x in range(2)]
                        product(pe, ps_v[q], pair, True, True).then_inc(v_chunk[q], 1)

            run(pe, step)


def finish(nc, I, O, S, C, sem):
    ctx = ExitStack()
    sb = lambda n, s, d=F32: ctx.enter_context(nc.sbuf_tensor(n, s, d))
    ps = lambda n, s, d=F32: ctx.enter_context(nc.psum_tensor(n, s, d))
    with ctx:
        acc, mod = S["acc"], S["mod"]
        x = sb("x2", [P, KC, T])
        sq = [sb(f"sq3_{u}", [P, T]) for u in range(2)]
        std, rstd, g_f = sb("std3", [P, T]), sb("rstd3", [P, T]), sb("g_f", [P, KC])
        ps_norm = ps("ps_norm3", [P, 2, 512])
        x_in, g_in, added = [sem(f"x2_in{n}") for n in range(4)], sem("g_f_in"), sem("x2_added")
        scaled, sq_done, sq_used, std_done, y_done, y_out = (sem(n) for n in ("acc_scaled", "sq3_done", "sq3_used",
                                                                             "std3_done", "y_done_f", "y_out"))
        v_step = sem("fin_v_step")
        block = ctx.enter_context(nc.Block())

        @block.sync
        def _(sp):
            x_v = S["x1_dram"].rearrange("(k p) t -> p k t", p=P)
            y_v = O["yT"].rearrange("(k p) t -> p k t", p=P)
            sp.dma_start(g_f[:], I["gfT"]).then_inc(g_in, 16)
            for n in range(4):
                sp.dma_start(x[:, 4 * n:4 * n + 4, :], x_v[:, 4 * n:4 * n + 4, :]).then_inc(x_in[n], 16)
            for n in range(4):
                sp.wait_ge(y_done, 4 * n + 4)
                sp.dma_start(y_v[:, 4 * n:4 * n + 4, :], x[:, 4 * n:4 * n + 4, :]).then_inc(y_out, 16)
            sp.wait_ge(y_out, 64)

        @block.scalar
        def _(act):
            for c in range(KC):
                act.wait_ge(added, c + 1)
                if c >= 2:
                    act.wait_ge(sq_used, c - 1)
                act.activation(sq[c % 2][:], x[:, c, :], ACT.Square).then_inc(sq_done, 1)
            act.wait_ge(sq_used, KC)
            act.activation(halves(std[:]), fold(ps_norm), ACT.Sqrt, scale=1.0 / D, bias=C["eps"][:, 0:1]
                           ).then_inc(std_done, 1)

        @block.tensor
        def _(pe):
            for c in range(KC):
                pe.wait_ge(sq_done, c + 1)
                for a in range(2):
                    mm = pe.matmul(ps_norm[:, a, 0:HT], C["ones"][:], sq[c % 2][:, a * HT:(a + 1) * HT],
                                   start=(c == 0), stop=(c == KC - 1))
                mm.then_inc(sq_used, 1)

        @block.vector
        def _(dve):
            step = Chain(dve, v_step)
            gate = mod[:, 5 * KC:6 * KC, :]
            acc_s = acc[:, :, NPR:T].rearrange("p c (b t) -> p c b t", b=DB)
            step(dve.tensor_tensor(acc_s, acc_s, bc(gate[:, :, 1:NC_], 3, [P, KC, DB, DS]), ALU.mult))
            for c in range(KC):
                if c % 4 == 0:
                    dve.wait_ge(x_in[c // 4], 16)
                    step(dve.tensor_tensor(x[:, c:c + 4, NPR:T], x[:, c:c + 4, NPR:T], acc[:, c:c + 4, NPR:T], ALU.add))
                dve.scalar_tensor_tensor(x[:, c, 0:NPR], acc[:, c, 0:NPR], gate[:, c, 0:1], x[:, c, 0:NPR],
                                         ALU.mult, ALU.add).then_inc(added, 1)
            dve.wait_ge(std_done, 1)
            dve.wait_ge(g_in, 16)
            dve.wait_ge(added, KC)
            step(dve.reciprocal(rstd[:], std[:]))
            for c in range(KC):
                dve.scalar_tensor_tensor(x[:, c, :], x[:, c, :], g_f[:, c:c + 1], rstd[:], ALU.mult, ALU.mult
                                         ).then_inc(y_done, 1)


def set_constants(nc, I, O, S, C, sem):
    ready = sem(f"{C["ident"].name}_ready")
    with nc.Block() as block:
        @block.gpsimd
        def _(pool):
            pool.memset(C["eps"][:], EPS).then_inc(ready, 1)
            pool.memset(C["ones"][:], 1.0).then_inc(ready, 1)
            pool.memset(C["ident"][:], 0.0).then_inc(ready, 1)
            pool.wait_ge(ready, 3)
            pool.affine_select(out=C["ident"][:], in_=C["ident"][:], compare_op=ALU.not_equal, fill=1.0,
                               base=0, pattern=[[-1, P]], channel_multiplier=1).then_inc(ready, 1)
            pool.wait_ge(ready, 4)


def stage(nc, program, *args):
    used = []

    def sem(name):
        used.append(nc.alloc_semaphore(name=name))
        return used[-1]

    program(nc, *args, sem)
    nc.clear_and_free_semaphores(used)
    nc.all_engine_barrier()


def build(nc, I, O):
    tile = lambda n, s: nc.sbuf_tensor(n, s, F32)
    scratch = lambda n, s: nc.dram_tensor(n, s, F32).ap()
    S = {"att_dram": scratch("att_scratch", [FW, T]), "ssm_dram": scratch("ssm_scratch", [SW, T]),
         "x1_dram": scratch("x1_scratch", [D, T]), "q_dram": scratch("q_scratch", [D, NTT * P]),
         "gates_dram": scratch("gates_scratch", [NTB, P, NK * TB])}
    C = {}
    args = (I, O, S, C)
    with tile("eps", [P, 1]) as C["eps"], tile("ones", [P, P]) as C["ones"], tile("mod", [P, NMOD, NC_]) as S["mod"]:
        with tile("ident_a", [P, P]) as C["ident"], tile("qkvu", [P, 4 * H, T]) as S["qkvu"], \
                tile("logf", [H, T]) as S["logf"]:
            stage(nc, set_constants, *args)
            with nc.sbuf_tensor("h_hi", [P, KC, T], F32R) as S["h_hi"], \
                    nc.sbuf_tensor("h_lo", [P, KC, T], F32R) as S["h_lo"]:
                stage(nc, modulate, *args)
                stage(nc, project_inputs, *args)
            with tile("att", [P, H, T]) as S["att"]:
                stage(nc, attend_prompt, *args)
                stage(nc, attend_sample, *args)
            stage(nc, s5_layer, *args)
        with nc.sbuf_tensor("h2_hi", [P, KC, T], F32R) as S["h_hi"], \
                nc.sbuf_tensor("h2_lo", [P, KC, T], F32R) as S["h_lo"]:
            stage(nc, merge_and_query, *args)
            with tile("ident_b", [P, P]) as C["ident"]:
                stage(nc, set_constants, *args)
                stage(nc, select_experts, *args)
            with tile("acc", [P, KC, T]) as S["acc"]:
                stage(nc, experts, *args)
                stage(nc, finish, *args)


def layout(inputs):
    import numpy as np
    f = {n: np.asarray(a) for n, a in inputs.items()}
    cols = lambda v, n: np.ascontiguousarray(v.reshape(n, P).T)
    a = {}
    a["xT"] = np.concatenate([f["x_prompt"].reshape(NPR, D), f["x_sample"].reshape(NSM, D)]).T
    a["cT"] = np.concatenate([f["c_prompt"], f["c_sample"]]).T
    blocks = lambda w, n: w.reshape(KC, P, -1, n).transpose(2, 1, 0, 3).reshape(-1, P, KC * n)
    a["w_ada"] = blocks(f["w_ada"][0], WB)
    a["b_adaT"] = cols(f["b_ada"][0], NMOD)
    a["g1T"] = cols(f["g_norm1"][0], KC)
    w_in = f["w_in"][0]
    a["w_in"] = blocks(np.concatenate([w_in[:, :3 * FW], w_in[:, 3 * FW + H:]], axis=1), P)
    a["w_fg"] = w_in[:, 3 * FW:3 * FW + H]
    a["b_fg"] = f["b_forget"][0].reshape(H, 1)
    a["pages"] = f["page_table"].reshape(1, DB * NPG)
    a["cache_k"] = f["cache_k"][0].reshape(-1, PAGE, FW)
    a["cache_v"] = f["cache_v"][0].reshape(-1, PAGE, FW)
    a["cache_lfT"] = f["cache_logf"][0].transpose(0, 2, 1)
    g_ = lambda v: v.reshape(G, NST, -1).transpose(1, 0, 2).reshape(NST, -1)
    two = lambda x, y: np.concatenate([g_(x), g_(y)])
    a["a_re"], a["a_im"] = two(f["ssm_a_re"], f["ssm_a_re"]), two(f["ssm_a_im"], f["ssm_a_im"])
    a["log_dt"] = np.broadcast_to(f["ssm_log_dt"], (P, G))
    br, bi = f["ssm_b_re"], f["ssm_b_im"]
    cr, ci = f["ssm_c_re"][0].transpose(0, 2, 1), f["ssm_c_im"][0].transpose(0, 2, 1)
    a["b_ri"], a["b_ir"], a["c_ri"], a["c_ir"] = two(br, bi), two(bi, br), two(cr, ci), two(ci, cr)
    hr, hi = (f[n][0].transpose(2, 0, 1).reshape(NST, DB * G) for n in ("state_ssm_re", "state_ssm_im"))
    a["h0_ri"], a["h0_ir"] = np.concatenate([hr, hi]), np.concatenate([hi, hr])
    a["d_col"] = np.tile(f["ssm_d"][0].reshape(G, CG).T, (LC, 1))
    a["w_glu"], a["b_gluT"] = f["w_glu"][0], cols(f["b_glu"][0], NGB)
    a["w_out_q"] = np.concatenate([blocks(f["w_out"][0], P), blocks(f["peer_w_q"][0], P)])
    a["g_mixT"] = cols(np.concatenate([f["g_attn_out"][0], f["g_ssm_out"][0]]), KC)
    a["g2T"], a["gfT"] = cols(f["g_norm2"][0], KC), cols(f["g_final"], KC)
    a["subkeysT"] = f["peer_subkeys"][0].transpose(3, 0, 1, 2).reshape(P, 2 * PH * NK)
    a["uT"] = f["peer_u"][0].reshape(NK, NK, KC, P).transpose(1, 3, 2, 0).reshape(NK, P, D)
    a["peer_v"] = f["peer_v"][0]
    a["tri"] = np.where(np.tril(np.ones((P, P))) > 0, 0, NEG).astype(np.float32)
    own = np.eye(H, dtype=np.float32)
    a["sel_neg"] = np.repeat(own[:, :, None] * np.float32(-1 / SCALE), P, axis=2)
    a["sel_pos_s"] = np.repeat(own, DS, axis=1)
    a["sel_neg_s"] = a["sel_pos_s"] * np.float32(-1 / SCALE)
    a["own_q"] = np.tile(np.eye(DS, dtype=np.float32), (H, 1))
    b_, q_, t_ = np.arange(DB), np.tile(np.arange(DS), H), np.arange(DS)
    seen = (b_[None, :, None, None] == b_[None, None, :, None]) & (t_[None, None, None, :] <= q_[:, None, None, None])
    a["mask_s"] = np.where(seen, 0, NEG).astype(np.float32).reshape(H * DS, DB, NSM)
    a["number"] = np.broadcast_to(np.arange(TK, dtype=np.float32), (P, TK))
    a["count"] = np.broadcast_to(np.arange(P, dtype=np.float32), (P, P))
    a["sgn"] = np.repeat(np.array([[-1, 1], [1, -1]], np.float32), NST, axis=0)
    return {n: np.ascontiguousarray(v) for n, v in a.items()}


OUTS = {"kvT": (2 * FW, T), "logfT": (H, T), "yT": (D, T), "end_prompt": (P, G), "end_sample": (P, DB * G)}


def kernel(**inputs):
    import numpy as np
    import concourse.bacc as bacc
    from concourse.bass_utils import run_bass_kernel_spmd

    nc = bacc.Bacc("TRN2", target_bir_lowering=False, num_devices=1)
    arrays, I, O = {}, {}, {}
    for name, a in layout(inputs).items():
        arrays["in_" + name] = a
        I[name] = nc.dram_tensor("in_" + name, a.shape, mybir.dt.from_np(a.dtype), kind="ExternalInput").ap()
    for name, shape in OUTS.items():
        O[name] = nc.dram_tensor("out_" + name, shape, F32, kind="ExternalOutput").ap()
    build(nc, I, O)
    r = run_bass_kernel_spmd(nc, [arrays], core_ids=[0]).results[0]
    out = {n: np.asarray(r["out_" + n]) for n in OUTS}
    y, kv, lf = out["yT"].T, out["kvT"].T, out["logfT"].T
    k, v = kv[:, :FW], kv[:, FW:]
    ep = out["end_prompt"].reshape(2, NST, G).transpose(0, 2, 1)
    es = out["end_sample"].reshape(2, NST, DB, G).transpose(0, 2, 3, 1)
    pr = lambda a, *s: np.ascontiguousarray(a[:NPR]).reshape(1, 1, NPR, *s)
    sm = lambda a, *s: np.ascontiguousarray(a[NPR:]).reshape(1, DB, DS, *s)
    one = lambda a, *s: np.ascontiguousarray(a).reshape(1, *s)
    return (one(y[:NPR], NPR, D), np.ascontiguousarray(y[NPR:]).reshape(DB, DS, D),
            pr(k, H, DH), pr(v, H, DH), pr(lf, H), one(ep[0], 1, G, NST), one(ep[1], 1, G, NST),
            sm(k, H, DH), sm(v, H, DH), sm(lf, H), one(es[0], DB, G, NST), one(es[1], DB, G, NST))
```
